# Optimizing a Trainium2 kernel written in Bass

```python
import math
import functools
import jax
import jax.numpy as jnp
from jax import lax
import numpy as np

D_MODEL = 1024
BATCH = 1
SEQ = 512
DEPTH = 2

GRID_W = 64
CTX_LEN = 256
CHUNK = 64
EPS = 1e-6
N_MOD = 6

HY_WIDTH = D_MODEL // 4
HY_ORDER = 2
HY_SHORT = 3
HY_EMB = 33
HY_HIDDEN = 64
HY_FAST_DECAY = 0.3
HY_SLOW_DECAY = 1.5
HY_TARGET = 1e-2
GDN_HEADS = D_MODEL // 256
GDN_DK = 128
GDN_DV = 128
GDN_SHORT = 3
RET_HEADS = D_MODEL // 256
RET_DK = 64
RET_DV = 64
ROPE_BASE = 10000.0

MIX_WIDTH = HY_WIDTH + GDN_HEADS * GDN_DV + RET_HEADS * RET_DV
FFN_HIDDEN = ((8 * D_MODEL + 3 * 256 - 1) // (3 * 256)) * 256
IN_SIZES = (
    3 * HY_WIDTH,
    2 * GDN_HEADS * GDN_DK + GDN_HEADS * GDN_DV,
    GDN_HEADS * GDN_DV,
    2 * GDN_HEADS,
    2 * GDN_HEADS,
    RET_HEADS * RET_DK,
    RET_HEADS * RET_DK,
    RET_HEADS * RET_DV,
    RET_HEADS * RET_DV,
)
IN_WIDTH = sum(IN_SIZES)

kernel_name = 'hybrid_hyena_gdn_retention_dit'

def rmsnorm(x, g):
    xf = x.astype(jnp.float32)
    y = xf * lax.rsqrt(jnp.mean(xf * xf, axis=-1, keepdims=True) + EPS)
    return (y * g.astype(jnp.float32)).astype(x.dtype)

def modulate(h, shift, scale):
    return h * (1 + scale) + shift

def split_cols(p, sizes):
    parts, start = [], 0
    for s in sizes:
        parts.append(p[..., start:start + s])
        start += s
    return parts

def short_conv(x, w):
    k_w = w.shape[0]
    pad = k_w // 2
    L = x.shape[1]
    xp = jnp.pad(x, ((0, 0), (pad, pad), (0, 0)))
    return sum(xp[:, j:j + L] * w[j] for j in range(k_w))

def to_heads(t, n_heads, d_head):
    b, l, _ = t.shape
    return t.reshape(b, l, n_heads, d_head).transpose(0, 2, 1, 3).astype(jnp.float32)

def l2norm(x):
    return x * lax.rsqrt(jnp.sum(x * x, axis=-1, keepdims=True) + EPS)

def hyena_filters(L, lp):
    pos = jnp.arange(L, dtype=jnp.float32)
    t = jnp.linspace(0.0, 1.0, L, dtype=jnp.float32)
    bands = (HY_EMB - 1) // 2
    f = jnp.linspace(1e-4, bands - 1, bands, dtype=jnp.float32)
    ang = (2.0 * math.pi / L) * pos[:, None] * f[None, :]
    z = jnp.concatenate([t[:, None], jnp.cos(ang), -jnp.sin(ang)], axis=-1)
    h = jnp.sin(lp['hy_f_freq1'] * (z @ lp['hy_f_w1'] + lp['hy_f_b1']))
    h = jnp.sin(lp['hy_f_freq2'] * (h @ lp['hy_f_w2'] + lp['hy_f_b2']))
    h = (h @ lp['hy_f_w3']).astype(jnp.float32).reshape(L, HY_ORDER, 2, HY_WIDTH)
    max_decay = math.log(HY_TARGET) / HY_FAST_DECAY
    min_decay = math.log(HY_TARGET) / HY_SLOW_DECAY
    deltas = jnp.abs(jnp.linspace(min_decay, max_decay, HY_WIDTH, dtype=jnp.float32))
    window = jnp.exp(-t[:, None] * deltas[None, :])
    return h * window[:, None, None, :]

def two_sided_kernel(h_pos, h_neg):
    return jnp.concatenate([h_pos, jnp.zeros_like(h_pos[:1]), h_neg[:0:-1]], axis=0)

def long_conv(u, kern):
    L = u.shape[1]
    uf = jnp.fft.rfft(u, n=2 * L, axis=1)
    kf = jnp.fft.rfft(kern, axis=0)
    return jnp.fft.irfft(uf * kf[None], n=2 * L, axis=1)[:, :L]

def hyena_mixer(p, lp):
    L = p.shape[1]
    p = (short_conv(p, lp['hy_conv_w']) + lp['hy_conv_b']).astype(jnp.float32)
    v, x1, x2 = jnp.split(p, 3, axis=-1)
    h = hyena_filters(L, lp)
    bias_d = lp['hy_bias'].astype(jnp.float32)
    z = v
    for n, gate in enumerate((x1, x2)):
        kern = two_sided_kernel(h[:, n, 0], h[:, n, 1])
        z = gate * (long_conv(z, kern) + z * bias_d[n])
    return z

def gdn_prepare(qkv, a, b, lp):
    qkv = jax.nn.silu(short_conv(qkv, lp['gdn_conv_w']))
    q, k, v = split_cols(qkv, (GDN_HEADS * GDN_DK, GDN_HEADS * GDN_DK, GDN_HEADS * GDN_DV))
    q = l2norm(to_heads(q, GDN_HEADS, GDN_DK)) * (GDN_DK ** -0.5)
    k = l2norm(to_heads(k, GDN_HEADS, GDN_DK))
    v = to_heads(v, GDN_HEADS, GDN_DV)
    bsz, L, _ = a.shape
    a = a.astype(jnp.float32).reshape(bsz, L, 2, GDN_HEADS)
    b = b.astype(jnp.float32).reshape(bsz, L, 2, GDN_HEADS)
    a_log = lp['gdn_a_log'].astype(jnp.float32)
    dt_bias = lp['gdn_dt_bias'].astype(jnp.float32)
    g = -jnp.exp(a_log) * jax.nn.softplus(a + dt_bias)
    beta = jax.nn.sigmoid(b)
    return q, k, v, g.transpose(2, 0, 3, 1), beta.transpose(2, 0, 3, 1)

def gated_delta_chunk(q, k, v, g, beta, s0):
    bsz, nh, L, dk = q.shape
    dv = v.shape[-1]
    n = L // CHUNK
    if s0 is None:
        s0 = jnp.zeros((bsz, nh, dk, dv), jnp.float32)
    q, k, v = (t.reshape(bsz, nh, n, CHUNK, t.shape[-1]) for t in (q, k, v))
    g, beta = (t.reshape(bsz, nh, n, CHUNK) for t in (g, beta))
    gc = jnp.cumsum(g, axis=-1)
    idx = jnp.arange(CHUNK)
    incl = idx[:, None] >= idx[None, :]
    strict = idx[:, None] > idx[None, :]
    decay = jnp.exp(jnp.where(incl, gc[..., :, None] - gc[..., None, :], -jnp.inf))
    kb = k * beta[..., None]
    lmat = jnp.where(strict, jnp.einsum('bhncd,bhnsd->bhncs', kb, k) * decay, 0.0)
    eye = jnp.eye(CHUNK, dtype=jnp.float32)
    t_inv = lax.linalg.triangular_solve(eye + lmat, jnp.broadcast_to(eye, lmat.shape),
                                        left_side=True, lower=True, unit_diagonal=True)
    u = jnp.einsum('bhncs,bhnsv->bhncv', t_inv, v * beta[..., None])
    w = jnp.einsum('bhncs,bhnsd->bhncd', t_inv, kb * jnp.exp(gc)[..., None])
    attn = jnp.einsum('bhncd,bhnsd->bhncs', q, k) * decay
    qg = q * jnp.exp(gc)[..., None]
    kg = k * jnp.exp(gc[..., -1:] - gc)[..., None]
    glast = jnp.exp(gc[..., -1])

    def step(s, xs):
        u_n, w_n, attn_n, qg_n, kg_n, gl_n = xs
        v_new = u_n - jnp.einsum('bhck,bhkv->bhcv', w_n, s)
        o = jnp.einsum('bhck,bhkv->bhcv', qg_n, s) + jnp.einsum('bhcs,bhsv->bhcv', attn_n, v_new)
        s = s * gl_n[..., None, None] + jnp.einsum('bhck,bhcv->bhkv', kg_n, v_new)
        return s, o

    xs = tuple(jnp.moveaxis(t, 2, 0) for t in (u, w, attn, qg, kg, glast))
    s, o = lax.scan(step, s0, xs)
    return jnp.moveaxis(o, 0, 2).reshape(bsz, nh, L, dv), s

def axial_rope_angles(rows_n):
    row = jnp.repeat(jnp.arange(rows_n, dtype=jnp.float32), GRID_W)
    col = jnp.tile(jnp.arange(GRID_W, dtype=jnp.float32), rows_n)
    nf = RET_DK // 4
    inv = ROPE_BASE ** (-jnp.arange(nf, dtype=jnp.float32) / nf)
    ang = jnp.concatenate([row[:, None] * inv, col[:, None] * inv], axis=-1)
    return jnp.cos(ang), jnp.sin(ang)

def apply_rope(x, cos, sin):
    x1, x2 = jnp.split(x, 2, axis=-1)
    return jnp.concatenate([x1 * cos - x2 * sin, x1 * sin + x2 * cos], axis=-1)

def ret_prepare(q, k, v, rope):
    q = to_heads(q, RET_HEADS, RET_DK)
    k = to_heads(k, RET_HEADS, RET_DK) * (RET_DK ** -0.5)
    v = to_heads(v, RET_HEADS, RET_DV)
    if rope is not None:
        q, k = apply_rope(q, *rope), apply_rope(k, *rope)
    return q, k, v

def retention_chunk(q, k, v, s0, log_gamma):
    bsz, nh, L, dk = q.shape
    dv = v.shape[-1]
    n = L // CHUNK
    if s0 is None:
        s0 = jnp.zeros((bsz, nh, dk, dv), jnp.float32)
    q, k, v = (t.reshape(bsz, nh, n, CHUNK, t.shape[-1]) for t in (q, k, v))
    idx = jnp.arange(CHUNK, dtype=jnp.float32)
    rel = idx[:, None] - idx[None, :]
    dmat = jnp.exp(jnp.where(rel >= 0, rel * log_gamma[:, None, None], -jnp.inf))
    scores = jnp.einsum('bhncd,bhnsd->bhncs', q, k) * dmat[None, :, None]
    inner = jnp.einsum('bhncs,bhnsv->bhncv', scores, v)
    qd = q * jnp.exp((idx + 1.0)[None, :] * log_gamma[:, None])[None, :, None, :, None]
    kd = k * jnp.exp((CHUNK - 1.0 - idx)[None, :] * log_gamma[:, None])[None, :, None, :, None]
    g_chunk = jnp.exp(CHUNK * log_gamma)[None, :, None, None]

    def step(s, xs):
        qd_n, kd_n, v_n = xs
        o = jnp.einsum('bhck,bhkv->bhcv', qd_n, s)
        s = s * g_chunk + jnp.einsum('bhck,bhcv->bhkv', kd_n, v_n)
        return s, o

    xs = tuple(jnp.moveaxis(t, 2, 0) for t in (qd, kd, v))
    s, o_cross = lax.scan(step, s0, xs)
    o = inner + jnp.moveaxis(o_cross, 0, 2)
    return o.reshape(bsz, nh, L, dv), s

def prefix_scan(scan_fn, ctx_seq, lat_seq, reverse):
    if reverse:
        ctx_seq = tuple(jnp.flip(t, 2) for t in ctx_seq)
        lat_seq = tuple(jnp.flip(t, 2) for t in lat_seq)
    o_ctx, s_ctx = scan_fn(*ctx_seq, None)
    o_lat, _ = scan_fn(*lat_seq, s_ctx)
    if reverse:
        o_ctx, o_lat = jnp.flip(o_ctx, 2), jnp.flip(o_lat, 2)
    return o_ctx, o_lat

def gdn_output(o, z, norm_g):
    bsz, nh, L, dv = o.shape
    o = o.transpose(0, 2, 1, 3)
    z = z.astype(jnp.float32).reshape(bsz, L, nh, dv)
    y = o * lax.rsqrt(jnp.mean(o * o, axis=-1, keepdims=True) + EPS) * norm_g.astype(jnp.float32)
    return (y * jax.nn.silu(z)).reshape(bsz, L, nh * dv)

def ret_output(o, gate):
    bsz, nh, L, dv = o.shape
    o = o.transpose(0, 2, 1, 3)
    mu = jnp.mean(o, axis=-1, keepdims=True)
    var = jnp.mean(jnp.square(o - mu), axis=-1, keepdims=True)
    y = ((o - mu) * lax.rsqrt(var + EPS)).reshape(bsz, L, nh * dv)
    return y * jax.nn.silu(gate.astype(jnp.float32))

def token_mixers(h_lat, h_ctx, rope, lp, need_ctx):
    lat = split_cols(h_lat @ lp['w_in'], IN_SIZES)
    ctx = split_cols(h_ctx @ lp['w_in'], IN_SIZES)
    hy_lat = hyena_mixer(lat[0], lp)
    q_l, k_l, v_l, g_l, b_l = gdn_prepare(lat[1], lat[3], lat[4], lp)
    q_c, k_c, v_c, g_c, b_c = gdn_prepare(ctx[1], ctx[3], ctx[4], lp)
    gc_f, gl_f = prefix_scan(gated_delta_chunk, (q_c, k_c, v_c, g_c[0], b_c[0]),
                             (q_l, k_l, v_l, g_l[0], b_l[0]), reverse=False)
    gc_b, gl_b = prefix_scan(gated_delta_chunk, (q_c, k_c, v_c, g_c[1], b_c[1]),
                             (q_l, k_l, v_l, g_l[1], b_l[1]), reverse=True)
    log_gamma = jax.nn.log_sigmoid(lp['ret_decay_logit'].astype(jnp.float32))
    rq_l, rk_l, rv_l = ret_prepare(lat[5], lat[6], lat[7], rope)
    rq_c, rk_c, rv_c = ret_prepare(ctx[5], ctx[6], ctx[7], None)
    rc_f, rl_f = prefix_scan(functools.partial(retention_chunk, log_gamma=log_gamma[0]),
                             (rq_c, rk_c, rv_c), (rq_l, rk_l, rv_l), reverse=False)
    rc_b, rl_b = prefix_scan(functools.partial(retention_chunk, log_gamma=log_gamma[1]),
                             (rq_c, rk_c, rv_c), (rq_l, rk_l, rv_l), reverse=True)
    dt = h_lat.dtype
    y_lat = jnp.concatenate([hy_lat,
                             gdn_output(gl_f + gl_b, lat[2], lp['gdn_norm_g']),
                             ret_output(rl_f + rl_b, lat[8])], axis=-1).astype(dt) @ lp['w_out']
    y_ctx = None
    if need_ctx:
        y_ctx = jnp.concatenate([hyena_mixer(ctx[0], lp),
                                 gdn_output(gc_f + gc_b, ctx[2], lp['gdn_norm_g']),
                                 ret_output(rc_f + rc_b, ctx[8])], axis=-1).astype(dt) @ lp['w_out']
    return y_lat, y_ctx

def swiglu(h, lp):
    gate, up = jnp.split(h @ lp['ffn_w_in'], 2, axis=-1)
    return (jax.nn.silu(gate) * up) @ lp['ffn_w_out']

def trunk_layer(x, ctx, c, c_ctx, rope, lp, need_ctx):
    d = x.shape[-1]
    mod_lat = (jax.nn.silu(c) @ lp['mod_w'] + lp['mod_b']).reshape(c.shape[0], N_MOD, 1, d)
    mod_ctx = (jax.nn.silu(c_ctx) @ lp['mod_w'] + lp['mod_b']).reshape(N_MOD, d)
    h_lat = modulate(rmsnorm(x, lp['norm1_g']), mod_lat[:, 0], mod_lat[:, 1])
    h_ctx = modulate(rmsnorm(ctx, lp['norm1_g']), mod_ctx[0], mod_ctx[1])
    y_lat, y_ctx = token_mixers(h_lat, h_ctx, rope, lp, need_ctx)
    x = x + mod_lat[:, 2] * y_lat
    x = x + mod_lat[:, 5] * swiglu(modulate(rmsnorm(x, lp['norm2_g']), mod_lat[:, 3], mod_lat[:, 4]), lp)
    if need_ctx:
        ctx = ctx + mod_ctx[2] * y_ctx
        ctx = ctx + mod_ctx[5] * swiglu(modulate(rmsnorm(ctx, lp['norm2_g']), mod_ctx[3], mod_ctx[4]), lp)
    return x, ctx

def setup_inputs(seed: int = 0) -> dict:
    key = jax.random.key(seed)
    it = iter(jax.random.split(key, 32))
    f32 = jnp.float32

    def nrm(shape, scale):
        return scale * jax.random.normal(next(it), shape, f32)

    D = D_MODEL
    qkv_w = 2 * GDN_HEADS * GDN_DK + GDN_HEADS * GDN_DV
    gamma0 = 1.0 - 2.0 ** (-5.0 - jnp.arange(RET_HEADS, dtype=f32))
    dt0 = jnp.exp(jax.random.uniform(next(it), (DEPTH, 2, GDN_HEADS), f32, math.log(1e-3), math.log(1e-1)))
    return {
        'x': nrm((BATCH, SEQ, D), 1.0),
        'c': nrm((BATCH, D), 1.0),
        'ctx': nrm((BATCH, CTX_LEN, D), 1.0),
        'c_ctx': nrm((D,), 1.0),
        'mod_w': nrm((DEPTH, D, N_MOD * D), 0.5 * D ** -0.5),
        'mod_b': nrm((DEPTH, N_MOD * D), 0.02),
        'norm1_g': 1.0 + nrm((DEPTH, D), 0.02),
        'w_in': nrm((DEPTH, D, IN_WIDTH), D ** -0.5),
        'hy_conv_w': nrm((DEPTH, HY_SHORT, 3 * HY_WIDTH), HY_SHORT ** -0.5),
        'hy_conv_b': nrm((DEPTH, 3 * HY_WIDTH), 0.02),
        'hy_f_w1': nrm((DEPTH, HY_EMB, HY_HIDDEN), HY_EMB ** -0.5),
        'hy_f_b1': nrm((DEPTH, HY_HIDDEN), 0.02),
        'hy_f_freq1': 1.0 + nrm((DEPTH, HY_HIDDEN), 0.02),
        'hy_f_w2': nrm((DEPTH, HY_HIDDEN, HY_HIDDEN), HY_HIDDEN ** -0.5),
        'hy_f_b2': nrm((DEPTH, HY_HIDDEN), 0.02),
        'hy_f_freq2': 1.0 + nrm((DEPTH, HY_HIDDEN), 0.02),
        'hy_f_w3': nrm((DEPTH, HY_HIDDEN, HY_ORDER * 2 * HY_WIDTH), 0.05 * HY_HIDDEN ** -0.5),
        'hy_bias': nrm((DEPTH, HY_ORDER, HY_WIDTH), 0.5),
        'gdn_conv_w': nrm((DEPTH, GDN_SHORT, qkv_w), GDN_SHORT ** -0.5),
        'gdn_a_log': jnp.log(jax.random.uniform(next(it), (DEPTH, 2, GDN_HEADS), f32, 1.0, 16.0)),
        'gdn_dt_bias': dt0 + jnp.log(-jnp.expm1(-dt0)),
        'gdn_norm_g': 1.0 + nrm((DEPTH, GDN_DV), 0.02),
        'ret_decay_logit': jnp.log(gamma0 / (1.0 - gamma0)) + nrm((DEPTH, 2, RET_HEADS), 0.1),
        'w_out': nrm((DEPTH, MIX_WIDTH, D), MIX_WIDTH ** -0.5),
        'norm2_g': 1.0 + nrm((DEPTH, D), 0.02),
        'ffn_w_in': nrm((DEPTH, D, 2 * FFN_HIDDEN), D ** -0.5),
        'ffn_w_out': nrm((DEPTH, FFN_HIDDEN, D), FFN_HIDDEN ** -0.5),
        'final_norm_g': 1.0 + nrm((D,), 0.02),
    }

def reference(x, c, ctx, c_ctx, mod_w, mod_b, norm1_g, w_in, hy_conv_w, hy_conv_b, hy_f_w1, hy_f_b1,
              hy_f_freq1, hy_f_w2, hy_f_b2, hy_f_freq2, hy_f_w3, hy_bias, gdn_conv_w, gdn_a_log,
              gdn_dt_bias, gdn_norm_g, ret_decay_logit, w_out, norm2_g, ffn_w_in, ffn_w_out, final_norm_g):
    rows_n = x.shape[1] // GRID_W
    rope = axial_rope_angles(rows_n)
    for i in range(DEPTH):
        lp = {
            'mod_w': mod_w[i], 'mod_b': mod_b[i], 'norm1_g': norm1_g[i], 'w_in': w_in[i],
            'hy_conv_w': hy_conv_w[i], 'hy_conv_b': hy_conv_b[i],
            'hy_f_w1': hy_f_w1[i], 'hy_f_b1': hy_f_b1[i], 'hy_f_freq1': hy_f_freq1[i],
            'hy_f_w2': hy_f_w2[i], 'hy_f_b2': hy_f_b2[i], 'hy_f_freq2': hy_f_freq2[i],
            'hy_f_w3': hy_f_w3[i], 'hy_bias': hy_bias[i],
            'gdn_conv_w': gdn_conv_w[i], 'gdn_a_log': gdn_a_log[i], 'gdn_dt_bias': gdn_dt_bias[i],
            'gdn_norm_g': gdn_norm_g[i], 'ret_decay_logit': ret_decay_logit[i],
            'w_out': w_out[i], 'norm2_g': norm2_g[i], 'ffn_w_in': ffn_w_in[i], 'ffn_w_out': ffn_w_out[i],
        }
        x, ctx = trunk_layer(x, ctx, c, c_ctx, rope, lp, need_ctx=(i < DEPTH - 1))
    return rmsnorm(x, final_norm_g)


_drawn_inputs = setup_inputs


def setup_inputs(seed=0):
    import zlib

    import numpy as np

    out = dict(_drawn_inputs(seed))
    spreads = {}
    factors = {'norm1_g': 6.278,
     'hy_conv_b': 8.0,
     'hy_f_b1': 8.0,
     'hy_f_freq1': 8.0,
     'hy_f_b2': 8.0,
     'hy_f_freq2': 8.0,
     'gdn_norm_g': 8.0,
     'norm2_g': 6.773,
     'final_norm_g': 3.12}
    for name, (base, spread) in spreads.items():
        noise = np.random.default_rng([zlib.crc32(name.encode()), seed]).standard_normal(out[name].shape)
        drawn = base * np.exp(spread * noise) if base else spread * noise
        out[name] = jnp.asarray(drawn.astype(out[name].dtype))
    for name, factor in factors.items():
        out[name] = (out[name] * factor).astype(out[name].dtype)
    return out
```

```python
import math
from contextlib import ExitStack

import numpy as np

import concourse.bass as bass
from concourse import mybir

F32 = mybir.dt.float32
BF16 = mybir.dt.bfloat16
ALU = mybir.AluOpType
ACT = mybir.ActivationFunctionType

P = 128
D = 1024
DC = D // P
CTX = 256
LAT = 512
TOK = CTX + LAT
DEPTH = 2
FF = 2816
FC = FF // P
HYW = 256
HEADS = 4
EPS = 1e-6
NLEV = 7
CHUNKS = TOK // P
SEG = {"ctx": (0, CTX), "lat": (CTX, LAT)}
BLK = 2048
RING = 4

HY_COL, QKV_COL, Z_COL, AB_COL = 0, 768, 2304, 2816
RQ_COL, RK_COL, RV_COL, RG_COL = 2832, 3088, 3344, 3600
N_MODB, N_OUTB, N_FIB, N_FOB = 24, 4, FC, 2 * DC
IN_BLOCKS = [HY_COL, HY_COL + 256, HY_COL + 512, RQ_COL, RK_COL, RV_COL, RG_COL] \
    + [QKV_COL + 256 * i for i in range(6)] + [Z_COL, Z_COL + 256]
N_INB = len(IN_BLOCKS)

MODB, N1G, N2G, FNG = 0, 48, 56, 64
HCW, HCB, GCW, GNG = 72, 90, 96, 132
ALOG, DTB, RLOG, EPSC, LNQ = 136, 144, 152, 160, 161
NPAR = 164

IDENT, ONES, PERM, BD64, LE, GT, GE, LT = range(8)

FW1, FW2, FW3, FVEC, FBIAS = 0, 64, 128, 1152, 1156
NFP = FBIAS + 512

MAGIC = 1.5 * 2.0 ** 23
TWO_PI_HI = 6.28125
TWO_PI_LO = 2 * math.pi - 6.28125
PI_IN = 3.1415925

WORK = 22528 + 160
W_TAB, W_K, W_CONV, W_RAW, W_TOK = 0, 8192, 14336, 17408, 19724
W_RQK, W_RV, W_RC, W_ROPE, W_D, W_DT, W_P = 0, 3072, 4608, 8576, 9600, 12672, 14208
W_RM = 17280
W_QKV, W_G, W_GRAW = 0, 9216, 9216
RC_POS, RC_NEG, RC_EYE, RC_CF, RC_CB = 0, 896, 1792, 2688, 3328


class Steps:

    def __init__(self, sem, name, values):
        self.sem, self.name, self.values, self.n = sem, name, values, 0

    def did(self, key=None):
        self.n += 1
        if key is not None:
            self.values[(self.name, key)] = self.n
        return self.sem, 1

    def at(self, *key):
        return self.sem, self.values.get((self.name, key[0] if len(key) == 1 else key), 1)


def backbone(nc, values, tokens, cond, weights, w_ab, layer_params, filter_params, mats, level_masks,
             tab_lat, tab_ctx, win_lat, win_ctx, zpos, ret_tab, rope_tab, out):
    with ExitStack() as stack:
        def sb(name, shape, dt=F32):
            return stack.enter_context(nc.sbuf_tensor(name, shape, dt))

        def semaphore(name):
            return stack.enter_context(nc.semaphore(name))

        xT = sb("xT", [P, DC, TOK])
        hT = sb("hT", [P, DC, TOK])
        mix = sb("mix", [P, DC, TOK])
        ring = sb("ring", [P, RING, BLK])
        work = sb("work", [P, WORK])
        mat = sb("mat", [P, 8, P])
        lev = sb("lev", [P, 2, NLEV, P], BF16)
        par = sb("par", [P, NPAR])
        wab = sb("wab", [P, DC * 16])
        condT = sb("condT", [P, DC, 2])
        modv = sb("modv", [P, 48, 2])
        amp = sb("amp", [P, 2, DC, 2])
        rstd = sb("rstd", [P, TOK])
        gs = sb("gs", [P, 10, CHUNKS, 8])
        lam = sb("lam", [P, 4, 8])
        ps = stack.enter_context(nc.psum_tensor("ps", [P, 8, 512], F32))

        mixf = mix[:, :, :].rearrange("p a b -> p (a b)")
        hTf = hT[:, :, :].rearrange("p a b -> p (a b)")

        def wk(at, *shape):
            n = int(np.prod(shape))
            v = work[:, at:at + n]
            if len(shape) == 2:
                return v.rearrange("p (a b) -> p a b", b=shape[1])
            if len(shape) == 3:
                return v.rearrange("p (a b c) -> p a b c", b=shape[1], c=shape[2])
            return v

        ident = mat[:, IDENT, :]
        ones = mat[:, ONES, :]
        eps = par[:, EPSC:EPSC + 1]
        lnq = par[:, LNQ:LNQ + 1]

        landed = [semaphore(f"weights_landed_{i}") for i in range(RING)]
        params_in = semaphore("params_in")
        tables_in = semaphore("tables_in")
        start_in = semaphore("start_in")
        stored = semaphore("out_stored")

        PARTS = ("proj", "hyena", "ret", "gdn")
        engines = ("tensor", "vector", "scalar", "pool")
        S = {(e, p): Steps(semaphore(f"{e}_{p}_steps"), f"{e}_{p}", values) for e in engines for p in PARTS}

        def close(e, stage):
            for p in PARTS:
                values[(e, p, stage)] = S[e, p].n

        def fence(eng, stage):
            for e in engines:
                for p in PARTS:
                    v = values.get((e, p, stage), 0)
                    if v:
                        eng.wait_ge(S[e, p].sem, v)

        def stages():
            for l in range(DEPTH):
                yield "mod", l
                yield "norm1", l
                for seg in (("lat", "ctx") if l == 0 else ("lat",)):
                    yield "filter_" + seg, l
                    if seg == "lat":
                        yield "hy_proj", l
                    yield "conv_" + seg, l
                yield "ret_proj", l
                yield "ret", l
                yield "gdn_proj", l
                yield "gdn_prep", l
                yield "gdn", l
                yield "gdn_out", l
                yield "out", l
                yield "norm2", l
                yield "ffn_in", l
                yield "ffn_out", l
            yield "final", DEPTH - 1

        ORDER = list(stages())

        def before(stage):
            i = ORDER.index(stage)
            return ORDER[i - 1] if i else None

        def block_no(l, part, i):
            base = l * (N_MODB + N_INB + N_OUTB + N_FIB + N_FOB)
            off = {"mod": 0, "in": N_MODB, "out": N_MODB + N_INB, "fi": N_MODB + N_INB + N_OUTB,
                   "fo": N_MODB + N_INB + N_OUTB + N_FIB}[part]
            return base + off + i
        NBLK = DEPTH * (N_MODB + N_INB + N_OUTB + N_FIB + N_FOB)

        def wait_block(eng, n):
            eng.wait_ge(landed[n % RING], 16 * (n // RING + 1))

        def segs(l, both=False):
            return ["lat", "ctx"] if (l == 0 or both) else ["lat"]

        def tables(s):
            n = SEG[s][1]
            return work[:, W_TAB:W_TAB + 4 * (n // P) * n].rearrange("p (i t f) -> p i t f", i=4, f=n)

        def sum_diff(s):
            n = SEG[s][1] // P
            at = W_CONV if s == "lat" else W_TOK
            return work[:, at:at + 2 * n * 512].rearrange("p (i t c) -> p i t c", i=2, c=512)

        def halves(s):
            at = W_TOK if s == "lat" else W_RAW
            return wk(at, 2, 512), wk(at + 1024, 2, 512)

        def products():
            return mixf[:, 1536:1536 + 2048].rearrange("p (i c) -> p i c", c=512)

        def spectrum():
            return wk(W_K, 4, 2 * 768)

        def tables_count(stage, l):
            n = 0
            for st, k in ORDER:
                if st.startswith("filter_"):
                    n += 4
                elif st == "ret":
                    n += 2
                if (st, k) == (stage, l):
                    return 16 * n

        def ret_work(l):
            for s in segs(l):
                for h in range(HEADS):
                    yield s, h, (list(range(CHUNKS)) if s == "lat" else [0, 1])

        def ret_unit(l, s, h, i):
            return h * CHUNKS + i if s == "lat" else HEADS * CHUNKS + 2 * h + i

        def ret_out(s, p):
            w = SEG[s][1]
            v = work[:, W_RM:W_RM + 4 * 512].rearrange("p (i t) -> p i t", i=4)
            return [v[:, i, 0:w] for i in range(4)]

        def norm_units(l):
            for c in range(8):
                for s in segs(l, both=(c >= 4)):
                    yield c, s

        def out_units(l):
            for h in range(HEADS):
                for s in segs(l):
                    yield h, s

        def chunk_of(n, d):
            if d == 0:
                return n
            return 1 - n if n < 2 else CHUNKS + 1 - n

        def group(d):
            names = ["decm", "bdec", "kbg", "kg", "vb", "qg", "L", "attn", "LT", "attnT", "qgT", "X", "Y"]
            at = W_G + d * len(names) * 512
            g = {k: wk(at + 512 * i, HEADS, P) for i, k in enumerate(names)}
            g["Ag"] = g["vn"] = g["bdec"]
            g["nwT"] = g["decm"]
            g["P"] = g["qg"]
            g["NT"] = [g["attn"], g["L"]]
            for i, k in enumerate(("S", "Sgl")):
                o = 3072 + (2 * d + i) * 512
                g[k] = hTf[:, o:o + 512].rearrange("p (h c) -> p h c", c=P)
            return g

        oacc = hTf[:, 0:4 * TOK].rearrange("p (h t) -> p h t", t=TOK)

        def per_head(v):
            return v.unsqueeze(2).broadcast_to([P, HEADS, P])

        def all_heads(m):
            return m.unsqueeze(1).broadcast_to([P, HEADS, P])

        def decay_of(h):
            return (work[:, W_D + 1536 * (h % 2):W_D + 1536 * (h % 2) + 1536], work[:, W_DT:W_DT + 1536])

        def ctx_decay(h):
            return work[:, W_CD + 384 * h - 256:W_CD + 384 * h + 640]

        block = stack.enter_context(nc.Block())

        @block.sync
        def _(sp):
            sp.dma_start(condT[:, :, :], cond).then_inc(start_in, 16)
            sp.dma_start(xT[:, :, :], tokens).then_inc(start_in, 16)
            sp.dma_start(mat[:, :, :], mats).then_inc(start_in, 16)
            sp.dma_start(lev[:, :, :, :], level_masks).then_inc(start_in, 16)
            for n in range(NBLK):
                if n >= RING:
                    sp.wait_ge(*S["tensor", "proj"].at("block", n - RING))
                sp.dma_start(ring[:, n % RING, :], weights[n, :, :]).then_inc(landed[n % RING], 16)
            sp.wait_ge(*S["vector", "proj"].at("final", 7))
            sp.dma_start(out, hT[:, :, CTX:TOK]).then_inc(stored, 16)
            sp.wait_ge(stored, 16)

        @block.tensor
        def _(pe):
            T = S["tensor", "proj"]
            V = S["vector", "proj"]
            A = S["scalar", "proj"]

            def mod(l):
                if l == 0:
                    pe.wait_ge(start_in, 64)
                pe.wait_ge(*A.at("silu_c"))
                for b in range(N_MODB):
                    n = block_no(l, "mod", b)
                    wait_block(pe, n)
                    w = ring[:, n % RING, :].rearrange("p (k c) -> p k c", k=DC)
                    for m in range(2):
                        for k in range(DC):
                            mm = pe.matmul(ps[:, 7, 4 * b + 2 * m:4 * b + 2 * m + 2], w[:, k, P * m:P * m + P],
                                           condT[:, k, :], start=(k == 0), stop=(k == DC - 1))
                    mm.then_inc(*T.did(("block", n)))

            def norm(name, l, sgs):
                for s in sgs:
                    t0, w = SEG[s]
                    for k in range(DC):
                        pe.wait_ge(*A.at(name, l, s, "sq", k))
                        mm = pe.matmul(ps[:, 0 if s == "lat" else 1, 0:w], ones, hT[:, k, t0:t0 + w],
                                       start=(k == 0), stop=(k == DC - 1))
                    mm.then_inc(*T.did((name, l, s)))

            def product(name, l, item, m, n, s, src, kc, free, cols=None):
                t0, w = SEG[s]
                bank = item % 3 + (0 if s == "lat" else 3)
                if free is not None:
                    pe.wait_ge(*free)
                wv = ring[:, n % RING, :].rearrange("p (k c) -> p k c", c=256)
                for k in range(kc):
                    mm = pe.matmul(ps[:, bank, 0:w], wv[:, k, P * m:P * m + P], src[:, k, t0:t0 + w],
                                   start=(k == 0), stop=(k == kc - 1))
                mm.then_inc(*T.did((name, l, item, s)))

            def columns(name, l, part, blocks, sgs_of, src, evac, kc=DC):
                item = 0
                for b in blocks:
                    n = block_no(l, part, b)
                    wait_block(pe, n)
                    for m in range(2):
                        ss = sgs_of(item)
                        for s in ss:
                            free = evac(item - 3, s) if item >= 3 and s in sgs_of(item - 3) else None
                            product(name, l, item, m, n, s, src, kc, free)
                        item += 1
                    T.values[(T.name, ("block", n))] = T.n

            def hy_proj(l):
                columns("hy", l, "in", range(0, 3), lambda i: segs(l), hT,
                        lambda i, s: A.at("hy", l, i, s))

            def ret_proj(l):
                both = lambda i: segs(l, both=(i in (2, 3)))
                columns("ret", l, "in", (3, 4), both, hT, lambda i, s: A.at("ret", l, i, s))
                n = block_no(l, "in", 5)
                wait_block(pe, n)
                wv = ring[:, n % RING, :].rearrange("p (k c) -> p k c", c=256)
                for c in range(CHUNKS):
                    bank = 6 + c % 2
                    if c >= 2:
                        pe.wait_ge(*V.at("rv", l, c - 2))
                    for k in range(DC):
                        mm = pe.matmul(ps[:, bank, 0:256], hT[:, k, P * c:P * c + P], wv[:, k, :],
                                       start=(k == 0), stop=(k == DC - 1))
                    mm.then_inc(*T.did(("rv", l, c)))
                T.values[(T.name, ("block", n))] = T.n
                n = block_no(l, "in", 6)
                wait_block(pe, n)
                for m in range(2):
                    for s in segs(l):
                        item = 4 + m
                        free = A.at("ret", l, item - 3, s) if s in both(item - 3) else None
                        product("ret", l, item, m, n, s, hT, DC, free)
                T.values[(T.name, ("block", n))] = T.n

            def gdn_proj(l):
                pe.wait_ge(params_in, 32 * (l + 1))
                for c in range(CHUNKS):
                    for k in range(DC):
                        mm = pe.matmul(ps[:, 6, 16 * c:16 * c + 16], hT[:, k, P * c:P * c + P],
                                       wab[:, 16 * k:16 * k + 16], start=(k == 0), stop=(k == DC - 1))
                mm.then_inc(*T.did(("ab", l)))
                columns("gd", l, "in", range(7, 15), lambda i: segs(l, both=(4 <= i < 12)), hT,
                        lambda i, s: A.at("gd", l, i, s))

            def out_proj(l):
                columns("out", l, "out", range(4), lambda i: segs(l), mix,
                        lambda i, s: V.at("out", l, i, s))

            def ffn_in(l):
                columns("fi", l, "fi", range(FC), lambda i: segs(l), hT,
                        lambda i, s: A.at("fi", l, i // 2, s) if i % 2 == 0 else V.at("fi", l, i, s))

            def ffn_out(l):
                hid = wk(0, FC, TOK)
                for item in range(DC):
                    for half in range(2):
                        n = block_no(l, "fo", 2 * item + half)
                        wait_block(pe, n)
                        wv = ring[:, n % RING, 0:11 * P].rearrange("p (k c) -> p k c", c=P)
                        for s in segs(l):
                            t0, w = SEG[s]
                            bank = item % 3 + (0 if s == "lat" else 3)
                            if half == 0 and item >= 3:
                                pe.wait_ge(*V.at("fo", l, item - 3, s))
                            for k in range(11):
                                mm = pe.matmul(ps[:, bank, 0:w], wv[:, k, :], hid[:, 11 * half + k, t0:t0 + w],
                                               start=(half == 0 and k == 0), stop=(half == 1 and k == 10))
                            mm.then_inc(*T.did(("fo", l, item, half, s)))
                        T.values[(T.name, ("block", n))] = T.n

            TH, VH, AH, GH = (S[e, "hyena"] for e in engines)

            def filters(l, s):
                L = SEG[s][1]
                nt = L // P
                o = 0 if s == "lat" else 1536
                fp = mixf[0:64, o:o + NFP]
                zT = mixf[0:64, o + NFP:o + NFP + L]
                hb = mixf[0:64, o + NFP + L:o + NFP + 2 * L]
                pe.wait_ge(tables_in, tables_count("filter_" + s, l))
                pe.matmul(ps[0:64, 0, 0:L], fp[:, FW1:FW1 + 64], zT, start=True, stop=True)\
                    .then_inc(*TH.did((l, s, "h1")))
                pe.wait_ge(*AH.at(l, s, "sin", 0))
                pe.matmul(ps[0:64, 1, 0:L], fp[:, FW2:FW2 + 64], hb, start=True, stop=True)\
                    .then_inc(*TH.did((l, s, "h2")))
                pe.wait_ge(*AH.at(l, s, "sin", 1))
                for t in range(nt):
                    if t >= 2:
                        pe.wait_ge(*VH.at(l, s, "hn", t - 2))
                    for a in range(2):
                        mm = pe.matmul(ps[:, 2 + 2 * (t % 2) + a, :], hb[:, P * t:P * t + P],
                                       fp[:, FW3 + 512 * a:FW3 + 512 * a + 512], start=True, stop=True)
                    mm.then_inc(*TH.did((l, s, "h3", t)))
                tab = tables(s)
                sd = sum_diff(s)
                pe.wait_ge(*VH.at(l, s, "bias"))
                pe.wait_ge(*GH.at(l, s, "diff", nt - 1))
                for j in range(nt):
                    for i, b in ((0, 6), (1, 7)):
                        if j >= 1:
                            pe.wait_ge(*AH.at(l, s, "K", i, j - 1))
                        for t in range(nt):
                            mm = pe.matmul(ps[:, b, :], tab[:, i, t, P * j:P * j + P], sd[:, i, t, :],
                                           start=(t == 0), stop=(t == nt - 1))
                        mm.then_inc(*TH.did((l, s, "K", i, j)))

            def long_conv(l, s):
                t0, L = SEG[s]
                nt = L // P
                tab = tables(s)
                conv = wk(W_CONV, 4, TOK)
                tok = wk(W_TOK, 4, 512)
                yf = wk(W_RAW, 4, 512)
                for t in range(nt):
                    if t >= 2:
                        pe.wait_ge(*AH.at(l, s, "tok", t - 2))
                    for c in range(4):
                        mm = pe.transpose(ps[:, t % 2, P * c:P * c + P], conv[:, c, t0 + P * t:t0 + P * t + P], ident)
                    mm.then_inc(*TH.did((l, s, "tok", t)))
                for n in range(2):
                    if n == 0:
                        pe.wait_ge(*AH.at(l, s, "tok", nt - 1))
                    else:
                        pe.wait_ge(*VH.at(l, s, "z1", nt - 1))
                    for j in range(nt):
                        if j >= 2:
                            pe.wait_ge(*VH.at(l, s, n, "p2", j - 2))
                        for i in range(2):
                            for t in range(nt):
                                mm = pe.matmul(ps[:, 2 + j % 2, 256 * i:256 * i + 256],
                                               tab[:, i, t, P * j:P * j + P], tok[:, t, 0:256],
                                               start=(t == 0), stop=(t == nt - 1))
                        mm.then_inc(*TH.did((l, s, n, "U", j)))
                    pe.wait_ge(*GH.at(l, s, n, "Y", nt - 1))
                    if n == 0:
                        for t in range(nt):
                            if t >= 2:
                                pe.wait_ge(*VH.at(l, s, "z1", t - 2))
                            for j in range(nt):
                                for i in range(2):
                                    mm = pe.matmul(ps[:, 4 + t % 2, 0:256], tab[:, 2 + i, j, P * t:P * t + P],
                                                   yf[:, j, 256 * i:256 * i + 256],
                                                   start=(i == 0 and j == 0), stop=(i == 1 and j == nt - 1))
                            mm.then_inc(*TH.did((l, s, "y1", t)))
                    else:
                        for c in range(2):
                            for j in range(nt):
                                for i in range(2):
                                    mm = pe.matmul(ps[:, 6 + c, 0:L], yf[:, j, 256 * i + P * c:256 * i + P * c + P],
                                                   tab[:, 2 + i, j, :],
                                                   start=(i == 0 and j == 0), stop=(i == 1 and j == nt - 1))
                            mm.then_inc(*TH.did((l, s, "y2", c)))

            TR, VR, AR, GR = (S[e, "ret"] for e in engines)

            def retention(l):
                rqk = wk(W_RQK, 4, TOK)
                rv = wk(W_RV, CHUNKS, 256)
                pr = wk(W_P, 6, 512)
                pe.wait_ge(tables_in, tables_count("ret", l))
                for c in range(4):
                    pe.matmul(ps[:, c, :], mat[:, PERM, :], rqk[:, c, CTX:TOK], start=True, stop=True)\
                        .then_inc(*TR.did((l, "perm", c)))
                pe.wait_ge(*VR.at(l, "rope", 3))
                for s, h, chunks in ret_work(l):
                    t0, w = SEG[s]
                    r = 64 * (h % 2)
                    obank = (6 if s == "lat" else 4) + h // 2

                    def score(i):
                        c = chunks[i]
                        u = ret_unit(l, s, h, i)
                        if u >= 4:
                            pe.wait_ge(*VR.at(l, "P", u - 4))
                        pe.matmul(ps[:, u % 4, 0:w], rqk[r:r + 64, 2 + h // 2, P * c:P * c + P],
                                  rqk[r:r + 64, h // 2, t0:t0 + w], start=True, stop=True)\
                            .then_inc(*TR.did((l, "S", u)))

                    def pv(i):
                        u = ret_unit(l, s, h, i)
                        pe.wait_ge(*VR.at(l, "P", u))
                        pe.matmul(ps[r:r + 64, obank, 0:w], rv[:, chunks[i], 64 * h:64 * h + 64], pr[:, u % 6, 0:w],
                                  start=(i == 0), stop=(i == len(chunks) - 1))\
                            .then_inc(*TR.did((l, "PV", u)))
                    for i in range(len(chunks) + 2):
                        if i < len(chunks):
                            score(i)
                        if i >= 2:
                            pv(i - 2)
                for s in segs(l):
                    w = SEG[s][1]
                    for p in range(2):
                        oc, cc, sq, rs = ret_out(s, p)
                        b = p
                        pe.wait_ge(*AR.at(l, s, p, "oc"))
                        pe.matmul(ps[:, b, 0:w], mat[:, BD64, :], oc, start=True, stop=True)\
                            .then_inc(*TR.did((l, s, p, "mu")))
                        pe.wait_ge(*AR.at(l, s, p, "sq"))
                        pe.matmul(ps[:, 2 + b, 0:w], mat[:, BD64, :], sq, start=True, stop=True)\
                            .then_inc(*TR.did((l, s, p, "var")))

            TG, VG, AG, GG = (S[e, "gdn"] for e in engines)

            def gdn_prep(l):
                pe.wait_ge(*VG.at(l, "g"))
                g = gs[:, 0, :, :]
                for d in range(2):
                    gd = g[:, :, 4 * d:4 * d + 4]
                    for i, m in enumerate((LE if d == 0 else GE, GT if d == 0 else LT, ONES)):
                        mm = pe.matmul(ps[:, 7, (3 * d + i) * 24:(3 * d + i) * 24 + 24]
                                       .rearrange("p (c h) -> p c h", h=4), mat[:, m, :], gd,
                                       start=True, stop=True)
                mm.then_inc(*TG.did((l, "gc")))
                for u, (c, s) in enumerate(norm_units(l)):
                    t0, w = SEG[s]
                    if u >= 2:
                        pe.wait_ge(*AG.at(l, "ln", u - 2))
                    pe.wait_ge(*AG.at(l, "nsq", u))
                    pe.matmul(ps[:, u % 2, 0:w], ones, wk(W_G, 2, 512)[:, u % 2, 0:w], start=True, stop=True)\
                        .then_inc(*TG.did((l, "nrm", u)))

            def four(out_, lhs, rhs, start=True, stop=True, skip=False):
                for h in range(HEADS):
                    mm = pe.matmul(out_[:, P * h:P * h + P], lhs(h), rhs(h), start=start, stop=stop)
                return mm

            def gdn(l):
                qkv = wk(W_QKV, 12, TOK)
                for n in range(CHUNKS):
                    G = [group(d) for d in range(2)]
                    need_o = [l == 0 or n >= 2] * 2
                    for d in range(2):
                        c = chunk_of(n, d)
                        B = [ps[:, 4 * d + i, :] for i in range(4)]
                        cs = slice(P * c, P * c + P)
                        if n >= 1:
                            if l == 0 or n - 1 >= 2:
                                pe.wait_ge(*VG.at(l, n - 1, d, "o"))
                            pe.wait_ge(*VG.at(l, n - 1, d, "S"))
                        for i, off in ((0, 4), (1, 8), (2, 0)):
                            if i == 2 and not need_o[d]:
                                continue
                            for h in range(HEADS):
                                mm = pe.transpose(B[i][:, P * h:P * h + P], qkv[:, off + h, cs], ident)
                            mm.then_inc(*TG.did((l, n, d, "tok", i)))
                        pe.wait_ge(*GG.at(l, n, d, "Ag"))
                        four(B[3], lambda h: G[d]["Ag"][:, h, :], lambda h: mat[:, GT if d == 0 else LT, :])\
                            .then_inc(*TG.did((l, n, d, "dec")))
                    for d in range(2):
                        c = chunk_of(n, d)
                        B = [ps[:, 4 * d + i, :] for i in range(4)]
                        cs = slice(P * c, P * c + P)
                        pe.wait_ge(*VG.at(l, n, d, "kg"))
                        four(B[0], lambda h: qkv[:, 4 + h, cs], lambda h: qkv[:, 4 + h, cs])\
                            .then_inc(*TG.did((l, n, d, "G")))
                        pe.wait_ge(*VG.at(l, n, d, "vb"))
                        if need_o[d]:
                            four(B[1], lambda h: qkv[:, h, cs], lambda h: qkv[:, 4 + h, cs])\
                                .then_inc(*TG.did((l, n, d, "A")))
                    for d in range(2):
                        B = [ps[:, 4 * d + i, :] for i in range(4)]
                        g = G[d]
                        pe.wait_ge(*VG.at(l, n, d, "L"))
                        for h in range(HEADS):
                            mm = pe.transpose(B[3][:, P * h:P * h + P], g["L"][:, h, :], ident)
                        mm.then_inc(*TG.did((l, n, d, "LT")))
                        if need_o[d]:
                            pe.wait_ge(*VG.at(l, n, d, "qg"))
                            for h in range(HEADS):
                                mm = pe.transpose(B[2][:, P * h:P * h + P], g["qg"][:, h, :], ident)
                            mm.then_inc(*TG.did((l, n, d, "qgT")))
                            pe.wait_ge(*VG.at(l, n, d, "attn"))
                            for h in range(HEADS):
                                mm = pe.transpose(B[0][:, P * h:P * h + P], g["attn"][:, h, :], ident)
                            mm.then_inc(*TG.did((l, n, d, "attnT")))
                    for i in range(1, NLEV):
                        for d in range(2):
                            B = [ps[:, 4 * d + k, :] for k in range(4)]
                            g = G[d]
                            pe.wait_ge(*GG.at(l, n, d, "NT", i))
                            if i > 1:
                                pe.wait_ge(*VG.at(l, n, d, "X", i - 1))
                            four(B[1], lambda h: g["NT"][i % 2][:, h, :], lambda h: g["X"][:, h, :])\
                                .then_inc(*TG.did((l, n, d, "P", i)))
                        for d in range(2):
                            B = [ps[:, 4 * d + k, :] for k in range(4)]
                            g = G[d]
                            pe.wait_ge(*AG.at(l, n, d, "P", i))
                            if i == 1:
                                pe.wait_ge(*AG.at(l, n, d, "LT"))
                                if need_o[d]:
                                    pe.wait_ge(*AG.at(l, n, d, "qgT"))
                            if i > 1:
                                pe.wait_ge(*VG.at(l, n, d, "Y", i - 1))
                            if i < NLEV - 1:
                                four(B[2], lambda h: g["Y"][:, h, :], lambda h: g["P"][:, h, :])\
                                    .then_inc(*TG.did((l, n, d, "XP", i)))
                            four(B[3], lambda h: g["P"][:, h, :], lambda h: g["Y"][:, h, :])\
                                .then_inc(*TG.did((l, n, d, "YP", i)))
                    for d in range(2):
                        B = [ps[:, 4 * d + k, :] for k in range(4)]
                        g = G[d]
                        pe.wait_ge(*VG.at(l, n, d, "Y", NLEV - 1))
                        if n > 0:
                            if need_o[d]:
                                pe.wait_ge(*AG.at(l, n, d, "attnT"))
                            four(B[0], lambda h: g["kbg"][:, h, :], lambda h: g["Y"][:, h, :])\
                                .then_inc(*TG.did((l, n, d, "wT")))
                    for d in range(2):
                        B = [ps[:, 4 * d + k, :] for k in range(4)]
                        g = G[d]
                        if n > 0:
                            pe.wait_ge(*AG.at(l, n, d, "nwT"))
                        for h in range(HEADS):
                            o = B[1][:, P * h:P * h + P]
                            mm = pe.matmul(o, g["Y"][:, h, :], g["vb"][:, h, :], start=True, stop=(n == 0))
                            if n > 0:
                                mm = pe.matmul(o, g["nwT"][:, h, :], g["S"][:, h, :], start=False, stop=True)
                        mm.then_inc(*TG.did((l, n, d, "vn")))
                    for d in range(2):
                        B = [ps[:, 4 * d + k, :] for k in range(4)]
                        g = G[d]
                        pe.wait_ge(*AG.at(l, n, d, "vn"))
                        if need_o[d]:
                            for h in range(HEADS):
                                o = B[2][:, P * h:P * h + P]
                                if n > 0:
                                    pe.matmul(o, g["S"][:, h, :], g["qgT"][:, h, :], start=True, stop=False)
                                else:
                                    pe.wait_ge(*AG.at(l, n, d, "attnT"))
                                mm = pe.matmul(o, g["vn"][:, h, :], g["attnT"][:, h, :], start=(n == 0), stop=True)
                            mm.then_inc(*TG.did((l, n, d, "o")))
                        four(B[3], lambda h: g["kg"][:, h, :], lambda h: g["vn"][:, h, :])\
                            .then_inc(*TG.did((l, n, d, "upd")))

            def gdn_out(l):
                osq = wk(W_G, 2, 512)
                for u, (h, s) in enumerate(out_units(l)):
                    w = SEG[s][1]
                    if u >= 2:
                        pe.wait_ge(*AG.at(l, "oln", u - 2))
                    pe.wait_ge(*AG.at(l, "osq", u))
                    pe.matmul(ps[:, u % 2, 0:w], ones, osq[:, u % 2, 0:w], start=True, stop=True)\
                        .then_inc(*TG.did((l, "onrm", u)))

            for stage, l in ORDER:
                if before((stage, l)):
                    fence(pe, before((stage, l)))
                if stage == "mod":
                    mod(l)
                elif stage == "norm1":
                    norm("norm1", l, ["lat", "ctx"])
                elif stage.startswith("filter_"):
                    filters(l, stage[7:])
                elif stage == "hy_proj":
                    hy_proj(l)
                elif stage.startswith("conv_"):
                    long_conv(l, stage[5:])
                elif stage == "ret_proj":
                    ret_proj(l)
                elif stage == "ret":
                    retention(l)
                elif stage == "gdn_proj":
                    gdn_proj(l)
                elif stage == "gdn_prep":
                    gdn_prep(l)
                elif stage == "gdn":
                    gdn(l)
                elif stage == "gdn_out":
                    gdn_out(l)
                elif stage == "out":
                    out_proj(l)
                elif stage == "norm2":
                    norm("norm2", l, segs(l))
                elif stage == "ffn_in":
                    ffn_in(l)
                elif stage == "ffn_out":
                    ffn_out(l)
                elif stage == "final":
                    norm("final", l, ["lat"])
                close("tensor", (stage, l))

        @block.scalar
        def _(act):
            T, V, A, G = (S[e, "proj"] for e in engines)
            TH, VH, AH, GH = (S[e, "hyena"] for e in engines)
            TR, VR, AR, GR = (S[e, "ret"] for e in engines)
            TG, VG, AG, GG = (S[e, "gdn"] for e in engines)

            def rsqrt(out_, in_, scale, steps, key, bias=None):
                act.activation(out_, in_, ACT.Ln, bias=eps, scale=scale).then_inc(*steps.did(key + ("ln",)))
                act.wait_ge(*steps.at(*key, "ln"))
                kw = {} if bias is None else {"bias": bias}
                act.activation(out_, out_, ACT.Exp, scale=-0.5, **kw).then_inc(*steps.did(key + ("rs",)))

            def norm(name, l, sgs):
                for s in sgs:
                    t0, w = SEG[s]
                    for k in range(DC):
                        act.activation(hT[:, k, t0:t0 + w], xT[:, k, t0:t0 + w], ACT.Square)\
                            .then_inc(*A.did((name, l, s, "sq", k)))
                for s in sgs:
                    t0, w = SEG[s]
                    act.wait_ge(*T.at(name, l, s))
                    rsqrt(rstd[:, t0:t0 + w], ps[:, 0 if s == "lat" else 1, 0:w], 1.0 / D, A, (name, l, s))
                if name == "final":
                    return
                which = 0 if name == "norm1" else 1
                for s in sgs:
                    t0, w = SEG[s]
                    e = 0 if s == "lat" else 1
                    for k in range(DC):
                        act.wait_ge(*V.at(name, l, s, k))
                        act.activation(hT[:, k, t0:t0 + w], hT[:, k, t0:t0 + w], ACT.Identity,
                                       bias=modv[:, 24 * which + k, e:e + 1]).then_inc(*A.did())

            def raw_copy(name, l, item, s, at):
                w = SEG[s][1]
                raw = wk(at, 3, 772)
                o = 1 if s == "ctx" else 259
                if item >= 3:
                    act.wait_ge(*V.at(name, l, item - 3, "conv"))
                act.wait_ge(*T.at(name, l, item, s))
                act.activation(raw[:, item % 3, o:o + w], ps[:, item % 3 + (0 if s == "lat" else 3), 0:w], ACT.Copy)\
                    .then_inc(*A.did((name, l, item, s)))

            def hy_proj(l):
                act.wait_ge(*G.at("halo", l, "hy"))
                for i in range(6):
                    for s in segs(l):
                        raw_copy("hy", l, i, s, W_RAW)

            def ret_proj(l):
                rqk = wk(W_RQK, 4, TOK)
                for i in range(6):
                    for s in segs(l, both=(i in (2, 3))):
                        t0, w = SEG[s]
                        act.wait_ge(*T.at("ret", l, i, s))
                        dst = rqk[:, i, t0:t0 + w] if i < 4 else mix[:, 6 + i - 4, t0:t0 + w]
                        act.activation(dst, ps[:, i % 3 + (0 if s == "lat" else 3), 0:w],
                                       ACT.Copy if i < 4 else ACT.Silu).then_inc(*A.did(("ret", l, i, s)))

            def gdn_proj(l):
                qkv = wk(W_QKV, 12, TOK)
                act.wait_ge(*G.at("halo", l, "gd"))

                def silu(i):
                    act.wait_ge(*V.at("gd", l, i, "conv"))
                    ss = segs(l, both=(i >= 4))
                    lo = min(SEG[s][0] for s in ss)
                    act.activation(qkv[:, i, lo:TOK], qkv[:, i, lo:TOK], ACT.Silu).then_inc(*A.did(("gds", l, i)))
                for i in range(12):
                    for s in segs(l, both=(i >= 4)):
                        raw_copy("gd", l, i, s, W_GRAW)
                    if i >= 1:
                        silu(i - 1)
                for i in range(12, 16):
                    for s in segs(l):
                        t0, w = SEG[s]
                        act.wait_ge(*T.at("gd", l, i, s))
                        act.activation(mix[:, 2 + i - 12, t0:t0 + w], ps[:, i % 3 + (0 if s == "lat" else 3), 0:w],
                                       ACT.Silu).then_inc(*A.did(("gd", l, i, s)))
                    if i == 12:
                        silu(11)

            def ffn_in(l):
                hid = wk(0, FC, TOK)
                for i in range(FC):
                    for s in segs(l):
                        t0, w = SEG[s]
                        act.wait_ge(*T.at("fi", l, 2 * i, s))
                        act.activation(hid[:, i, t0:t0 + w], ps[:, (2 * i) % 3 + (0 if s == "lat" else 3), 0:w],
                                       ACT.Silu).then_inc(*A.did(("fi", l, i, s)))

            def filters(l, s):
                L = SEG[s][1]
                nt = L // P
                o = (0 if s == "lat" else 1536) + NFP + L
                hb, arg = mixf[0:64, o:o + L], mixf[0:64, o + L:o + 2 * L]
                for i in range(2):
                    act.wait_ge(*VH.at(l, s, "arg", i))
                    act.activation(hb, arg, ACT.Sin).then_inc(*AH.did((l, s, "sin", i)))
                K = spectrum()
                for j in range(nt):
                    kj = K[:, j, :].rearrange("p (n c) -> p n c", n=2)
                    for i in range(2):
                        act.wait_ge(*TH.at(l, s, "K", i, j))
                        src = ps[:, 6 + i, :].rearrange("p (n c) -> p n c", n=2)
                        if i == 0:
                            act.activation(kj[:, :, 0:256], src, ACT.Copy).then_inc(*AH.did())
                            act.activation(kj[:, :, 512:768], src, ACT.Copy).then_inc(*AH.did((l, s, "K", i, j)))
                        else:
                            act.activation(kj[:, :, 256:512], src, ACT.Copy).then_inc(*AH.did((l, s, "K", i, j)))

            def long_conv(l, s):
                nt = SEG[s][1] // P
                tok = wk(W_TOK, 4, 512)
                for t in range(nt):
                    act.wait_ge(*TH.at(l, s, "tok", t))
                    act.activation(tok[:, t, :], ps[:, t % 2, :], ACT.Copy).then_inc(*AH.did((l, s, "tok", t)))

            def retention(l):
                rc = work[:, W_RC:W_RC + 3968]
                act.wait_ge(tables_in, tables_count("ret", l))
                act.wait_ge(*VR.at(l, "negabs"))
                act.activation(lam[:, 1, :], lam[:, 0, :], ACT.Exp).then_inc(*AR.did((l, "e")))
                act.wait_ge(*VR.at(l, "u"))
                act.activation(lam[:, 0, :], lam[:, 2, :], ACT.Ln).then_inc(*AR.did((l, "lnu")))
                for h in range(HEADS):
                    dt, tmp = decay_of(h)
                    act.wait_ge(*VR.at(l, "darg", h))
                    act.activation(dt[:, 0:896], dt[:, 0:896], ACT.Exp).then_inc(*AR.did((l, "D", h)))
                    if h >= 1:
                        act.wait_ge(*GR.at(l, "D2", h - 1))
                    act.activation(dt[:, 896:1536], rc[:, RC_CF:RC_CF + 640], ACT.Exp, scale=lam[:, 3, h:h + 1])\
                        .then_inc(*AR.did())
                    act.activation(tmp[:, 896:1536], rc[:, RC_CB:RC_CB + 640], ACT.Exp, scale=lam[:, 3, 4 + h:5 + h])\
                        .then_inc(*AR.did((l, "D2", h)))
                for s in segs(l):
                    w = SEG[s][1]
                    for p in range(2):
                        oc, cc, sq, rs = ret_out(s, p)
                        us = [ret_unit(l, s, h, (5 if s == "lat" else 1)) for h in (2 * p, 2 * p + 1)]
                        act.wait_ge(*TR.at(l, "PV", us[1]))
                        if (s, p) != ("lat", 0):
                            act.wait_ge(*VR.at(l, "yprev", s, p))
                        act.activation(oc, ps[:, (6 if s == "lat" else 4) + p, 0:w], ACT.Copy)\
                            .then_inc(*AR.did((l, s, p, "oc")))
                        act.wait_ge(*VR.at(l, s, p, "cc"))
                        act.activation(sq, cc, ACT.Square).then_inc(*AR.did((l, s, p, "sq")))
                        act.wait_ge(*TR.at(l, s, p, "var"))
                        rsqrt(rs, ps[:, 2 + p, 0:w], 1.0, AR, (l, s, p))

            def gdn_prep(l):
                qkv = wk(W_QKV, 12, TOK)
                sq, rs = wk(W_G, 2, 512), wk(W_G + 1024, 2, 512)
                act.wait_ge(*VG.at(l, "negabs"))
                act.activation(gs[:, 2, :, :], gs[:, 2, :, :], ACT.Exp).then_inc(*AG.did((l, "e")))
                act.wait_ge(*VG.at(l, "u"))
                act.activation(gs[:, 4, :, :], gs[:, 3, :, :], ACT.Ln).then_inc(*AG.did((l, "lnu")))
                act.activation(gs[:, 9, 0, :], par[:, ALOG:ALOG + 8], ACT.Exp).then_inc(*AG.did((l, "ea")))
                act.activation(gs[:, 5, :, :], ps[:, 6, 0:96].rearrange("p (c x) -> p c x", x=16)[:, :, 8:16],
                               ACT.Exp, scale=-1.0).then_inc(*AG.did((l, "eb")))
                act.wait_ge(*TG.at(l, "gc"))
                gc = ps[:, 7, 0:144].rearrange("p (d i c h) -> p d i c h", d=2, i=3, c=CHUNKS)
                act.wait_ge(*VG.at(l, "g"))
                for d in range(2):
                    for i, k in ((0, 6), (1, 8), (2, 9)):
                        ins = act.activation(gs[:, k, :, 4 * d:4 * d + 4], gc[:, d, i, :, :], ACT.Exp)
                        ins.then_inc(*AG.did((l, "gexp", d, i)))
                units = list(norm_units(l))

                def square(u):
                    c, s = units[u]
                    t0, w = SEG[s]
                    if u >= 2:
                        act.wait_ge(*TG.at(l, "nrm", u - 2))
                    act.activation(sq[:, u % 2, 0:w], qkv[:, c, t0:t0 + w], ACT.Square)\
                        .then_inc(*AG.did((l, "nsq", u)))
                square(0)
                for u, (c, s) in enumerate(units):
                    w = SEG[s][1]
                    if u + 1 < len(units):
                        square(u + 1)
                    act.wait_ge(*TG.at(l, "nrm", u))
                    if u >= 2:
                        act.wait_ge(*VG.at(l, "nmul", u - 2))
                    act.activation(rs[:, u % 2, 0:w], ps[:, u % 2, 0:w], ACT.Ln, bias=eps)\
                        .then_inc(*AG.did((l, "ln", u)))
                    act.wait_ge(*AG.at(l, "ln", u))
                    kw = {"bias": lnq} if c < 4 else {}
                    act.activation(rs[:, u % 2, 0:w], rs[:, u % 2, 0:w], ACT.Exp, scale=-0.5, **kw)\
                        .then_inc(*AG.did((l, "nrs", u)))

            def flat(v):
                return v.rearrange("p h c -> p (h c)")

            def gdn(l):
                for n in range(CHUNKS):
                    G_ = [group(d) for d in range(2)]
                    need_o = l == 0 or n >= 2
                    for d in range(2):
                        act.wait_ge(*TG.at(l, n, d, "dec"))
                        if n > 0:
                            act.wait_ge(*TG.at(l, n - 1, d, "vn"))
                        act.activation(flat(G_[d]["decm"]), ps[:, 4 * d + 3, :], ACT.Exp)\
                            .then_inc(*AG.did((l, n, d, "dec")))
                    for d in range(2):
                        act.wait_ge(*TG.at(l, n, d, "LT"))
                        act.activation(flat(G_[d]["LT"]), ps[:, 4 * d + 3, :], ACT.Copy)\
                            .then_inc(*AG.did((l, n, d, "LT")))
                        if need_o:
                            act.wait_ge(*TG.at(l, n, d, "qgT"))
                            act.activation(flat(G_[d]["qgT"]), ps[:, 4 * d + 2, :], ACT.Copy)\
                                .then_inc(*AG.did((l, n, d, "qgT")))
                            act.wait_ge(*TG.at(l, n, d, "attnT"))
                            act.activation(flat(G_[d]["attnT"]), ps[:, 4 * d, :], ACT.Copy)\
                                .then_inc(*AG.did((l, n, d, "attnT")))
                    for i in range(1, NLEV):
                        for d in range(2):
                            act.wait_ge(*TG.at(l, n, d, "P", i))
                            if i > 1:
                                act.wait_ge(*TG.at(l, n, d, "YP", i - 1))
                            act.activation(flat(G_[d]["P"]), ps[:, 4 * d + 1, :], ACT.Copy)\
                                .then_inc(*AG.did((l, n, d, "P", i)))
                    for d in range(2):
                        if n > 0:
                            act.wait_ge(*TG.at(l, n, d, "wT"))
                            act.activation(flat(G_[d]["nwT"]), ps[:, 4 * d, :], ACT.Copy, scale=-1.0)\
                                .then_inc(*AG.did((l, n, d, "nwT")))
                    for d in range(2):
                        act.wait_ge(*TG.at(l, n, d, "vn"))
                        act.activation(flat(G_[d]["vn"]), ps[:, 4 * d + 1, :], ACT.Copy)\
                            .then_inc(*AG.did((l, n, d, "vn")))

            def gdn_out(l):
                osq, rs = wk(W_G, 2, 512), wk(W_G + 1024, 2, 512)
                units = list(out_units(l))
                for u, (h, s) in enumerate(units):
                    t0, w = SEG[s]
                    if u >= 2:
                        act.wait_ge(*TG.at(l, "onrm", u - 2))
                    act.activation(osq[:, u % 2, 0:w], oacc[:, h, t0:t0 + w], ACT.Square)\
                        .then_inc(*AG.did((l, "osq", u)))
                    act.wait_ge(*TG.at(l, "onrm", u))
                    if u >= 2:
                        act.wait_ge(*VG.at(l, "omul", u - 2))
                    act.activation(rs[:, u % 2, 0:w], ps[:, u % 2, 0:w], ACT.Ln, bias=eps, scale=1.0 / P)\
                        .then_inc(*AG.did((l, "oln", u)))
                    act.wait_ge(*AG.at(l, "oln", u))
                    act.activation(rs[:, u % 2, 0:w], rs[:, u % 2, 0:w], ACT.Exp, scale=-0.5)\
                        .then_inc(*AG.did((l, "ors", u)))

            for stage, l in ORDER:
                if before((stage, l)):
                    fence(act, before((stage, l)))
                if stage == "mod":
                    if l == 0:
                        act.wait_ge(start_in, 64)
                        act.activation(condT[:, :, :], condT[:, :, :], ACT.Silu).then_inc(*A.did("silu_c"))
                elif stage == "norm1":
                    norm("norm1", l, ["lat", "ctx"])
                elif stage.startswith("filter_"):
                    filters(l, stage[7:])
                elif stage == "hy_proj":
                    hy_proj(l)
                elif stage.startswith("conv_"):
                    long_conv(l, stage[5:])
                elif stage == "ret_proj":
                    ret_proj(l)
                elif stage == "ret":
                    retention(l)
                elif stage == "gdn_proj":
                    gdn_proj(l)
                elif stage == "gdn_prep":
                    gdn_prep(l)
                elif stage == "gdn":
                    gdn(l)
                elif stage == "gdn_out":
                    gdn_out(l)
                elif stage == "norm2":
                    norm("norm2", l, segs(l))
                elif stage == "ffn_in":
                    ffn_in(l)
                elif stage == "final":
                    norm("final", l, ["lat"])
                close("scalar", (stage, l))

        @block.vector
        def _(dve):
            T, V, A, G = (S[e, "proj"] for e in engines)
            TH, VH, AH, GH = (S[e, "hyena"] for e in engines)
            TR, VR, AR, GR = (S[e, "ret"] for e in engines)
            TG, VG, AG, GG = (S[e, "gdn"] for e in engines)

            def step(ins, steps, key=None):
                ins.then_inc(*steps.did(key))
                dve.wait_ge(steps.sem, steps.n)

            def mod(l):
                dve.wait_ge(params_in, 32 * (l + 1))
                dve.wait_ge(*T.at("block", block_no(l, "mod", N_MODB - 1)))
                step(dve.tensor_tensor(modv[:, :, :], ps[:, 7, 0:96].rearrange("p (c e) -> p c e", e=2),
                                       par[:, MODB:MODB + 48].unsqueeze(2).broadcast_to([P, 48, 2]), ALU.add), V)
                for i, (sc, g) in enumerate(((8, N1G), (32, N2G))):
                    step(dve.scalar_tensor_tensor(amp[:, i, :, :], modv[:, sc:sc + 8, :], 1.0,
                                                  par[:, g:g + 8].unsqueeze(2).broadcast_to([P, 8, 2]),
                                                  ALU.add, ALU.mult), V)

            def norm(name, l, sgs):
                for s in sgs:
                    t0, w = SEG[s]
                    e = 0 if s == "lat" else 1
                    dve.wait_ge(*A.at(name, l, s, "rs"))
                    for k in range(DC):
                        a = par[:, FNG + k:FNG + k + 1] if name == "final" else \
                            amp[:, 0 if name == "norm1" else 1, k, e:e + 1]
                        dve.scalar_tensor_tensor(hT[:, k, t0:t0 + w], xT[:, k, t0:t0 + w], a, rstd[:, t0:t0 + w],
                                                 ALU.mult, ALU.mult)\
                            .then_inc(*V.did(("final", k) if name == "final" else (name, l, s, k)))

            def conv(name, l, item, at, ss, dst, wcol, bias):
                raw = wk(at, 3, 772)[:, item % 3, :]
                n_w = 6 if name == "hy" else 12
                w = [par[:, wcol + n_w * j + item:wcol + n_w * j + item + 1] for j in range(3)]
                for s in ss:
                    dve.wait_ge(*A.at(name, l, item, s))
                    t0, wd = SEG[s]
                    o = 0 if s == "ctx" else 258
                    d_ = dst[:, t0:t0 + wd]
                    if bias is None:
                        step(dve.tensor_scalar(d_, raw[:, o:o + wd], w[0], None, ALU.mult), V)
                    else:
                        step(dve.tensor_scalar(d_, raw[:, o:o + wd], w[0], bias, ALU.mult, ALU.add), V)
                    step(dve.scalar_tensor_tensor(d_, raw[:, o + 1:o + 1 + wd], w[1], d_, ALU.mult, ALU.add), V)
                    step(dve.scalar_tensor_tensor(d_, raw[:, o + 2:o + 2 + wd], w[2], d_, ALU.mult, ALU.add), V,
                         (name, l, item, "conv") if s == ss[-1] else None)

            def hy_proj(l):
                cv = wk(W_CONV, 4, TOK)
                for i in range(6):
                    dst = cv[:, i, :] if i < 4 else mix[:, i - 4, :]
                    conv("hy", l, i, W_RAW, segs(l), dst, HCW, par[:, HCB + i:HCB + i + 1])

            def ret_proj(l):
                rv = wk(W_RV, CHUNKS, 256)
                for c in range(CHUNKS):
                    dve.wait_ge(*T.at("rv", l, c))
                    dve.tensor_copy(rv[:, c, :], ps[:, 6 + c % 2, 0:256]).then_inc(*V.did(("rv", l, c)))

            def gdn_proj(l):
                qkv = wk(W_QKV, 12, TOK)
                for i in range(12):
                    conv("gd", l, i, W_GRAW, segs(l, both=(i >= 4)), qkv[:, i, :], GCW, None)

            def residual(name, l, item, s, gate, bank):
                t0, w = SEG[s]
                e = 0 if s == "lat" else 1
                x = xT[:, item, t0:t0 + w]
                dve.scalar_tensor_tensor(x, ps[:, bank, 0:w], modv[:, gate + item, e:e + 1], x,
                                         ALU.mult, ALU.add).then_inc(*V.did((name, l, item, s)))

            def out_proj(l):
                for i in range(DC):
                    for s in segs(l):
                        dve.wait_ge(*T.at("out", l, i, s))
                        residual("out", l, i, s, 16, i % 3 + (0 if s == "lat" else 3))

            def ffn_in(l):
                hid = wk(0, FC, TOK)
                for i in range(FC):
                    for s in segs(l):
                        t0, w = SEG[s]
                        dve.wait_ge(*T.at("fi", l, 2 * i + 1, s))
                        dve.wait_ge(*A.at("fi", l, i, s))
                        h = hid[:, i, t0:t0 + w]
                        dve.tensor_tensor(h, ps[:, (2 * i + 1) % 3 + (0 if s == "lat" else 3), 0:w], h, ALU.mult)\
                            .then_inc(*V.did(("fi", l, 2 * i + 1, s)))

            def ffn_out(l):
                for i in range(DC):
                    for s in segs(l):
                        dve.wait_ge(*T.at("fo", l, i, 1, s))
                        residual("fo", l, i, s, 40, i % 3 + (0 if s == "lat" else 3))

            def filters(l, s):
                L = SEG[s][1]
                nt = L // P
                o = 0 if s == "lat" else 1536
                fp = mixf[0:64, o:o + NFP]
                o += NFP
                arg, rnd = mixf[0:64, o + 2 * L:o + 3 * L], mixf[0:64, o + 3 * L:o + 4 * L]
                win = mixf[:, o + 4 * L:o + 4 * L + 256 * (nt + 1)].rearrange("p (t c) -> p t c", c=256)
                for i in range(2):
                    dve.wait_ge(*TH.at(l, s, "h1" if i == 0 else "h2"))
                    b_, f_ = fp[:, FVEC + 2 * i:FVEC + 2 * i + 1], fp[:, FVEC + 2 * i + 1:FVEC + 2 * i + 2]
                    if i == 0:
                        dve.wait_ge(tables_in, tables_count("filter_" + s, l))
                    step(dve.tensor_scalar(arg, ps[0:64, i, 0:L], b_, f_, ALU.add, ALU.mult), VH)
                    step(dve.tensor_scalar(rnd, arg, 1.0 / (2 * math.pi), MAGIC, ALU.mult, ALU.add), VH)
                    step(dve.tensor_scalar(rnd, rnd, -MAGIC, None, ALU.add), VH)
                    step(dve.scalar_tensor_tensor(arg, rnd, -TWO_PI_HI, arg, ALU.mult, ALU.add), VH)
                    step(dve.scalar_tensor_tensor(arg, rnd, -TWO_PI_LO, arg, ALU.mult, ALU.add), VH)
                    step(dve.tensor_scalar(arg, arg, PI_IN, -PI_IN, ALU.min, ALU.max), VH, (l, s, "arg", i))
                hp, hn = halves(s)
                for t in range(nt):
                    dve.wait_ge(*TH.at(l, s, "h3", t))
                    if t >= 2:
                        dve.wait_ge(*GH.at(l, s, "diff", t - 2))
                    b = ps[:, 2 + 2 * (t % 2):4 + 2 * (t % 2), :]
                    wp = win[:, t, :].unsqueeze(1).broadcast_to([P, 2, 256])
                    wn = (win[:, nt, :] if t == 0 else win[:, t, :]).unsqueeze(1).broadcast_to([P, 2, 256])
                    dve.tensor_tensor(hp[:, t % 2, :].rearrange("p (n c) -> p n c", n=2), b[:, :, 0:256], wp, ALU.mult)\
                        .then_inc(*VH.did((l, s, "hp", t)))
                    dve.tensor_tensor(hn[:, t % 2, :].rearrange("p (n c) -> p n c", n=2), b[:, :, 256:512], wn, ALU.mult)\
                        .then_inc(*VH.did((l, s, "hn", t)))
                sd = sum_diff(s)
                dve.wait_ge(*GH.at(l, s, "diff", nt - 1))
                for i in range(2):
                    ins = dve.tensor_tensor(sd[0:1, i, 0, :], sd[0:1, i, 0, :], fp[0:1, FBIAS:FBIAS + 512], ALU.add)
                    ins.then_inc(*VH.did((l, s, "bias") if i == 1 else None))

            def long_conv(l, s):
                t0, L = SEG[s]
                nt = L // P
                K = spectrum()
                tok = wk(W_TOK, 4, 512)
                prod = products()
                for n in range(2):
                    for j in range(nt):
                        dve.wait_ge(*TH.at(l, s, n, "U", j))
                        if j >= 2 or n > 0:
                            dve.wait_ge(*GH.at(l, s, n, "Y", j - 2) if j >= 2 else GH.at(l, s, 0, "Y", nt - 2 + j))
                        b = ps[:, 2 + j % 2, :]
                        k = K[:, j, 768 * n:768 * n + 768]
                        dve.tensor_tensor(prod[:, 2 * (j % 2), :], b, k[:, 0:512], ALU.mult).then_inc(*VH.did())
                        dve.tensor_tensor(prod[:, 2 * (j % 2) + 1, :], b, k[:, 256:768], ALU.mult)\
                            .then_inc(*VH.did((l, s, n, "p2", j)))
                    if n == 0:
                        for t in range(nt):
                            dve.wait_ge(*TH.at(l, s, "y1", t))
                            dve.tensor_tensor(tok[:, t, 0:256], ps[:, 4 + t % 2, 0:256], tok[:, t, 256:512], ALU.mult)\
                                .then_inc(*VH.did((l, s, "z1", t)))
                    else:
                        for c in range(2):
                            dve.wait_ge(*TH.at(l, s, "y2", c))
                            x2 = mix[:, c, t0:t0 + L]
                            dve.tensor_tensor(x2, ps[:, 6 + c, 0:L], x2, ALU.mult).then_inc(*VH.did())

            def retention(l):
                rc = work[:, W_RC:W_RC + 3968]
                rope = wk(W_ROPE, 2, 512)
                rqk = wk(W_RQK, 4, TOK)
                x = par[:, RLOG:RLOG + 8]
                step(dve.scalar_tensor_tensor(lam[:, 0, :], x, -1.0, x, ALU.mult, ALU.min), VR, (l, "negabs"))
                dve.wait_ge(*AR.at(l, "e"))
                step(dve.tensor_scalar(lam[:, 2, :], lam[:, 1, :], 1.0, None, ALU.add), VR, (l, "u"))
                step(dve.reciprocal(lam[:, 3, :], lam[:, 2, :]), VR)
                dve.wait_ge(*AR.at(l, "lnu"))
                step(dve.scalar_tensor_tensor(lam[:, 2, :], lam[:, 2, :], -1.0, lam[:, 1, :], ALU.add, ALU.subtract), VR)
                step(dve.tensor_tensor(lam[:, 2, :], lam[:, 2, :], lam[:, 3, :], ALU.mult), VR)
                step(dve.tensor_tensor(lam[:, 2, :], lam[:, 2, :], lam[:, 0, :], ALU.subtract), VR)
                step(dve.scalar_tensor_tensor(lam[:, 3, :], x, 0.0, lam[:, 2, :], ALU.min, ALU.add), VR, (l, "lam"))
                dve.wait_ge(tables_in, tables_count("ret", l))

                def darg(h):
                    dt, tmp = decay_of(h)
                    if h >= 2:
                        dve.wait_ge(*VR.at(l, "P", 6 * (h - 2) + 5))
                        if l == 0:
                            dve.wait_ge(*GR.at(l, "CD", h - 2))
                    step(dve.tensor_scalar(tmp[:, 0:896], rc[:, RC_NEG:RC_NEG + 896], lam[:, 3, 4 + h:5 + h], None,
                                           ALU.mult), VR)
                    step(dve.scalar_tensor_tensor(dt[:, 0:896], rc[:, RC_POS:RC_POS + 896], lam[:, 3, h:h + 1],
                                                  tmp[:, 0:896], ALU.mult, ALU.add), VR, (l, "darg", h))
                darg(0)
                for c in range(4):
                    q = rqk[:, c, CTX:TOK]
                    tmp = wk(W_P, 6, 512)[:, c, :]
                    dve.wait_ge(*TR.at(l, "perm", c))
                    step(dve.tensor_tensor(tmp, ps[:, c, :], rope[:, 1, :], ALU.mult), VR)
                    step(dve.tensor_tensor(q, q, rope[:, 0, :], ALU.mult), VR)
                    step(dve.tensor_tensor(q, q, tmp, ALU.add), VR, (l, "rope", c))
                work_list = list(ret_work(l))
                for s, h, chunks in work_list:
                    w = SEG[s][1]
                    if s == "lat":
                        if h + 1 < HEADS:
                            darg(h + 1)
                        dt = decay_of(h)[0]
                        dve.wait_ge(*GR.at(l, "D1", h))
                        dve.wait_ge(*GR.at(l, "D2", h))
                    else:
                        dve.wait_ge(*GR.at(l, "CD", h))
                    for i, c in enumerate(chunks):
                        u = ret_unit(l, s, h, i)
                        if s == "lat":
                            o = 896 + 128 - P * c if c < 2 else 384 - P * (c - 2)
                        else:
                            o = 384 - P * c
                        dve.wait_ge(*TR.at(l, "S", u))
                        if u >= 6:
                            dve.wait_ge(*TR.at(l, "PV", u - 6))
                        src = dt if s == "lat" else ctx_decay(h)
                        dve.scalar_tensor_tensor(wk(W_P, 6, 512)[:, u % 6, 0:w], ps[:, u % 4, 0:w], 0.125,
                                                 src[:, o:o + w], ALU.mult, ALU.mult)\
                            .then_inc(*VR.did((l, "P", u)))
                for s in segs(l):
                    t0, w = SEG[s]
                    for p in range(2):
                        oc, cc, sq, rs = ret_out(s, p)
                        dve.wait_ge(*TR.at(l, s, p, "mu"))
                        step(dve.tensor_tensor(cc, oc, ps[:, p, 0:w], ALU.subtract), VR, (l, s, p, "cc"))
                        dve.wait_ge(*AR.at(l, s, p, "rs"))
                        step(dve.tensor_tensor(cc, cc, rs, ALU.mult), VR)
                        gate = mix[:, 6 + p, t0:t0 + w]
                        nxt = {("lat", 0): ("lat", 1), ("lat", 1): ("ctx", 0), ("ctx", 0): ("ctx", 1),
                               ("ctx", 1): ("end", 0)}[s, p]
                        step(dve.tensor_tensor(gate, cc, gate, ALU.mult), VR, (l, "yprev") + nxt)

            def gdn_prep(l):
                ab = ps[:, 6, 0:96].rearrange("p (c x) -> p c x", x=16)
                dve.wait_ge(*T.at("ab", l))

                def rows(v):
                    return v.unsqueeze(1).broadcast_to([P, CHUNKS, 8])
                g_, t_, e_, u_, r_, beta = (gs[:, i, :, :] for i in range(6))
                step(dve.tensor_tensor(t_, ab[:, :, 0:8], rows(par[:, DTB:DTB + 8]), ALU.add), VG)
                step(dve.scalar_tensor_tensor(e_, t_, -1.0, t_, ALU.mult, ALU.min), VG, (l, "negabs"))
                dve.wait_ge(*AG.at(l, "e"))
                step(dve.tensor_scalar(u_, e_, 1.0, None, ALU.add), VG, (l, "u"))
                step(dve.scalar_tensor_tensor(e_, u_, -1.0, e_, ALU.add, ALU.subtract), VG)
                dve.wait_ge(*AG.at(l, "lnu"))
                step(dve.reciprocal(u_, u_), VG)
                step(dve.tensor_tensor(e_, e_, u_, ALU.mult), VG)
                step(dve.tensor_tensor(r_, r_, e_, ALU.subtract), VG)
                step(dve.scalar_tensor_tensor(r_, t_, 0.0, r_, ALU.max, ALU.add), VG)
                dve.wait_ge(*AG.at(l, "ea"))
                step(dve.scalar_tensor_tensor(g_, r_, -1.0, rows(gs[:, 9, 0, :]), ALU.mult, ALU.mult), VG, (l, "g"))
                dve.wait_ge(*AG.at(l, "eb"))
                step(dve.tensor_scalar(beta, beta, 1.0, None, ALU.add), VG)
                step(dve.reciprocal(beta, beta), VG)
                dve.wait_ge(*AG.at(l, "gexp", 1, 2))
                step(dve.tensor_tensor(gs[:, 7, :, :], beta, gs[:, 6, :, :], ALU.mult), VG)
                qkv = wk(W_QKV, 12, TOK)
                rs = wk(W_G + 1024, 2, 512)
                for u, (c, s) in enumerate(norm_units(l)):
                    t0, w = SEG[s]
                    dve.wait_ge(*AG.at(l, "nrs", u))
                    dve.tensor_tensor(qkv[:, c, t0:t0 + w], qkv[:, c, t0:t0 + w], rs[:, u % 2, 0:w], ALU.mult)\
                        .then_inc(*VG.did((l, "nmul", u)))

            def gdn(l):
                for n in range(CHUNKS):
                    GR_ = [group(d) for d in range(2)]
                    need_o = l == 0 or n >= 2

                    def bank(d, i):
                        return ps[:, 4 * d + i, :].rearrange("p (h c) -> p h c", c=P)

                    def scal(k, c, d):
                        return per_head(gs[:, k, c, 4 * d:4 * d + 4])
                    for d in range(2):
                        g, c = GR_[d], chunk_of(n, d)
                        dve.wait_ge(*TG.at(l, n, d, "tok", 0))
                        if n > 0:
                            dve.wait_ge(*TG.at(l, n - 1, d, "upd"))
                        dve.tensor_tensor(g["kbg"], bank(d, 0), scal(7, c, d), ALU.mult).then_inc(*VG.did())
                        dve.tensor_tensor(g["kg"], bank(d, 0), scal(8, c, d), ALU.mult).then_inc(*VG.did((l, n, d, "kg")))
                        dve.wait_ge(*TG.at(l, n, d, "tok", 1))
                        dve.tensor_tensor(g["vb"], bank(d, 1), scal(5, c, d), ALU.mult).then_inc(*VG.did((l, n, d, "vb")))
                        if need_o:
                            dve.wait_ge(*TG.at(l, n, d, "tok", 2))
                            dve.tensor_tensor(g["qg"], bank(d, 2), scal(6, c, d), ALU.mult)\
                                .then_inc(*VG.did((l, n, d, "qg")))
                    for d in range(2):
                        g = GR_[d]
                        dve.wait_ge(*TG.at(l, n, d, "G"))
                        dve.wait_ge(*GG.at(l, n, d, "bdec"))
                        dve.tensor_tensor(g["L"], bank(d, 0), g["bdec"], ALU.mult).then_inc(*VG.did((l, n, d, "L")))
                        if need_o:
                            dve.wait_ge(*TG.at(l, n, d, "A"))
                            dve.tensor_tensor(g["attn"], bank(d, 1), g["decm"], ALU.mult)\
                                .then_inc(*VG.did((l, n, d, "attn")))
                    for i in range(1, NLEV):
                        for d in range(2):
                            g = GR_[d]
                            if i < NLEV - 1:
                                dve.wait_ge(*TG.at(l, n, d, "XP", i))
                                if i == 1:
                                    dve.wait_ge(*GG.at(l, n, d, "X0"))
                                dve.tensor_tensor(g["X"], g["X"], bank(d, 2), ALU.subtract)\
                                    .then_inc(*VG.did((l, n, d, "X", i)))
                            dve.wait_ge(*TG.at(l, n, d, "YP", i))
                            if i == 1:
                                dve.wait_ge(*GG.at(l, n, d, "Y0"))
                            dve.tensor_tensor(g["Y"], g["Y"], bank(d, 3), ALU.subtract)\
                                .then_inc(*VG.did((l, n, d, "Y", i)))
                    for d in range(2):
                        g, c = GR_[d], chunk_of(n, d)
                        dve.wait_ge(*TG.at(l, n, d, "upd"))
                        if n == 0:
                            dve.tensor_copy(g["S"], bank(d, 3)).then_inc(*VG.did((l, n, d, "S")))
                        else:
                            dve.wait_ge(*GG.at(l, n, d, "Sgl"))
                            dve.tensor_tensor(g["S"], g["Sgl"], bank(d, 3), ALU.add).then_inc(*VG.did((l, n, d, "S")))
                        if need_o:
                            o = oacc[:, :, P * c:P * c + P]
                            other = next(m for m in range(CHUNKS) if chunk_of(m, 1 - d) == c)
                            if n < other:
                                dve.tensor_copy(o, bank(d, 2)).then_inc(*VG.did((l, n, d, "o")))
                            else:
                                dve.wait_ge(*VG.at(l, other, 1 - d, "o"))
                                dve.tensor_tensor(o, o, bank(d, 2), ALU.add).then_inc(*VG.did((l, n, d, "o")))

            def gdn_out(l):
                rs = wk(W_G + 1024, 2, 512)
                for u, (h, s) in enumerate(out_units(l)):
                    t0, w = SEG[s]
                    dve.wait_ge(*AG.at(l, "ors", u))
                    o = oacc[:, h, t0:t0 + w]
                    step(dve.scalar_tensor_tensor(o, o, par[:, GNG:GNG + 1], rs[:, u % 2, 0:w], ALU.mult, ALU.mult),
                         VG, (l, "omul", u))
                    z = mix[:, 2 + h, t0:t0 + w]
                    step(dve.tensor_tensor(z, z, o, ALU.mult), VG)

            for stage, l in ORDER:
                if before((stage, l)):
                    fence(dve, before((stage, l)))
                if stage == "mod":
                    mod(l)
                elif stage == "norm1":
                    norm("norm1", l, ["lat", "ctx"])
                elif stage.startswith("filter_"):
                    filters(l, stage[7:])
                elif stage == "hy_proj":
                    hy_proj(l)
                elif stage.startswith("conv_"):
                    long_conv(l, stage[5:])
                elif stage == "ret_proj":
                    ret_proj(l)
                elif stage == "ret":
                    retention(l)
                elif stage == "gdn_proj":
                    gdn_proj(l)
                elif stage == "gdn_prep":
                    gdn_prep(l)
                elif stage == "gdn":
                    gdn(l)
                elif stage == "gdn_out":
                    gdn_out(l)
                elif stage == "out":
                    out_proj(l)
                elif stage == "norm2":
                    norm("norm2", l, segs(l))
                elif stage == "ffn_in":
                    ffn_in(l)
                elif stage == "ffn_out":
                    ffn_out(l)
                elif stage == "final":
                    norm("final", l, ["lat"])
                close("vector", (stage, l))

        @block.gpsimd
        def _(pool):
            T, V, A, G = (S[e, "proj"] for e in engines)
            TH, VH, AH, GH = (S[e, "hyena"] for e in engines)
            TR, VR, AR, GR = (S[e, "ret"] for e in engines)
            TG, VG, AG, GG = (S[e, "gdn"] for e in engines)

            def halo(l, name, at):
                raw = wk(at, 3, 772)
                for o, w in ((0, 1), (257, 2), (771, 1)):
                    ins = pool.memset(raw[:, :, o:o + w], 0.0)
                    ins.then_inc(*G.did(("halo", l, name) if o == 771 else None))

            def filters(l, s):
                L = SEG[s][1]
                nt = L // P
                o = 0 if s == "lat" else 1536
                n0 = 0 if s == "lat" else LAT
                pool.dma_start(mixf[0:64, o:o + NFP], filter_params[l, :, :]).then_inc(tables_in, 16)
                pool.dma_start(mixf[0:64, o + NFP:o + NFP + L], zpos[:, n0:n0 + L]).then_inc(tables_in, 16)
                o += NFP + 4 * L
                pool.dma_start(mixf[:, o:o + 256 * (nt + 1)], win_lat if s == "lat" else win_ctx).then_inc(tables_in, 16)
                pool.dma_start(work[:, W_TAB:W_TAB + 4 * nt * L], tab_lat if s == "lat" else tab_ctx)\
                    .then_inc(tables_in, 16)
                hp, hn = halves(s)
                sd = sum_diff(s)
                for t in range(nt):
                    pool.wait_ge(*VH.at(l, s, "hn", t))
                    pool.tensor_tensor(sd[:, 0, t, :], hp[:, t % 2, :], hn[:, t % 2, :], ALU.add).then_inc(*GH.did())
                    pool.tensor_tensor(sd[:, 1, t, :], hp[:, t % 2, :], hn[:, t % 2, :], ALU.subtract)\
                        .then_inc(*GH.did((l, s, "diff", t)))

            def long_conv(l, s):
                nt = SEG[s][1] // P
                prod = products()
                yf = wk(W_RAW, 4, 512)
                for n in range(2):
                    for j in range(nt):
                        pool.wait_ge(*VH.at(l, s, n, "p2", j))
                        if n == 1:
                            pool.wait_ge(*TH.at(l, s, "y1", nt - 1))
                        a, b = prod[:, 2 * (j % 2), :], prod[:, 2 * (j % 2) + 1, :]
                        pool.tensor_tensor(yf[:, j, 0:256], a[:, 0:256], a[:, 256:512], ALU.subtract).then_inc(*GH.did())
                        pool.tensor_tensor(yf[:, j, 256:512], b[:, 0:256], b[:, 256:512], ALU.add)\
                            .then_inc(*GH.did((l, s, n, "Y", j)))

            def retention(l):
                rc = work[:, W_RC:W_RC + 3968]
                pool.dma_start(rc, ret_tab).then_inc(tables_in, 16)
                pool.dma_start(wk(W_ROPE, 2, 512), rope_tab).then_inc(tables_in, 16)
                pool.wait_ge(tables_in, tables_count("ret", l))
                for h in range(HEADS):
                    dt, tmp = decay_of(h)
                    pool.wait_ge(*AR.at(l, "D", h))
                    pool.tensor_tensor(dt[:, 0:896], dt[:, 0:896], rc[:, RC_EYE:RC_EYE + 896], ALU.add)\
                        .then_inc(*GR.did((l, "D1", h)))
                    pool.wait_ge(*AR.at(l, "D2", h))
                    pool.tensor_tensor(dt[:, 896:1536], dt[:, 896:1536], tmp[:, 896:1536], ALU.add)\
                        .then_inc(*GR.did((l, "D2", h)))
                    if l == 0:
                        pool.wait_ge(*GR.at(l, "D1", h))
                        pool.tensor_copy(work[:, W_CD + 384 * h:W_CD + 384 * h + 384], dt[:, 256:640])\
                            .then_inc(*GR.did((l, "CD", h)))

            def gdn(l):
                for n in range(CHUNKS):
                    GR_ = [group(d) for d in range(2)]
                    need_o = l == 0 or n >= 2
                    for d in range(2):
                        g, c = GR_[d], chunk_of(n, d)
                        if n > 0:
                            pool.wait_ge(*TG.at(l, n - 1, d, "upd"))
                        pool.tensor_tensor(g["Ag"], all_heads(mat[:, LE if d == 0 else GE, :]),
                                           per_head(gs[:, 0, c, 4 * d:4 * d + 4]), ALU.mult)\
                            .then_inc(*GG.did((l, n, d, "Ag")))
                    for d in range(2):
                        g, c = GR_[d], chunk_of(n, d)
                        pool.wait_ge(*AG.at(l, n, d, "dec"))
                        pool.tensor_tensor(g["decm"], g["decm"], all_heads(mat[:, GE if d == 0 else LE, :]), ALU.mult)\
                            .then_inc(*GG.did((l, n, d, "decm")))
                        pool.wait_ge(*GG.at(l, n, d, "decm"))
                        pool.tensor_tensor(g["bdec"], g["decm"], per_head(gs[:, 5, c, 4 * d:4 * d + 4]), ALU.mult)\
                            .then_inc(*GG.did((l, n, d, "bdec")))
                    if n > 0:
                        for d in range(2):
                            g, c = GR_[d], chunk_of(n, d)
                            pool.wait_ge(*VG.at(l, n - 1, d, "S"))
                            pool.tensor_tensor(g["Sgl"], g["S"], per_head(gs[:, 9, c, 4 * d:4 * d + 4]), ALU.mult)\
                                .then_inc(*GG.did((l, n, d, "Sgl")))
                    for d in range(2):
                        g = GR_[d]
                        eye = all_heads(ident)
                        pool.wait_ge(*VG.at(l, n, d, "L"))
                        m = lev[:, d, :, :]
                        mx = lev[:, 1 - d, :, :]
                        pool.tensor_tensor(g["X"], g["L"], all_heads(mx[:, 0, :]), ALU.mult)\
                            .then_inc(*GG.did((l, n, d, "x")))
                        pool.wait_ge(*GG.at(l, n, d, "x"))
                        pool.tensor_tensor(g["X"], eye, g["X"], ALU.subtract).then_inc(*GG.did((l, n, d, "X0")))
                        pool.wait_ge(*AG.at(l, n, d, "LT"))
                        pool.tensor_tensor(g["Y"], g["LT"], all_heads(m[:, 0, :]), ALU.mult)\
                            .then_inc(*GG.did((l, n, d, "y")))
                        pool.wait_ge(*GG.at(l, n, d, "y"))
                        pool.tensor_tensor(g["Y"], eye, g["Y"], ALU.subtract).then_inc(*GG.did((l, n, d, "Y0")))
                    for i in range(1, NLEV):
                        for d in range(2):
                            g = GR_[d]
                            if i == 1:
                                pool.wait_ge(*TG.at(l, n, d, "LT"))
                                pool.wait_ge(*GG.at(l, n, d, "X0"))
                            elif i == 2:
                                if need_o:
                                    pool.wait_ge(*TG.at(l, n, d, "attnT"))
                            else:
                                pool.wait_ge(*TG.at(l, n, d, "P", i - 2))
                            pool.tensor_tensor(g["NT"][i % 2], g["LT"], all_heads(lev[:, d, i, :]), ALU.mult)\
                                .then_inc(*GG.did((l, n, d, "NT", i)))

            for stage, l in ORDER:
                if before((stage, l)):
                    fence(pool, before((stage, l)))
                if stage == "mod":
                    pool.dma_start(par[:, :], layer_params[l, :, :]).then_inc(params_in, 16)
                    pool.dma_start(wab[:, :], w_ab[l, :, :]).then_inc(params_in, 16)
                elif stage.startswith("filter_"):
                    filters(l, stage[7:])
                elif stage == "hy_proj":
                    halo(l, "hy", W_RAW)
                elif stage.startswith("conv_"):
                    long_conv(l, stage[5:])
                elif stage == "ret":
                    retention(l)
                elif stage == "gdn_proj":
                    halo(l, "gd", W_GRAW)
                elif stage == "gdn":
                    gdn(l)
                close("pool", (stage, l))


W_CD = W_RM + 2048


def constants():
    i = np.arange(P)
    r, c = i[:, None], i[None, :]
    mats = np.zeros((P, 8, P))
    mats[:, IDENT] = r == c
    mats[:, ONES] = 1
    half = (c % 64) // 32
    mats[:, PERM] = np.where(half == 0, -(r == c + 32).astype(float), (r == c - 32).astype(float))
    mats[:, BD64] = (r // 64 == c // 64) / 64.0
    mats[:, LE], mats[:, GT], mats[:, GE], mats[:, LT] = r <= c, r > c, r >= c, r < c
    lev = np.zeros((P, 2, NLEV, P))
    for k in range(NLEV):
        b = 1 << k
        m = (r // (2 * b) == c // (2 * b)) & ((r // b) % 2 == 1) & ((c // b) % 2 == 0)
        lev[:, 0, k], lev[:, 1, k] = m.T, m

    def dft(L):
        n = L // P
        k, t = np.arange(L), np.arange(L)
        th = 2 * np.pi * ((2 * k[None, :] + 1) * t[:, None] % (4 * L)) / (4 * L)
        fw = [f(th).reshape(n, P, L).transpose(1, 0, 2) for f in (np.cos, np.sin)]
        bw = [(f(th).T / L).reshape(n, P, L).transpose(1, 0, 2) for f in (np.cos, np.sin)]
        return np.stack(fw + bw, axis=1).reshape(P, -1)

    def window(L):
        t = np.linspace(0.0, 1.0, L)
        lo, hi = math.log(1e-2) / 1.5, math.log(1e-2) / 0.3
        w = np.exp(-t[:, None] * np.abs(np.linspace(lo, hi, HYW))[None, :])
        w = w.reshape(L // P, P, HYW)
        first = w[0:1].copy()
        first[0, 0] = 0
        return np.concatenate([w, first]).transpose(1, 0, 2).reshape(P, -1)

    f32 = np.float32
    z = np.zeros((64, TOK), f32)
    for L, at in ((LAT, 0), (CTX, LAT)):
        pos = np.arange(L, dtype=f32)
        f = np.linspace(1e-4, 15, 16, dtype=f32)
        ang = (f32(2.0 * math.pi / L) * pos[:, None]) * f[None, :]
        z[0, at:at + L] = np.linspace(0.0, 1.0, L, dtype=f32)
        z[1:17, at:at + L] = np.cos(ang).T
        z[17:33, at:at + L] = -np.sin(ang).T
    d = np.arange(896)[None, :] - 384 - r
    dc = np.arange(640)[None, :] - 128 - r
    ret = np.concatenate([np.maximum(d, 0), np.maximum(-d, 0), d == 0, dc + 256, 512 - dc], axis=1)
    inv = 10000.0 ** (-np.arange(16) / 16)
    tok = np.arange(LAT)
    ang = np.concatenate([(tok // 64)[:, None] * inv, (tok % 64)[:, None] * inv], axis=1)
    rope = np.stack([f(ang).T[np.arange(P) % 32] for f in (np.cos, np.sin)], axis=1)
    return {"mats": mats.astype(f32), "level_masks": lev, "tab_lat": dft(LAT).astype(f32),
            "tab_ctx": dft(CTX).astype(f32), "win_lat": window(LAT).astype(f32),
            "win_ctx": window(CTX).astype(f32), "zpos": z, "ret_tab": ret.astype(f32),
            "rope_tab": rope.astype(f32)}


def kernel(**inputs):
    import ml_dtypes
    import concourse.bacc as bacc
    from concourse.bass_utils import run_bass_kernel_spmd

    a = {k: np.asarray(v) for k, v in inputs.items()}
    f32 = np.float32

    def feature_major(v):
        return v.T.reshape(v.shape[1] // P, P, v.shape[0]).transpose(1, 0, 2)

    def per_partition(v):
        return v.reshape(-1, P).T

    blocks = []

    def add(w):
        v = w.reshape(w.shape[0] // P, P, w.shape[1]).transpose(1, 0, 2).reshape(P, -1)
        b = np.zeros((P, BLK), f32)
        b[:, :v.shape[1]] = v
        blocks.append(b)

    params, fparams, wabs = [], [], []
    for l in range(DEPTH):
        for b in range(N_MODB):
            add(a["mod_w"][l][:, 256 * b:256 * b + 256])
        for c in IN_BLOCKS:
            add(a["w_in"][l][:, c:c + 256])
        for b in range(N_OUTB):
            add(a["w_out"][l][:, 256 * b:256 * b + 256])
        for b in range(N_FIB):
            add(np.concatenate([a["ffn_w_in"][l][:, P * b:P * b + P],
                                a["ffn_w_in"][l][:, FF + P * b:FF + P * b + P]], axis=1))
        for b in range(DC):
            for half in range(2):
                add(a["ffn_w_out"][l][FF // 2 * half:FF // 2 * (half + 1), P * b:P * b + P])
        p = np.zeros((P, NPAR), f32)
        p[:, MODB:MODB + 48] = per_partition(a["mod_b"][l])
        p[:, N1G:N1G + 8] = per_partition(a["norm1_g"][l])
        p[:, N2G:N2G + 8] = per_partition(a["norm2_g"][l])
        p[:, FNG:FNG + 8] = per_partition(a["final_norm_g"])
        p[:, HCW:HCW + 18] = per_partition(a["hy_conv_w"][l].reshape(-1))
        p[:, HCB:HCB + 6] = per_partition(a["hy_conv_b"][l])
        p[:, GCW:GCW + 36] = per_partition(a["gdn_conv_w"][l].reshape(-1))
        p[:, GNG] = a["gdn_norm_g"][l]
        p[:, ALOG:ALOG + 8] = a["gdn_a_log"][l].reshape(-1)
        p[:, DTB:DTB + 8] = a["gdn_dt_bias"][l].reshape(-1)
        p[:, RLOG:RLOG + 8] = a["ret_decay_logit"][l].reshape(-1)
        p[:, EPSC] = EPS
        p[:, LNQ] = -0.5 * math.log(P)
        params.append(p)
        q = np.zeros((64, NFP), f32)
        q[0:33, FW1:FW1 + 64] = a["hy_f_w1"][l]
        q[:, FW2:FW2 + 64] = a["hy_f_w2"][l]
        q[:, FW3:FW3 + 1024] = a["hy_f_w3"][l]
        for i, k in enumerate(("hy_f_b1", "hy_f_freq1", "hy_f_b2", "hy_f_freq2")):
            q[:, FVEC + i] = a[k][l]
        q[0, FBIAS:FBIAS + 512] = a["hy_bias"][l].reshape(-1)
        fparams.append(q)
        wabs.append(a["w_in"][l][:, AB_COL:AB_COL + 16].reshape(DC, P, 16).transpose(1, 0, 2).reshape(P, -1))

    cst = constants()
    arrays = {
        "tokens": feature_major(np.concatenate([a["ctx"][0], a["x"][0]])),
        "cond": feature_major(np.stack([a["c"][0], a["c_ctx"]])),
        "weights": np.stack(blocks),
        "w_ab": np.stack(wabs),
        "layer_params": np.stack(params),
        "filter_params": np.stack(fparams),
        "mats": cst["mats"],
        "level_masks": cst["level_masks"].astype(ml_dtypes.bfloat16),
    }
    for k in ("tab_lat", "tab_ctx", "win_lat", "win_ctx", "zpos", "ret_tab", "rope_tab"):
        arrays[k] = cst[k]
    arrays = {k: np.ascontiguousarray(v) for k, v in arrays.items()}

    def program(values):
        nc = bacc.Bacc("TRN2", target_bir_lowering=False, num_devices=1)
        args = [nc.dram_tensor(f"in_{k}", v.shape, mybir.dt.from_np(v.dtype), kind="ExternalInput").ap()
                for k, v in arrays.items()]
        out = nc.dram_tensor("out_y", (P, DC, LAT), F32, kind="ExternalOutput").ap()
        backbone(nc, values, *args, out)
        return nc

    values = {}
    program(values)
    nc = program(values)
    r = run_bass_kernel_spmd(nc, [{f"in_{k}": v for k, v in arrays.items()}], core_ids=[0])
    y = r.results[0]["out_y"]
    return y.transpose(2, 1, 0).reshape(1, LAT, D)
```

```python
import math
from contextlib import ExitStack

import numpy as np

import concourse.bass as bass
from concourse import mybir

F32 = mybir.dt.float32
BF16 = mybir.dt.bfloat16
F32R = mybir.dt.float32r
ALU = mybir.AluOpType
ACT = mybir.ActivationFunctionType

P = 128
D = 1024
DC = D // P
CTX = 256
LAT = 512
TOK = CTX + LAT
DEPTH = 2
FF = 2816
FC = FF // P
HYW = 256
HEADS = 4
EPS = 1e-6
NLEV = 7
CHUNKS = TOK // P
SEG = {"ctx": (0, CTX), "lat": (CTX, LAT)}
BLK = 2048
RING = 3

HY_COL, QKV_COL, Z_COL, AB_COL = 0, 768, 2304, 2816
RQ_COL, RK_COL, RV_COL, RG_COL = 2832, 3088, 3344, 3600
N_MODB, N_OUTB, N_FIB, N_FOB = 24, 4, FC, 2 * DC
IN_BLOCKS = [HY_COL, HY_COL + 256, HY_COL + 512, RQ_COL, RK_COL, RV_COL, RG_COL] \
    + [QKV_COL + 256 * i for i in range(6)] + [Z_COL, Z_COL + 256]
N_INB = len(IN_BLOCKS)

MODB, N1G, N2G, FNG = 0, 48, 56, 64
HCW, HCB, GCW, GNG = 72, 90, 96, 132
ALOG, DTB, RLOG, EPSC, EPSQ = 136, 144, 152, 160, 161
NPAR = 164

IDENT, ONES, PERM, BD64, LE, GT, GE, LT = range(8)

FW1, FW2, FW3, FVEC, FBIAS = 0, 64, 128, 1152, 1156
NFP = FBIAS + 512

FILTERS_PE = (1, 4, 7, 8, 9, 10, 13, 15, 17, 19)
FILTERS_DVE = (2, 5, 8, 9, 10, 11, 12)
FILTERS_ACT = (3, 6, 14, 16, 18, 20)

MAGIC = 1.5 * 2.0 ** 23
TWO_PI_HI = 6.28125
TWO_PI_LO = 2 * math.pi - 6.28125
PI_IN = 3.1415925

WORK = 22528
W_TAB, W_K, W_CONV, W_RAW, W_TOK = 0, 8192, 14336, 17408, 19724
W_RQK, W_RV, W_RC, W_ROPE, W_D, W_DT, W_P = 0, 3072, 4608, 8576, 9600, 12672, 14208
W_RM = 17280
W_QKV, W_G, W_GRAW, W_GSQ = 0, 9216, 9216, 9216 + 3 * 772
W_HPART = 13584
RC_POS, RC_NEG, RC_EYE, RC_CF, RC_CB = 0, 896, 1792, 2688, 3328


class Steps:

    def __init__(self, sem, name, values):
        self.sem, self.name, self.values, self.n = sem, name, values, 0

    def did(self, key=None):
        self.n += 1
        if key is not None:
            self.values[(self.name, key)] = self.n
        return self.sem, 1

    def at(self, *key):
        return self.sem, self.values.get((self.name, key[0] if len(key) == 1 else key), 1)


def backbone(nc, values, tokens, cond, weights, w_ab, layer_params, filter_params, mats, level_masks,
             tab_lat, tab_ctx, win_lat, win_ctx, zpos, ret_tab, rope_tab, out):
    with ExitStack() as stack:
        def sb(name, shape, dt=F32):
            return stack.enter_context(nc.sbuf_tensor(name, shape, dt))

        def semaphore(name):
            return stack.enter_context(nc.semaphore(name))

        xT = sb("xT", [P, DC, TOK])
        ring = sb("ring", [P, RING, BLK])
        tmp_at = nc.sbuf_base
        tmp = sb("tmp", [P, 4, 512])
        area = nc.sbuf_base
        hT = sb("hT", [P, DC, TOK])
        mix = sb("mix", [P, DC, TOK])
        work = sb("work", [P, WORK])

        def over(name, shape, at):
            return nc.alloc_sbuf_tensor_at(name, shape, F32R, offset=area + 4 * at)
        hid = [over("hid_hi", [P, FC, LAT], DC * 2 * LAT), over("hid_lo", [P, FC, LAT], DC * 2 * LAT + FC * LAT)]
        hmod = [over("hmod_hi", [P, DC, LAT], 0), over("hmod_lo", [P, DC, LAT], DC * LAT)]
        mixp = [over("mix_hi", [P, DC, TOK], 2 * DC * TOK), over("mix_lo", [P, DC, TOK], 3 * DC * TOK)]
        w_at = DC * 2 * LAT + 2 * FC * LAT
        wpart = [over("w_hi", [P, 2, DC * P], w_at), over("w_lo", [P, 2, DC * P], w_at + 2 * DC * P)]
        mod_parts = [[over(f"mod_{part}_{i}", [P, BLK // 2], BLK // 2 * at) for i, at in enumerate(places)]
                     for part, places in (("hi", (1, 2, 3)), ("lo", (4, 5, 11)))]
        part_at = 2 * DC * TOK + W_HPART
        hpart = [over("h_hi", [P, DC, TOK], part_at), over("h_lo", [P, DC, TOK], 0)]
        in_parts = [over("in_hi", [P, 2, DC * P], part_at + DC * TOK),
                    nc.alloc_sbuf_tensor_at("in_lo", [P, 2, DC * P], F32R, offset=tmp_at)]
        mat = sb("mat", [P, 8, P])
        lev = sb("lev", [P, 2, P + 64 * (NLEV - 1)], BF16)
        par = sb("par", [P, NPAR])
        wab = sb("wab", [P, DC * 16])
        condT = sb("condT", [P, DC, 2])
        cond_parts = sb("cond_parts", [P, 4 * DC + P], F32R)
        cond_rows = cond_parts[:, 0:4 * DC].rearrange("p (k r e) -> p k r e", r=2, e=2)
        modv = sb("modv", [P, 48, 2])
        amp = sb("amp", [P, 2, DC, 2])
        rstd = sb("rstd", [P, TOK])
        gs = sb("gs", [P, 10, CHUNKS, 8])
        lam = sb("lam", [P, 4, 8])
        ps = stack.enter_context(nc.psum_tensor("ps", [P, 8, 512], F32))

        mixf = mix[:, :, :].rearrange("p a b -> p (a b)")
        hTf = hT[:, :, :].rearrange("p a b -> p (a b)")

        ab_rows = tmp[0:16, :, :].rearrange("p a b -> p (a b)")[:, 0:TOK]

        modrow = hTf[0:4, 0:512].rearrange("p (i c) -> p i c", i=2)

        def wk(at, *shape):
            n = int(np.prod(shape))
            v = work[:, at:at + n]
            if len(shape) == 2:
                return v.rearrange("p (a b) -> p a b", b=shape[1])
            if len(shape) == 3:
                return v.rearrange("p (a b c) -> p a b c", b=shape[1], c=shape[2])
            return v

        ident = mat[:, IDENT, :]
        ones = mat[:, ONES, :]
        eps = par[:, EPSC:EPSC + 1]
        epsq = par[:, EPSQ:EPSQ + 1]

        landed = [semaphore(f"weights_landed_{i}") for i in range(RING)]
        params_in = semaphore("params_in")
        tables_in = semaphore("tables_in")
        filter_in = semaphore("filter_params_in")
        start_in = semaphore("start_in")
        tokens_in = semaphore("tokens_in")
        stored = semaphore("out_stored")

        PARTS = ("proj", "hyena", "ret", "gdn")
        engines = ("tensor", "vector", "scalar", "pool")
        S = {(e, p): Steps(semaphore(f"{e}_{p}_steps"), f"{e}_{p}", values) for e in engines for p in PARTS}

        def close(e, stage):
            for p in PARTS:
                values[(e, p, stage)] = S[e, p].n

        def fence(eng, stage):
            for e in engines:
                for p in PARTS:
                    v = values.get((e, p, stage), 0)
                    if v:
                        eng.wait_ge(S[e, p].sem, v)

        def stages():
            for l in range(DEPTH):
                yield "mod", l
                yield "norm1", l
                for seg in (("lat", "ctx") if l == 0 else ("lat",)):
                    if seg == "lat":
                        yield "hy_proj", l
                    else:
                        yield "filter_ctx", l
                    yield "conv_" + seg, l
                yield "ret_proj", l
                yield "ret", l
                yield "gdn_proj", l
                yield "gdn", l
                yield "gdn_out", l
                yield "out", l
                for seg in (("lat", "ctx") if l == 0 else ("lat",)):
                    yield "norm2_" + seg, l
                    yield "ffn_in_" + seg, l
                    yield "ffn_out_" + seg, l
            yield "final", DEPTH - 1

        ORDER = list(stages())

        def chained(e, stage):
            return stage.startswith("ffn_in") or e == "tensor" and (stage.startswith("ffn_out") or stage == "hy_proj")

        def before(stage):
            i = ORDER.index(stage)
            return ORDER[i - 1] if i else None

        N_LAYER = N_MODB + N_INB + N_OUTB + N_FIB + N_FOB
        OFFSET = {"mod": 0, "in": N_MODB, "out": N_MODB + N_INB, "fi": N_MODB + N_INB + N_OUTB,
                  "fo": N_MODB + N_INB + N_OUTB + N_FIB}
        STREAM, POSITION = [], {}
        for l_ in range(DEPTH):
            for part, count in (("mod", N_MODB), ("in", N_INB), ("out", N_OUTB)):
                for i in range(count):
                    POSITION[l_, part, i] = len(STREAM)
                    STREAM.append(N_LAYER * l_ + OFFSET[part] + i)
            for s_ in (("lat", "ctx") if l_ == 0 else ("lat",)):
                for part, count in (("fi", N_FIB), ("fo", N_FOB)):
                    for i in range(count):
                        POSITION[l_, part + "_" + s_, i] = len(STREAM)
                        STREAM.append(N_LAYER * l_ + OFFSET[part] + i)

        def block_no(l, part, i):
            return POSITION[l, part, i]

        PIECES = []
        for l_ in range(DEPTH):
            cut_parts = [("mod", 0, N_MODB), ("in", 7, N_INB), ("out", 0, N_OUTB)]
            for s_ in (("lat", "ctx") if l_ == 0 else ("lat",)):
                cut_parts += [("fi_" + s_, 0, N_FIB), ("fo_" + s_, 0, N_FOB)]
            for part, first, count in cut_parts:
                PIECES += [(POSITION[l_, part, i], m) for i in range(first, count) for m in range(2)]
        PIECE = {p_: q for q, p_ in enumerate(PIECES)}
        OF_MOD = {POSITION[l_, "mod", i] for l_ in range(DEPTH) for i in range(N_MODB)}
        OF_IN = {POSITION[l_, "in", i] for l_ in range(DEPTH) for i in range(7, N_INB)}
        OF_ROWS = {POSITION[l_, "fo_" + s_, i] for l_ in range(DEPTH)
                   for s_ in (("lat", "ctx") if l_ == 0 else ("lat",)) for i in range(N_FOB)}

        def piece(q):
            n, m = PIECES[q]
            if n in OF_MOD:
                cut = [v.rearrange("p (k c) -> p k c", c=256) for v in
                       [ring[:, n % RING, BLK // 2 * m:BLK // 2 * (m + 1)]] + [w[q % 3][:, :] for w in mod_parts]]
                return n, 4 * m, 4, cut[0], cut[1:]
            if n in OF_ROWS:
                k0, k1 = ((0, 6), (6, 11))[m]
                raw = ring[:, n % RING, P * k0:P * k1].rearrange("p (k c) -> p k c", c=P)
            else:
                k0, k1 = 0, DC
                raw = ring[:, n % RING, :].rearrange("p (k c) -> p k c", k=DC)[:, :, P * m:P * m + P]
            parts = [w[:, q % 2, 0:P * (k1 - k0)].rearrange("p (k c) -> p k c", c=P)
                     for w in (in_parts if n in OF_IN else wpart)]
            return n, k0, k1 - k0, raw, parts

        def wait_block(eng, n):
            eng.wait_ge(landed[n % RING], 16 * (n // RING + 1))

        def segs(l, both=False):
            return ["lat", "ctx"] if (l == 0 or both) else ["lat"]

        def tables(s):
            n = SEG[s][1]
            return work[:, W_TAB:W_TAB + 4 * (n // P) * n].rearrange("p (i t f) -> p i t f", i=4, f=n)

        def sum_diff(s):
            n = SEG[s][1] // P
            at = W_CONV if s == "lat" else W_TOK
            return work[:, at:at + 2 * n * 512].rearrange("p (i t c) -> p i t c", i=2, c=512)

        def norm_area(name, s):
            t0, w = SEG[s]
            if name != "norm2":
                return hT[:, :, t0:t0 + w]
            at = DC * 2 * LAT - DC * TOK
            return mixf[:, at:at + DC * w].rearrange("p (k t) -> p k t", t=w)

        def halves(s):
            at = W_TOK if s == "lat" else W_RAW
            return wk(at, 2, 512), wk(at + 1024, 2, 512)

        def products():
            return mixf[:, 1536:1536 + 2048].rearrange("p (i c) -> p i c", c=512)

        def spectrum():
            return wk(W_K, 4, 2 * 768)

        def tables_count(stage, l):
            n = 0
            for st, k in ORDER:
                if st in ("mod", "filter_ctx"):
                    n += 2
                elif st == "ret_proj":
                    n += 2
                if (st, k) == (stage, l):
                    return 16 * n

        def filters_count(l, s):
            return 32 * (l + 1 + (1 if s == "ctx" or l > 0 else 0))

        def ret_work(l):
            for s in segs(l):
                for h in range(HEADS):
                    yield s, h, (list(range(CHUNKS)) if s == "lat" else [0, 1])

        def ret_unit(l, s, h, i):
            return h * CHUNKS + i if s == "lat" else HEADS * CHUNKS + 2 * h + i

        def ret_out(s, p):
            w = SEG[s][1]
            at = W_P if p else W_RM
            v = work[:, at:at + 4 * 512].rearrange("p (i t) -> p i t", i=4)
            return [v[:, i, 0:w] for i in range(4)]

        def units_of(l, c):
            at = sum(len(segs(l, both=(k >= 4))) for k in range(c))
            return list(enumerate(segs(l, both=(c >= 4)), at))

        def squares():
            return wk(W_GSQ, 2, 512)

        def roots():
            return wk(W_GSQ + 1024, 2, 512)

        def head_squares_of():
            return {"lat": wk(W_G, HEADS, LAT), "ctx": wk(W_G + HEADS * LAT, HEADS, CTX)}

        def head_roots_of():
            at = W_G + HEADS * TOK
            return {"lat": work[:, at:at + LAT], "ctx": work[:, at + LAT:at + TOK]}

        def norm_place(s, h):
            return ps[:, 2 + h, 0:LAT] if s == "lat" else ps[:, (6 + h) % 8, 0:CTX]

        def chunk_of(n, d):
            if d == 0:
                return n
            return 1 - n if n < 2 else CHUNKS + 1 - n

        def need_o(l, n):
            return l < DEPTH - 1 or n >= 2

        def flat(v):
            return v.rearrange("p h c -> p (h c)")

        def group(d):
            names = ["dec", "Ag", "kbg", "kg", "vb", "nwT", "L", "attn", "LT", "attnT", "qgT", "X", "Y"]
            at = W_G + d * len(names) * 512
            g = {k: wk(at + 512 * i, HEADS, P) for i, k in enumerate(names)}
            g["vn"] = g["egc"] = g["Ag"]
            g["P"] = flat(g["nwT"])[:, 0:256]
            for i, k in enumerate(("S", "Sgl")):
                o = 3072 + (2 * d + i) * 512
                g[k] = hTf[:, o:o + 512].rearrange("p (h c) -> p h c", c=P)
            return g

        oacc = hTf[:, 0:4 * TOK].rearrange("p (h t) -> p h t", t=TOK)

        def joined(v, d, i):
            return v.rearrange("p h (n t b) -> p h n t b", t=2, b=1 << i)[:, :, :, d, :]

        def packed(v, i):
            return v.rearrange("p (h n b) -> p h n b", h=HEADS, b=1 << i)

        def per_head(v):
            return v.unsqueeze(2).broadcast_to([P, HEADS, P])

        def all_heads(m):
            return m.unsqueeze(1).broadcast_to([P, HEADS, P])

        def decay_of(h):
            return (work[:, W_D + 1536 * (h % 2):W_D + 1536 * (h % 2) + 1536], work[:, W_DT:W_DT + 1536])

        def ctx_decay(h):
            return work[:, W_CD + 384 * h - 256:W_CD + 384 * h + 640]

        block = stack.enter_context(nc.Block())

        @block.sync
        def _(sp):
            sp.dma_start(condT[:, :, :], cond).then_inc(start_in, 16)
            sp.dma_start(mat[:, :, :], mats).then_inc(start_in, 16)
            sp.dma_start(lev[:, :, :], level_masks).then_inc(start_in, 16)
            for n, at in enumerate(STREAM):
                if n == 2 * RING:
                    sp.dma_start(xT[:, :, :], tokens).then_inc(tokens_in, 16)
                if n >= RING:
                    if (n - RING, 1) in PIECE:
                        sp.wait_ge(*S["vector", "proj"].at("lo", PIECE[n - RING, 1]))
                    else:
                        sp.wait_ge(*S["tensor", "proj"].at("block", n - RING))
                sp.dma_start(ring[:, n % RING, :], weights[at, :, :]).then_inc(landed[n % RING], 16)
            sp.wait_ge(*S["vector", "proj"].at("final", 7))
            sp.dma_start(out, hT[:, :, CTX:TOK]).then_inc(stored, 16)
            sp.wait_ge(stored, 16)

        @block.tensor
        def _(pe):
            T = S["tensor", "proj"]
            V = S["vector", "proj"]
            A = S["scalar", "proj"]

            def mod(l):
                if l == 0:
                    pe.wait_ge(start_in, 48)
                pe.wait_ge(*V.at("cond_lo"))
                filt = filters(l, "lat")

                def turn(b):
                    pe.wait_ge(*A.at("modrow", l, b))
                    for m in range(2):
                        mm = pe.transpose(ps[:, 7, 8 * b + 4 * m:8 * b + 4 * m + 4],
                                          modrow[:, b % 2, P * m:P * m + P], ident[0:4, 0:4])
                    mm.then_inc(*T.did(("turned", l, b)))
                for b in range(N_MODB):
                    n = block_no(l, "mod", b)
                    if b >= 2:
                        pe.wait_ge(*A.at("modrow", l, b - 2))
                    for m in range(2):
                        q = PIECE[n, m]
                        k0, kc, parts = piece(q)[1], piece(q)[2], piece(q)[4]
                        for i, ready in ((0, A.at("hi", q)), (1, V.at("lo", q))):
                            pe.wait_ge(*ready)
                            for k in range(kc):
                                at = 4 * (k0 + k)
                                mm = pe.matmul(ps[:, b % 2, 0:256], cond_parts[:, at:at + P], parts[i][:, k, :],
                                               start=(m == 0 and i == 0 and k == 0),
                                               stop=(m == 1 and i == 1 and k == kc - 1))
                        mm.then_inc(*T.did(("piece", q)))
                    T.values[(T.name, ("block", n))] = T.n
                    if b >= 1:
                        turn(b - 1)
                    if b in FILTERS_PE:
                        next(filt)
                turn(N_MODB - 1)
                for _ in filt:
                    pass

            def norm(name, l, sgs):
                for s in sgs:
                    t0, w = SEG[s]
                    for k in range(DC):
                        pe.wait_ge(*A.at(name, l, s, "sq", k))
                        sq = norm_area(name, s)[:, k, :]
                        mm = pe.matmul(ps[:, 0 if s == "lat" else 1, 0:w], ones, sq,
                                       start=(k == 0), stop=(k == DC - 1))
                    mm.then_inc(*T.did((name, l, s)))

            def product(name, l, item, m, n, s, src, kc, free):
                t0, w = SEG[s]
                bank = item % 3 + (0 if s == "lat" else 3)
                if free is not None:
                    pe.wait_ge(*free)
                wv = ring[:, n % RING, :].rearrange("p (k c) -> p k c", c=256)
                for k in range(kc):
                    if item == 0:
                        pe.wait_ge(*A.at("norm1", l, s, "h", k))
                    mm = pe.matmul(ps[:, bank, 0:w], wv[:, k, P * m:P * m + P], src[:, k, t0:t0 + w],
                                   start=(k == 0), stop=(k == kc - 1))
                mm.then_inc(*T.did((name, l, item, s)))

            def columns(name, l, part, blocks, sgs_of, src, evac, kc=DC):
                item = 0
                for b in blocks:
                    n = block_no(l, part, b)
                    wait_block(pe, n)
                    for m in range(2):
                        ss = sgs_of(item)
                        for s in ss:
                            free = evac(item - 3, s) if item >= 3 and s in sgs_of(item - 3) else None
                            product(name, l, item, m, n, s, src, kc, free)
                        if m == 1:
                            T.values[(T.name, ("block", n))] = T.n
                        item += 1

            def hy_proj(l):
                columns("hy", l, "in", range(0, 3), lambda i: segs(l), hT,
                        lambda i, s: A.at("hy", l, i, s))

            def ret_proj(l):
                both = lambda i: segs(l, both=(i in (2, 3)))
                columns("ret", l, "in", (3, 4), both, hT, lambda i, s: A.at("ret", l, i, s))
                n = block_no(l, "in", 5)
                wait_block(pe, n)
                wv = ring[:, n % RING, :].rearrange("p (k c) -> p k c", c=256)
                for c in range(CHUNKS):
                    bank = 6 + c % 2
                    if c >= 2:
                        pe.wait_ge(*V.at("rv", l, c - 2))
                    for k in range(DC):
                        mm = pe.matmul(ps[:, bank, 0:256], hT[:, k, P * c:P * c + P], wv[:, k, :],
                                       start=(k == 0), stop=(k == DC - 1))
                    mm.then_inc(*T.did(("rv", l, c)))
                T.values[(T.name, ("block", n))] = T.n
                n = block_no(l, "in", 6)
                wait_block(pe, n)
                for m in range(2):
                    for s in segs(l):
                        item = 4 + m
                        free = A.at("ret", l, item - 3, s) if s in both(item - 3) else None
                        product("ret", l, item, m, n, s, hT, DC, free)
                T.values[(T.name, ("block", n))] = T.n

            def gdn_proj(l):
                def between(i):
                    if i == 1:
                        gate_sums(l)
                    if 3 <= i < 11:
                        head_norm(l, i - 3)
                both = lambda i: segs(l, both=(4 <= i < 12))
                for item in range(16):
                    q = PIECE[block_no(l, "in", 7 + item // 2), item % 2]
                    pe.wait_ge(*V.at("lo", q))
                    for s in both(item):
                        t0, w = SEG[s]
                        if item >= 3 and s in both(item - 3):
                            pe.wait_ge(*A.at("gd", l, item - 3, s))
                        split_product(q, ps[:, item % 3 + (0 if s == "lat" else 3), 0:w],
                                      lambda b, k: hpart[b][:, k, t0:t0 + w], 0,
                                      made=(lambda k: A.at("hT_hi", l, k), lambda k: V.at("hT_lo", l, k))
                                      if item == 0 else None).then_inc(*T.did(("gd", l, item, s)))
                    T.values[(T.name, ("piece", q))] = T.n
                    between(item)

            def split_product(q, out_, src, k_at, start=True, stop=True, made=None):
                n, k0, kc, raw, parts = piece(q)
                for i, (a, b) in enumerate(((1, 0), (0, 1), (0, 0))):
                    for k in range(kc):
                        if made is not None and i < 2:
                            pe.wait_ge(*made[b](k))
                        mm = pe.matmul(out_, parts[a][:, k, :], src(b, k_at + k), start=(start and i == 0 and k == 0),
                                       stop=(stop and i == 2 and k == kc - 1))
                return mm

            def out_proj(l):
                for item in range(DC):
                    q = PIECE[block_no(l, "out", item // 2), item % 2]
                    pe.wait_ge(*V.at("lo", q))
                    for s in segs(l):
                        t0, w = SEG[s]
                        if item >= 3:
                            pe.wait_ge(*V.at("out", l, item - 3, s))
                        split_product(q, ps[:, item % 3 + (0 if s == "lat" else 3), 0:w],
                                      lambda b, k: mixp[b][:, k, t0:t0 + w], 0,
                                      made=(lambda k: A.at("mix_hi", l, k), lambda k: V.at("mix_lo", l, k))
                                      if item == 0 else None)\
                            .then_inc(*T.did(("out", l, item, s)))
                    T.values[(T.name, ("piece", q))] = T.n

            def ffn_in(l, s):
                w = SEG[s][1]
                for item in range(2 * FC):
                    q = PIECE[block_no(l, "fi_" + s, item // 2), item % 2]
                    pe.wait_ge(*V.at("lo", q))
                    if item >= 6:
                        pe.wait_ge(*(V if item % 2 else A).at("fi", l, s, item - 6))
                    split_product(q, ps[:, item % 6, 0:w], lambda b, k: hmod[b][:, k, 0:w], 0,
                                  made=(lambda k: A.at("h_hi", l, s, k), lambda k: V.at("h_lo", l, s, k))
                                  if item == 0 else None)\
                        .then_inc(*T.did(("fi", l, s, item)))
                    T.values[(T.name, ("piece", q))] = T.n

            def ffn_out(l, s):
                w = SEG[s][1]
                for item in range(DC):
                    for part in range(4):
                        q = PIECE[block_no(l, "fo_" + s, 2 * item + part // 2), part % 2]
                        pe.wait_ge(*V.at("lo", q))
                        if part == 0 and item >= 6:
                            pe.wait_ge(*V.at("fo", l, s, item - 6))
                        if part == 0 and item == 0:
                            pe.wait_ge(*A.at("fi", l, s, 2 * FC - 2))
                        at = 11 * (part // 2) + piece(q)[1]
                        split_product(q, ps[:, item % 6, 0:w], lambda b, k: hid[b][:, k, 0:w], at,
                                      start=(part == 0), stop=(part == 3),
                                      made=(lambda k: A.at("hid_hi", l, s, at + k),
                                            lambda k: V.at("hid_lo", l, s, at + k)) if item == 0 else None)\
                            .then_inc(*T.did(("fo", l, s, item, part)))
                        T.values[(T.name, ("piece", q))] = T.n

            TH, VH, AH, GH = (S[e, "hyena"] for e in engines)

            def filters(l, s):
                L = SEG[s][1]
                nt = L // P
                o = 0 if s == "lat" else 1536
                fp = mixf[0:64, o:o + NFP]
                zT = mixf[0:64, o + NFP:o + NFP + L]
                hb = mixf[0:64, o + NFP + L:o + NFP + 2 * L]
                pe.wait_ge(filter_in, filters_count(l, s))
                pe.matmul(ps[0:64, 2, 0:L], fp[:, FW1:FW1 + 64], zT, start=True, stop=True)\
                    .then_inc(*TH.did((l, s, "h1")))
                yield
                pe.wait_ge(*AH.at(l, s, "sin", 0))
                pe.matmul(ps[0:64, 3, 0:L], fp[:, FW2:FW2 + 64], hb, start=True, stop=True)\
                    .then_inc(*TH.did((l, s, "h2")))
                yield
                pe.wait_ge(*AH.at(l, s, "sin", 1))
                for t in range(nt):
                    if t >= 2:
                        pe.wait_ge(*VH.at(l, s, "hn", t - 2))
                    for a in range(2):
                        mm = pe.matmul(ps[:, 2 + 2 * (t % 2) + a, :], hb[:, P * t:P * t + P],
                                       fp[:, FW3 + 512 * a:FW3 + 512 * a + 512], start=True, stop=True)
                    mm.then_inc(*TH.did((l, s, "h3", t)))
                    yield
                tab = tables(s)
                sd = sum_diff(s)
                pe.wait_ge(tables_in, tables_count(("mod" if s == "lat" else "filter_ctx"), l))
                pe.wait_ge(*VH.at(l, s, "bias"))
                pe.wait_ge(*GH.at(l, s, "diff", nt - 1))
                for j in range(nt):
                    for i, b in ((0, 6), (1, 5)):
                        if j >= 1:
                            pe.wait_ge(*AH.at(l, s, "K", i, j - 1))
                        for t in range(nt):
                            mm = pe.matmul(ps[:, b, :], tab[:, i, t, P * j:P * j + P], sd[:, i, t, :],
                                           start=(t == 0), stop=(t == nt - 1))
                        mm.then_inc(*TH.did((l, s, "K", i, j)))
                    yield

            def long_conv(l, s):
                t0, L = SEG[s]
                nt = L // P
                tab = tables(s)
                conv = wk(W_CONV, 4, TOK)
                tok = wk(W_TOK, 4, 512)
                yf = wk(W_RAW, 4, 512)
                for t in range(nt):
                    if t >= 2:
                        pe.wait_ge(*AH.at(l, s, "tok", t - 2))
                    for c in range(4):
                        mm = pe.transpose(ps[:, t % 2, P * c:P * c + P], conv[:, c, t0 + P * t:t0 + P * t + P], ident)
                    mm.then_inc(*TH.did((l, s, "tok", t)))
                for n in range(2):
                    if n == 0:
                        pe.wait_ge(*AH.at(l, s, "tok", nt - 1))
                    else:
                        pe.wait_ge(*VH.at(l, s, "z1", nt - 1))
                    for j in range(nt):
                        if j >= 2:
                            pe.wait_ge(*VH.at(l, s, n, "p2", j - 2))
                        for i in range(2):
                            for t in range(nt):
                                mm = pe.matmul(ps[:, 2 + j % 2, 256 * i:256 * i + 256],
                                               tab[:, i, t, P * j:P * j + P], tok[:, t, 0:256],
                                               start=(t == 0), stop=(t == nt - 1))
                        mm.then_inc(*TH.did((l, s, n, "U", j)))
                    pe.wait_ge(*GH.at(l, s, n, "Y", nt - 1))
                    if n == 0:
                        for t in range(nt):
                            if t >= 2:
                                pe.wait_ge(*VH.at(l, s, "z1", t - 2))
                            for j in range(nt):
                                for i in range(2):
                                    mm = pe.matmul(ps[:, 4 + t % 2, 0:256], tab[:, 2 + i, j, P * t:P * t + P],
                                                   yf[:, j, 256 * i:256 * i + 256],
                                                   start=(i == 0 and j == 0), stop=(i == 1 and j == nt - 1))
                            mm.then_inc(*TH.did((l, s, "y1", t)))
                    else:
                        for c in range(2):
                            for j in range(nt):
                                for i in range(2):
                                    mm = pe.matmul(ps[:, 6 + c, 0:L], yf[:, j, 256 * i + P * c:256 * i + P * c + P],
                                                   tab[:, 2 + i, j, :],
                                                   start=(i == 0 and j == 0), stop=(i == 1 and j == nt - 1))
                            mm.then_inc(*TH.did((l, s, "y2", c)))

            TR, VR, AR, GR = (S[e, "ret"] for e in engines)

            def retention(l):
                rqk = wk(W_RQK, 4, TOK)
                rv = wk(W_RV, CHUNKS, 256)
                pr = wk(W_P, 6, 512)
                pe.wait_ge(tables_in, tables_count("ret_proj", l))
                for c in range(4):
                    pe.matmul(ps[:, c, :], mat[:, PERM, :], rqk[:, c, CTX:TOK], start=True, stop=True)\
                        .then_inc(*TR.did((l, "perm", c)))
                pe.wait_ge(params_in, 32 * (l + 1))
                for b, (t0, w) in zip((6, 7), (SEG["lat"], SEG["ctx"])):
                    for k in range(DC):
                        mm = pe.matmul(ps[0:16, b, 0:w], wab[:, 16 * k:16 * k + 16], hT[:, k, t0:t0 + w],
                                       start=(k == 0), stop=(k == DC - 1))
                    mm.then_inc(*T.did(("ab_row", l, b)))
                pe.wait_ge(*V.at("ab_row", l, 7))
                for c in range(CHUNKS):
                    mm = pe.transpose(ps[:, 6, 16 * c:16 * c + 16], ab_rows[:, P * c:P * c + P], ident[0:16, 0:16])
                mm.then_inc(*T.did(("ab", l)))
                pe.wait_ge(*VR.at(l, "rope", 3))
                pe.wait_ge(*S["vector", "gdn"].at(l, "ab"))
                for s, h, chunks in ret_work(l):
                    t0, w = SEG[s]
                    r = 64 * (h % 2)
                    obank = (6 if s == "lat" else 4) + h // 2

                    def score(i):
                        c = chunks[i]
                        u = ret_unit(l, s, h, i)
                        if u >= 4:
                            pe.wait_ge(*VR.at(l, "P", u - 4))
                        pe.matmul(ps[:, u % 4, 0:w], rqk[r:r + 64, 2 + h // 2, P * c:P * c + P],
                                  rqk[r:r + 64, h // 2, t0:t0 + w], start=True, stop=True)\
                            .then_inc(*TR.did((l, "S", u)))

                    def pv(i):
                        u = ret_unit(l, s, h, i)
                        pe.wait_ge(*VR.at(l, "P", u))
                        pe.matmul(ps[r:r + 64, obank, 0:w], rv[:, chunks[i], 64 * h:64 * h + 64], pr[:, u % 6, 0:w],
                                  start=(i == 0), stop=(i == len(chunks) - 1))\
                            .then_inc(*TR.did((l, "PV", u)))
                    for i in range(len(chunks) + 2):
                        if i < len(chunks):
                            score(i)
                        if i >= 2:
                            pv(i - 2)
                for s in segs(l):
                    w = SEG[s][1]
                    for p in range(2):
                        oc, cc, sq, rs = ret_out(s, p)
                        b = p
                        pe.wait_ge(*AR.at(l, s, p, "oc"))
                        pe.matmul(ps[:, b, 0:w], mat[:, BD64, :], oc, start=True, stop=True)\
                            .then_inc(*TR.did((l, s, p, "mu")))
                    for p in range(2):
                        oc, cc, sq, rs = ret_out(s, p)
                        b = p
                        pe.wait_ge(*AR.at(l, s, p, "sq"))
                        pe.matmul(ps[:, 2 + b, 0:w], mat[:, BD64, :], sq, start=True, stop=True)\
                            .then_inc(*TR.did((l, s, p, "var")))

            TG, VG, AG, GG = (S[e, "gdn"] for e in engines)

            def gate_sums(l):
                pe.wait_ge(*VG.at(l, "g"))
                g = gs[:, 0, :, :]
                for d in range(2):
                    gd = g[:, :, 4 * d:4 * d + 4]
                    for i, m in enumerate((LE if d == 0 else GE, GT if d == 0 else LT, ONES)):
                        mm = pe.matmul(ps[:, 7, (3 * d + i) * 24:(3 * d + i) * 24 + 24]
                                       .rearrange("p (c h) -> p c h", h=4), mat[:, m, :], gd,
                                       start=True, stop=True)
                mm.then_inc(*TG.did((l, "gc")))

            def head_norm(l, c):
                for u, s in units_of(l, c):
                    w = SEG[s][1]
                    if u == 1:
                        pe.wait_ge(*AG.at(l, "gexp", 1, 2))
                    if u >= 2:
                        pe.wait_ge(*AG.at(l, "sqrt", u - 2))
                    pe.wait_ge(*AG.at(l, "nsq", u))
                    pe.matmul(ps[:, 6 + u % 2, 0:w], ones, squares()[:, u % 2, 0:w], start=True, stop=True)\
                        .then_inc(*TG.did((l, "nrm", u)))

            def four(out_, lhs, rhs):
                for h in range(HEADS):
                    mm = pe.matmul(out_[:, P * h:P * h + P], lhs(h), rhs(h), start=True, stop=True)
                return mm

            def gdn(l):
                qkv = wk(W_QKV, 12, TOK)
                G = [group(d) for d in range(2)]

                def bank(d, i):
                    return ps[:, 4 * d + i, :]

                def turned(out_, src):
                    for h in range(HEADS):
                        mm = pe.transpose(out_[:, P * h:P * h + P], src(h), ident)
                    return mm

                def decay(n, d):
                    pe.wait_ge(*GG.at(l, n, d, "Ag"))
                    if n > 0:
                        if need_o(l, n - 1):
                            pe.wait_ge(*AG.at(l, n - 1, d, "attnT"))
                        pe.wait_ge(*AG.at(l, n - 1, d, "v"))
                    four(bank(d, 0), lambda h: G[d]["Ag"][:, h, :], lambda h: mat[:, GT if d == 0 else LT, :])\
                        .then_inc(*TG.did((l, n, d, "dec")))

                def gram(n, d):
                    cs = slice(P * chunk_of(n, d), P * chunk_of(n, d) + P)
                    pe.wait_ge(*AG.at(l, n, d, "dec"))
                    four(bank(d, 0), lambda h: qkv[:, 4 + h, cs], lambda h: qkv[:, 4 + h, cs])\
                        .then_inc(*TG.did((l, n, d, "G")))

                def scores(n, d):
                    cs = slice(P * chunk_of(n, d), P * chunk_of(n, d) + P)
                    pe.wait_ge(*VG.at(l, n, d, "L"))
                    if need_o(l, n):
                        four(bank(d, 0), lambda h: qkv[:, h, cs], lambda h: qkv[:, 4 + h, cs])\
                            .then_inc(*TG.did((l, n, d, "A")))

                def v_turned(n, d):
                    cs = slice(P * chunk_of(n, d), P * chunk_of(n, d) + P)
                    pe.wait_ge(*AG.at(l, n, d, "k"))
                    turned(bank(d, 0), lambda h: qkv[:, 8 + h, cs]).then_inc(*TG.did((l, n, d, "v")))

                def gates(n, d):
                    pe.wait_ge(*AG.at(l, n, d, "v"))
                    if need_o(l, n) and n > 0:
                        pe.wait_ge(*GG.at(l, n, d, "egc"))
                        four(bank(d, 0), lambda h: ones, lambda h: G[d]["egc"][:, h, :])\
                            .then_inc(*TG.did((l, n, d, "egc")))

                def attn_turned(n, d):
                    if need_o(l, n):
                        if n > 0:
                            pe.wait_ge(*VG.at(l, n, d, "qgT"))
                        turned(bank(d, 0), lambda h: G[d]["attn"][:, h, :]).then_inc(*TG.did((l, n, d, "attnT")))

                def x_turned(n, d, i):
                    pe.wait_ge(*VG.at(l, n, d, "X", i))
                    turned(bank(d, 3), lambda h: G[d]["X"][:, h, :]).then_inc(*TG.did((l, n, d, "YT", i)))

                for part in (decay, gram, scores):
                    for d in range(2):
                        part(0, d)
                for n in range(CHUNKS + 1):
                    m = n - 1
                    for d in range(2):
                        if m >= 1:
                            pe.wait_ge(*AG.at(l, m, d, "Y", NLEV - 1))
                            if n < CHUNKS:
                                pe.wait_ge(*VG.at(l, n, d, "attn" if need_o(l, n) else "L"))
                            else:
                                pe.wait_ge(*AG.at(l, m, d, "attnT"))
                            pe.wait_ge(*GG.at(l, m, d, "kbg"))
                            four(bank(d, 0), lambda h: G[d]["kbg"][:, h, :], lambda h: G[d]["Y"][:, h, :])\
                                .then_inc(*TG.did((l, m, d, "wT")))
                    for d in range(2):
                        if n < CHUNKS:
                            if m >= 0:
                                pe.wait_ge(*AG.at(l, m, d, "Y", NLEV - 1))
                            pe.wait_ge(*VG.at(l, n, d, "L"))
                            turned(bank(d, 3), lambda h: G[d]["L"][:, h, :]).then_inc(*TG.did((l, n, d, "LT")))
                    if m >= 0:
                        for d in range(2):
                            g = G[d]
                            pe.wait_ge(*GG.at(l, m, d, "vb"))
                            pe.wait_ge(*(AG.at(l, m, d, "nwT") if m > 0 else AG.at(l, m, d, "Y", NLEV - 1)))
                            for h in range(HEADS):
                                o = bank(d, 1)[:, P * h:P * h + P]
                                mm = pe.matmul(o, g["Y"][:, h, :], g["vb"][:, h, :], start=True, stop=(m == 0))
                                if m > 0:
                                    mm = pe.matmul(o, g["nwT"][:, h, :], g["S"][:, h, :], start=False, stop=True)
                            mm.then_inc(*TG.did((l, m, d, "vn")))
                        for d in range(2):
                            g = G[d]
                            if n < CHUNKS:
                                pe.wait_ge(*AG.at(l, n, d, "LT"))
                            pe.wait_ge(*AG.at(l, m, d, "vn"))
                            if need_o(l, m):
                                for h in range(HEADS):
                                    o = bank(d, 2)[:, P * h:P * h + P]
                                    if m > 0:
                                        pe.matmul(o, g["S"][:, h, :], g["qgT"][:, h, :], start=True, stop=False)
                                    mm = pe.matmul(o, g["vn"][:, h, :], g["attnT"][:, h, :], start=(m == 0), stop=True)
                                mm.then_inc(*TG.did((l, m, d, "o")))
                            four(bank(d, 3), lambda h: g["kg"][:, h, :], lambda h: g["vn"][:, h, :])\
                                .then_inc(*TG.did((l, m, d, "upd")))
                    if n == CHUNKS:
                        break
                    for d in range(2):
                        cs = slice(P * chunk_of(n, d), P * chunk_of(n, d) + P)
                        if need_o(l, n):
                            pe.wait_ge(*VG.at(l, n, d, "attn"))
                        turned(bank(d, 0), lambda h: qkv[:, 4 + h, cs]).then_inc(*TG.did((l, n, d, "k")))
                    for d in range(2):
                        pe.wait_ge(*(VG.at(l, m, d, "S") if m >= 0 else AG.at(l, n, d, "LT")))
                        x_turned(n, d, 0)
                    between = {1: (v_turned, 0), 2: (gates, 0), 3: (attn_turned, 0), 4: (decay, 1), 5: (gram, 1), 6: (scores, 1)}
                    for i in range(1, NLEV):
                        part, ahead = between.get(i, (None, 0))
                        for d in range(2):
                            g = G[d]
                            if i == 1:
                                pe.wait_ge(*AG.at(l, n, d, "LT"))
                            for h in range(HEADS):
                                mm = pe.matmul(bank(d, 1)[:, P * h:P * h + P], g["LT"][:, h, :], g["X"][:, h, :],
                                               start=True, stop=True)
                            mm.then_inc(*TG.did((l, n, d, "P", i)))
                        if part and n + ahead < CHUNKS:
                            part(n + ahead, 0)
                        for d in range(2):
                            g = G[d]
                            pe.wait_ge(*VG.at(l, n, d, "P", i))
                            pe.wait_ge(*AG.at(l, n, d, "Y", i - 1))
                            if i == 1 and m >= 0 and need_o(l, m):
                                pe.wait_ge(*VG.at(l, m, d, "o"))
                            for h in range(HEADS):
                                mm = pe.matmul(bank(d, 2)[:, 64 * h:64 * h + 64], g["Y"][:, h, :],
                                               g["P"][:, 64 * h:64 * h + 64], start=True, stop=True)
                            mm.then_inc(*TG.did((l, n, d, "XP", i)))
                        if part and n + ahead < CHUNKS:
                            part(n + ahead, 1)
                        for d in range(2):
                            x_turned(n, d, i)

            def gdn_out(l):
                osq, rs = head_squares_of(), head_roots_of()
                for s in segs(l):
                    w = SEG[s][1]
                    for h in range(HEADS):
                        pe.wait_ge(*AG.at(l, "osq", s, h))
                        mm = pe.matmul(ps[32 * h:32 * h + 32, 0 if s == "lat" else 1, 0:w], ones[:, 0:32],
                                       osq[s][:, h, :], start=True, stop=True)
                    mm.then_inc(*TG.did((l, "onrm", s)))
                for s in segs(l):
                    pe.wait_ge(*VG.at(l, "orec", s))
                    for h in range(HEADS):
                        pe.matmul(norm_place(s, h), ones[32 * h:32 * h + 1, :], rs[s][32 * h:32 * h + 1, :],
                                  start=True, stop=True).then_inc(*TG.did((l, "ospread", s, h)))

            for stage, l in ORDER:
                if before((stage, l)) and not chained("tensor", stage):
                    fence(pe, before((stage, l)))
                if stage == "mod":
                    mod(l)
                elif stage == "norm1":
                    norm("norm1", l, ["lat", "ctx"])
                elif stage == "filter_ctx":
                    for _ in filters(l, "ctx"):
                        pass
                elif stage == "hy_proj":
                    hy_proj(l)
                elif stage.startswith("conv_"):
                    long_conv(l, stage[5:])
                elif stage == "ret_proj":
                    ret_proj(l)
                elif stage == "ret":
                    retention(l)
                elif stage == "gdn_proj":
                    gdn_proj(l)
                elif stage == "gdn":
                    gdn(l)
                elif stage == "gdn_out":
                    gdn_out(l)
                elif stage == "out":
                    out_proj(l)
                elif stage.startswith("norm2_"):
                    norm("norm2", l, [stage[6:]])
                elif stage.startswith("ffn_in_"):
                    ffn_in(l, stage[7:])
                elif stage.startswith("ffn_out_"):
                    ffn_out(l, stage[8:])
                elif stage == "final":
                    norm("final", l, ["lat"])
                close("tensor", (stage, l))

        @block.scalar
        def _(act):
            T, V, A, G = (S[e, "proj"] for e in engines)
            TH, VH, AH, GH = (S[e, "hyena"] for e in engines)
            TR, VR, AR, GR = (S[e, "ret"] for e in engines)
            TG, VG, AG, GG = (S[e, "gdn"] for e in engines)


            def square(name, l, s, k):
                t0, w = SEG[s]
                act.activation(norm_area(name, s)[:, k, :], xT[:, k, t0:t0 + w], ACT.Square)\
                    .then_inc(*A.did((name, l, s, "sq", k)))

            def norm(name, l, sgs):
                if name == "norm1" and l == 0:
                    act.wait_ge(tokens_in, 16)
                for s in sgs:
                    for k in range(DC):
                        if (name, s) != ("norm2", "lat"):
                            square(name, l, s, k)
                if name == "norm2":
                    split_hi(PIECE[block_no(l, "fi_" + sgs[0], 0), 0])
                for s in sgs:
                    t0, w = SEG[s]
                    act.wait_ge(*T.at(name, l, s))
                    act.activation(rstd[:, t0:t0 + w], ps[:, 0 if s == "lat" else 1, 0:w], ACT.Sqrt,
                                   bias=eps, scale=1.0 / D).then_inc(*A.did((name, l, s, "sqrt")))
                if name == "final":
                    return
                which = 0 if name == "norm1" else 1
                for s in sgs:
                    t0, w = SEG[s]
                    e = 0 if s == "lat" else 1
                    for k in range(DC):
                        act.wait_ge(*V.at(name, l, s, k))
                        h = norm_area(name, s)[:, k, :]
                        shift = modv[:, 24 * which + k, e:e + 1]
                        if name == "norm2":
                            act.activation(hmod[0][:, k, 0:w], h, ACT.Identity, bias=shift)\
                                .then_inc(*A.did(("h_hi", l, s, k)))
                        else:
                            act.activation(h, h, ACT.Identity, bias=shift).then_inc(*A.did((name, l, s, "h", k)))

            def raw_copy(name, l, item, s, at):
                w = SEG[s][1]
                raw = wk(at, 3, 772)
                o = 1 if s == "ctx" else 259
                if item >= 3:
                    act.wait_ge(*V.at(name, l, item - 3, "conv"))
                act.wait_ge(*T.at(name, l, item, s))
                act.activation(raw[:, item % 3, o:o + w], ps[:, item % 3 + (0 if s == "lat" else 3), 0:w], ACT.Copy)\
                    .then_inc(*A.did((name, l, item, s)))

            def hy_proj(l):
                act.wait_ge(*G.at("halo", l, "hy"))
                for i in range(6):
                    for s in segs(l):
                        raw_copy("hy", l, i, s, W_RAW)

            def ret_proj(l):
                rqk = wk(W_RQK, 4, TOK)
                log_gamma(l)
                for i in range(6):
                    for s in segs(l, both=(i in (2, 3))):
                        t0, w = SEG[s]
                        act.wait_ge(*T.at("ret", l, i, s))
                        dst = rqk[:, i, t0:t0 + w] if i < 4 else mix[:, 6 + i - 4, t0:t0 + w]
                        act.activation(dst, ps[:, i % 3 + (0 if s == "lat" else 3), 0:w],
                                       ACT.Copy if i < 4 else ACT.Silu).then_inc(*A.did(("ret", l, i, s)))

            def gdn_proj(l):
                qkv = wk(W_QKV, 12, TOK)
                act.wait_ge(*G.at("halo", l, "gd"))

                def silu(i):
                    act.wait_ge(*V.at("gd", l, i, "conv"))
                    ss = segs(l, both=(i >= 4))
                    lo = min(SEG[s][0] for s in ss)
                    act.activation(qkv[:, i, lo:TOK], qkv[:, i, lo:TOK], ACT.Silu).then_inc(*AG.did(("gds", l, i)))
                q0 = PIECE[block_no(l, "in", 7), 0]
                split_hi(q0)
                for k in range(DC):
                    act.activation(hpart[0][:, k, :], hT[:, k, :], ACT.Copy).then_inc(*A.did(("hT_hi", l, k)))
                split_hi(q0 + 1)
                gates_a(l)
                for i in range(12):
                    if 0 < i:
                        split_hi(q0 + i + 1)
                    if 3 <= i < 11:
                        head_squares(l, i - 3)
                    for s in segs(l, both=(i >= 4)):
                        raw_copy("gd", l, i, s, W_GRAW)
                    if i == 1:
                        gates_b(l)
                    if 3 <= i < 11:
                        head_roots(l, i - 3)
                    if i >= 1:
                        silu(i - 1)
                for i in range(12, 16):
                    if i < 15:
                        split_hi(q0 + i + 1)
                    for s in segs(l):
                        t0, w = SEG[s]
                        act.wait_ge(*T.at("gd", l, i, s))
                        act.activation(mix[:, 2 + i - 12, t0:t0 + w], ps[:, i % 3 + (0 if s == "lat" else 3), 0:w],
                                       ACT.Silu).then_inc(*A.did(("gd", l, i, s)))
                    if i == 12:
                        silu(11)

            def split_hi(q):
                n, k0, kc, raw, parts = piece(q)
                wait_block(act, n)
                depth = 3 if n in OF_MOD else 2
                if q >= depth:
                    act.wait_ge(*T.at("piece", q - depth))
                act.activation(parts[0], raw, ACT.Copy).then_inc(*A.did(("hi", q)))

            def mix_hi(l, k):
                lo = 0 if l == 0 else CTX
                act.activation(mixp[0][:, k, lo:TOK], mix[:, k, lo:TOK], ACT.Copy).then_inc(*A.did(("mix_hi", l, k)))

            def out_proj(l):
                q0 = PIECE[block_no(l, "out", 0), 0]
                split_hi(q0)
                for k in range(2, 6):
                    mix_hi(l, k)
                for item in range(1, DC + 1):
                    if item < DC:
                        split_hi(q0 + item)
                    if item >= 2:
                        act.wait_ge(*V.at("out", l, item - 2, "lat"))
                        square("norm2", l, "lat", item - 2)
                act.wait_ge(*V.at("out", l, DC - 1, "lat"))
                square("norm2", l, "lat", DC - 1)

            def ffn_in(l, s):
                w = SEG[s][1]
                q0 = PIECE[block_no(l, "fi_" + s, 0), 0]
                for item in range(2 * FC):
                    split_hi(q0 + item + 1)
                    i = item // 2
                    if item % 2 == 0:
                        act.wait_ge(*T.at("fi", l, s, item))
                        if i >= 2:
                            act.wait_ge(*V.at("fi", l, s, item - 3))
                        act.activation(tmp[:, i % 2, 0:w], ps[:, item % 6, 0:w], ACT.Silu)\
                            .then_inc(*A.did(("fi", l, s, item)))
                    else:
                        act.wait_ge(*V.at("fi", l, s, item))
                        act.activation(hid[0][:, i, 0:w], tmp[:, 2 + i % 2, 0:w], ACT.Copy)\
                            .then_inc(*A.did(("hid_hi", l, s, i)))

            def ffn_out(l, s):
                q0 = PIECE[block_no(l, "fo_" + s, 0), 0]
                for q in range(q0 + 1, q0 + 2 * N_FOB):
                    split_hi(q)

            def mod(l):
                filt = filters(l, "lat")
                q0 = PIECE[block_no(l, "mod", 0), 0]
                for q in range(3):
                    split_hi(q0 + q)
                for b in range(N_MODB):
                    for q in (2 * b + 3, 2 * b + 4):
                        if q < 2 * N_MODB:
                            split_hi(q0 + q)
                    act.wait_ge(*T.at("block", block_no(l, "mod", b)))
                    if b >= 2:
                        act.wait_ge(*T.at("turned", l, b - 2))
                    act.activation(modrow[:, b % 2, :], ps[0:4, b % 2, 0:256], ACT.Copy)\
                        .then_inc(*A.did(("modrow", l, b)))
                    if b in FILTERS_ACT:
                        next(filt)
                for _ in filt:
                    pass

            def filters(l, s):
                L = SEG[s][1]
                nt = L // P
                o = (0 if s == "lat" else 1536) + NFP + L
                hb, arg = mixf[0:64, o:o + L], mixf[0:64, o + L:o + 2 * L]
                for i in range(2):
                    act.wait_ge(*VH.at(l, s, "arg", i))
                    act.activation(hb, arg, ACT.Sin).then_inc(*AH.did((l, s, "sin", i)))
                    yield
                K = spectrum()
                for j in range(nt):
                    kj = K[:, j, :].rearrange("p (n c) -> p n c", n=2)
                    for i in range(2):
                        act.wait_ge(*TH.at(l, s, "K", i, j))
                        src = ps[:, 5 if i else 6, :].rearrange("p (n c) -> p n c", n=2)
                        if i == 0:
                            act.activation(kj[:, :, 0:256], src, ACT.Copy).then_inc(*AH.did())
                            act.activation(kj[:, :, 512:768], src, ACT.Copy).then_inc(*AH.did((l, s, "K", i, j)))
                        else:
                            act.activation(kj[:, :, 256:512], src, ACT.Copy).then_inc(*AH.did((l, s, "K", i, j)))
                    yield

            def long_conv(l, s):
                nt = SEG[s][1] // P
                tok = wk(W_TOK, 4, 512)
                for t in range(nt):
                    act.wait_ge(*TH.at(l, s, "tok", t))
                    act.activation(tok[:, t, :], ps[:, t % 2, :], ACT.Copy).then_inc(*AH.did((l, s, "tok", t)))

            def log_gamma(l):
                act.wait_ge(*VR.at(l, "negabs"))
                act.activation(lam[:, 1, :], lam[:, 0, :], ACT.Exp).then_inc(*AR.did((l, "e")))
                act.wait_ge(*VR.at(l, "u"))
                act.activation(lam[:, 0, :], lam[:, 2, :], ACT.Ln).then_inc(*AR.did((l, "lnu")))

            def retention(l):
                rc = work[:, W_RC:W_RC + 3968]
                act.wait_ge(tables_in, tables_count("ret_proj", l))
                for h in range(HEADS):
                    dt, tmp = decay_of(h)
                    act.wait_ge(*VR.at(l, "darg", h))
                    act.activation(dt[:, 0:896], dt[:, 0:896], ACT.Exp).then_inc(*AR.did((l, "D", h)))
                    if h >= 1:
                        act.wait_ge(*GR.at(l, "D2", h - 1))
                    act.activation(dt[:, 896:1536], rc[:, RC_CF:RC_CF + 640], ACT.Exp, scale=lam[:, 3, h:h + 1])\
                        .then_inc(*AR.did())
                    act.activation(tmp[:, 896:1536], rc[:, RC_CB:RC_CB + 640], ACT.Exp, scale=lam[:, 3, 4 + h:5 + h])\
                        .then_inc(*AR.did((l, "D2", h)))
                for s in segs(l):
                    w = SEG[s][1]
                    for p in range(2):
                        oc, cc, sq, rs = ret_out(s, p)
                        last = list(ret_work(l))[-1]
                        u = ret_unit(l, last[0], last[1], len(last[2]) - 1) if p else \
                            ret_unit(l, s, 1, 5 if s == "lat" else 1)
                        act.wait_ge(*TR.at(l, "PV", u))
                        if s == "ctx":
                            act.wait_ge(*VR.at(l, "y", "lat", p))
                        act.activation(oc, ps[:, (6 if s == "lat" else 4) + p, 0:w], ACT.Copy)\
                            .then_inc(*AR.did((l, s, p, "oc")))
                    for p in range(2):
                        oc, cc, sq, rs = ret_out(s, p)
                        act.wait_ge(*VR.at(l, s, p, "cc"))
                        act.activation(sq, cc, ACT.Square).then_inc(*AR.did((l, s, p, "sq")))
                    for p in range(2):
                        oc, cc, sq, rs = ret_out(s, p)
                        act.wait_ge(*TR.at(l, s, p, "var"))
                        act.activation(rs, ps[:, 2 + p, 0:w], ACT.Sqrt, bias=eps).then_inc(*AR.did((l, s, p, "sqrt")))

            def gates_a(l):
                act.wait_ge(*VG.at(l, "negabs"))
                act.activation(gs[:, 2, :, :], gs[:, 2, :, :], ACT.Exp).then_inc(*AG.did((l, "e")))
                act.activation(gs[:, 9, 0, :], par[:, ALOG:ALOG + 8], ACT.Exp).then_inc(*AG.did((l, "ea")))
                act.activation(gs[:, 5, :, :], gs[:, 5, :, :], ACT.Exp, scale=-1.0).then_inc(*AG.did((l, "eb")))
                act.wait_ge(*VG.at(l, "u"))
                act.activation(gs[:, 4, :, :], gs[:, 3, :, :], ACT.Ln).then_inc(*AG.did((l, "lnu")))

            def gates_b(l):
                act.wait_ge(*TG.at(l, "gc"))
                gc = ps[:, 7, 0:144].rearrange("p (d i c h) -> p d i c h", d=2, i=3, c=CHUNKS)
                for d in range(2):
                    for i, k in ((0, 6), (1, 8), (2, 9)):
                        act.activation(gs[:, k, :, 4 * d:4 * d + 4], gc[:, d, i, :, :], ACT.Exp)\
                            .then_inc(*AG.did((l, "gexp", d, i)))

            def head_squares(l, c):
                qkv = wk(W_QKV, 12, TOK)
                act.wait_ge(*AG.at("gds", l, c))
                for u, s in units_of(l, c):
                    t0, w = SEG[s]
                    if u >= 2:
                        act.wait_ge(*TG.at(l, "nrm", u - 2))
                    act.activation(squares()[:, u % 2, 0:w], qkv[:, c, t0:t0 + w], ACT.Square)\
                        .then_inc(*AG.did((l, "nsq", u)))

            def head_roots(l, c):
                for u, s in units_of(l, c):
                    w = SEG[s][1]
                    act.wait_ge(*TG.at(l, "nrm", u))
                    if u >= 2:
                        act.wait_ge(*GG.at(l, "nmul", u - 2))
                    act.activation(roots()[:, u % 2, 0:w], ps[:, 6 + u % 2, 0:w], ACT.Sqrt,
                                   bias=epsq if c < 4 else eps, scale=float(P) if c < 4 else 1.0)\
                        .then_inc(*AG.did((l, "sqrt", u)))

            def gdn(l):
                G_ = [group(d) for d in range(2)]

                def moved(to, n, d, b, step, key, func=ACT.Copy, scale=1.0):
                    act.wait_ge(*TG.at(l, n, d, *step))
                    act.activation(flat(G_[d][to]), ps[:, 4 * d + b, :], func, scale=scale)\
                        .then_inc(*AG.did((l, n, d, *key)))

                for d in range(2):
                    moved("dec", 0, d, 0, ("dec",), ("dec",), ACT.Exp)
                for n in range(CHUNKS + 1):
                    m = n - 1
                    for d in range(2):
                        if m >= 1:
                            moved("nwT", m, d, 0, ("wT",), ("nwT",), scale=-1.0)
                    for d in range(2):
                        if n < CHUNKS:
                            moved("LT", n, d, 3, ("LT",), ("LT",))
                    for d in range(2):
                        if m >= 0:
                            moved("vn", m, d, 1, ("vn",), ("vn",))
                    if n == CHUNKS:
                        break
                    for i in range(NLEV):
                        for d in range(2):
                            if i == 0:
                                moved("kbg", n, d, 0, ("k",), ("k",))
                            if i == 1:
                                moved("vb", n, d, 0, ("v",), ("v",))
                            if need_o(l, n) and i == 3:
                                moved("attnT", n, d, 0, ("attnT",), ("attnT",))
                            if i == 4 and n + 1 < CHUNKS:
                                moved("dec", n + 1, d, 0, ("dec",), ("dec",), ACT.Exp)
                        for d in range(2):
                            moved("Y", n, d, 3, ("YT", i), ("Y", i))

            def gdn_out(l):
                osq, rs = head_squares_of(), head_roots_of()
                for s in segs(l):
                    t0, w = SEG[s]
                    for h in range(HEADS):
                        act.activation(osq[s][:, h, :], oacc[:, h, t0:t0 + w], ACT.Square)\
                            .then_inc(*AG.did((l, "osq", s, h)))
                for s in segs(l):
                    w = SEG[s][1]
                    act.wait_ge(*TG.at(l, "onrm", s))
                    act.activation(rs[s], ps[:, 0 if s == "lat" else 1, 0:w], ACT.Sqrt, bias=eps, scale=1.0 / P)\
                        .then_inc(*AG.did((l, "osqrt", s)))
                for k in (0, 1, 6, 7):
                    mix_hi(l, k)

            for stage, l in ORDER:
                if before((stage, l)) and not chained("scalar", stage):
                    fence(act, before((stage, l)))
                if stage == "mod":
                    if l == 0:
                        act.wait_ge(start_in, 48)
                        act.activation(condT[:, :, :], condT[:, :, :], ACT.Silu).then_inc(*A.did("silu_c"))
                        act.activation(cond_parts[:, 4 * DC:4 * DC + P], ones, ACT.Copy).then_inc(*A.did())
                        act.wait_ge(*A.at("silu_c"))
                        act.activation(cond_rows[:, :, 0, :], condT[:, :, :], ACT.Copy).then_inc(*A.did("cond_hi"))
                    mod(l)
                elif stage == "norm1":
                    norm("norm1", l, ["lat", "ctx"])
                elif stage == "filter_ctx":
                    for _ in filters(l, "ctx"):
                        pass
                elif stage == "hy_proj":
                    hy_proj(l)
                elif stage.startswith("conv_"):
                    long_conv(l, stage[5:])
                elif stage == "ret_proj":
                    ret_proj(l)
                elif stage == "ret":
                    retention(l)
                elif stage == "gdn_proj":
                    gdn_proj(l)
                elif stage == "gdn":
                    gdn(l)
                elif stage == "gdn_out":
                    gdn_out(l)
                elif stage == "out":
                    out_proj(l)
                elif stage.startswith("norm2_"):
                    norm("norm2", l, [stage[6:]])
                elif stage.startswith("ffn_in_"):
                    ffn_in(l, stage[7:])
                elif stage.startswith("ffn_out_"):
                    ffn_out(l, stage[8:])
                elif stage == "final":
                    norm("final", l, ["lat"])
                close("scalar", (stage, l))

        @block.vector
        def _(dve):
            T, V, A, G = (S[e, "proj"] for e in engines)
            TH, VH, AH, GH = (S[e, "hyena"] for e in engines)
            TR, VR, AR, GR = (S[e, "ret"] for e in engines)
            TG, VG, AG, GG = (S[e, "gdn"] for e in engines)

            def step(ins, steps, key=None):
                ins.then_inc(*steps.did(key))
                dve.wait_ge(steps.sem, steps.n)

            def mod(l):
                if l == 0:
                    dve.wait_ge(*A.at("cond_hi"))
                    dve.tensor_tensor(cond_rows[:, :, 1, :], condT[:, :, :], cond_rows[:, :, 0, :].bitcast(F32),
                                      ALU.subtract).then_inc(*V.did("cond_lo"))
                filt = filters(l, "lat")
                for b in range(N_MODB):
                    for m in range(2):
                        split_lo(PIECE[block_no(l, "mod", b), m])
                    if b in FILTERS_DVE:
                        next(filt, None)
                for _ in filt:
                    pass
                dve.wait_ge(params_in, 32 * (l + 1))
                dve.wait_ge(*T.at("turned", l, N_MODB - 1))
                rows_of = ps[:, 7, 0:192].rearrange("p (c r e) -> p c r e", r=2, e=2)
                step(dve.tensor_tensor(modv[:, :, :], rows_of[:, :, 0, :],
                                       par[:, MODB:MODB + 48].unsqueeze(2).broadcast_to([P, 48, 2]), ALU.add), V)
                step(dve.tensor_tensor(modv[:, :, :], modv[:, :, :], rows_of[:, :, 1, :], ALU.add), V)
                for i, (sc, g) in enumerate(((8, N1G), (32, N2G))):
                    step(dve.scalar_tensor_tensor(amp[:, i, :, :], modv[:, sc:sc + 8, :], 1.0,
                                                  par[:, g:g + 8].unsqueeze(2).broadcast_to([P, 8, 2]),
                                                  ALU.add, ALU.mult), V)

            def norm(name, l, sgs):
                for s in sgs:
                    t0, w = SEG[s]
                    e = 0 if s == "lat" else 1
                    if name == "norm2":
                        split_lo(PIECE[block_no(l, "fi_" + s, 0), 0])
                    dve.wait_ge(*A.at(name, l, s, "sqrt"))
                    step(dve.reciprocal(rstd[:, t0:t0 + w], rstd[:, t0:t0 + w]), V)
                    for k in range(DC):
                        a = par[:, FNG + k:FNG + k + 1] if name == "final" else \
                            amp[:, 0 if name == "norm1" else 1, k, e:e + 1]
                        h = norm_area(name, s)[:, k, :]
                        dve.scalar_tensor_tensor(h, xT[:, k, t0:t0 + w], a, rstd[:, t0:t0 + w], ALU.mult, ALU.mult)\
                            .then_inc(*V.did(("final", k) if name == "final" else (name, l, s, k)))
                    if name == "norm2":
                        for k in range(DC):
                            dve.wait_ge(*A.at("h_hi", l, s, k))
                            dve.scalar_tensor_tensor(hmod[1][:, k, 0:w], norm_area(name, s)[:, k, :],
                                                     modv[:, 24 + k, e:e + 1], hmod[0][:, k, 0:w].bitcast(F32),
                                                     ALU.add, ALU.subtract)\
                                .then_inc(*V.did(("h_lo", l, s, k)))

            def conv(name, l, item, at, ss, dst, wcol, bias):
                raw = wk(at, 3, 772)[:, item % 3, :]
                n_w = 6 if name == "hy" else 12
                w = [par[:, wcol + n_w * j + item:wcol + n_w * j + item + 1] for j in range(3)]
                for s in ss:
                    dve.wait_ge(*A.at(name, l, item, s))
                    t0, wd = SEG[s]
                    o = 0 if s == "ctx" else 258
                    d_ = dst[:, t0:t0 + wd]
                    if bias is None:
                        step(dve.tensor_scalar(d_, raw[:, o:o + wd], w[0], None, ALU.mult), V)
                    else:
                        step(dve.tensor_scalar(d_, raw[:, o:o + wd], w[0], bias, ALU.mult, ALU.add), V)
                    step(dve.scalar_tensor_tensor(d_, raw[:, o + 1:o + 1 + wd], w[1], d_, ALU.mult, ALU.add), V)
                    step(dve.scalar_tensor_tensor(d_, raw[:, o + 2:o + 2 + wd], w[2], d_, ALU.mult, ALU.add), V,
                         (name, l, item, "conv") if s == ss[-1] else None)

            def hy_proj(l):
                cv = wk(W_CONV, 4, TOK)
                for i in range(6):
                    dst = cv[:, i, :] if i < 4 else mix[:, i - 4, :]
                    conv("hy", l, i, W_RAW, segs(l), dst, HCW, par[:, HCB + i:HCB + i + 1])

            def log_gamma(l):
                x = par[:, RLOG:RLOG + 8]
                step(dve.scalar_tensor_tensor(lam[:, 0, :], x, -1.0, x, ALU.mult, ALU.min), VR, (l, "negabs"))
                dve.wait_ge(*AR.at(l, "e"))
                step(dve.tensor_scalar(lam[:, 2, :], lam[:, 1, :], 1.0, None, ALU.add), VR, (l, "u"))
                step(dve.reciprocal(lam[:, 3, :], lam[:, 2, :]), VR)
                dve.wait_ge(*AR.at(l, "lnu"))
                step(dve.scalar_tensor_tensor(lam[:, 2, :], lam[:, 2, :], -1.0, lam[:, 1, :], ALU.add, ALU.subtract), VR)
                step(dve.tensor_tensor(lam[:, 2, :], lam[:, 2, :], lam[:, 3, :], ALU.mult), VR)
                step(dve.tensor_tensor(lam[:, 2, :], lam[:, 2, :], lam[:, 0, :], ALU.subtract), VR)
                step(dve.scalar_tensor_tensor(lam[:, 3, :], x, 0.0, lam[:, 2, :], ALU.min, ALU.add), VR, (l, "lam"))

            def ret_proj(l):
                rv = wk(W_RV, CHUNKS, 256)
                log_gamma(l)
                for c in range(CHUNKS):
                    dve.wait_ge(*T.at("rv", l, c))
                    dve.tensor_copy(rv[:, c, :], ps[:, 6 + c % 2, 0:256]).then_inc(*V.did(("rv", l, c)))

            def rows(v):
                return v.unsqueeze(1).broadcast_to([P, CHUNKS, 8])

            def gate_inputs(l):
                for b, (t0, w) in zip((6, 7), (SEG["lat"], SEG["ctx"])):
                    dve.wait_ge(*T.at("ab_row", l, b))
                    dve.tensor_copy(ab_rows[:, t0:t0 + w], ps[0:16, b, 0:w]).then_inc(*V.did(("ab_row", l, b)))
                ab = ps[:, 6, 0:96].rearrange("p (c x) -> p c x", x=16)
                dve.wait_ge(*T.at("ab", l))
                step(dve.tensor_tensor(gs[:, 1, :, :], ab[:, :, 0:8], rows(par[:, DTB:DTB + 8]), ALU.add), VG)
                step(dve.tensor_copy(gs[:, 5, :, :], ab[:, :, 8:16]), VG, (l, "ab"))

            def gates_a(l):
                g_, t_, e_, u_, r_, beta = (gs[:, i, :, :] for i in range(6))
                step(dve.scalar_tensor_tensor(e_, t_, -1.0, t_, ALU.mult, ALU.min), VG, (l, "negabs"))
                dve.wait_ge(*AG.at(l, "e"))
                step(dve.tensor_scalar(u_, e_, 1.0, None, ALU.add), VG, (l, "u"))
                step(dve.scalar_tensor_tensor(e_, u_, -1.0, e_, ALU.add, ALU.subtract), VG)
                dve.wait_ge(*AG.at(l, "lnu"))
                step(dve.reciprocal(u_, u_), VG)
                step(dve.tensor_tensor(e_, e_, u_, ALU.mult), VG)
                step(dve.tensor_tensor(r_, r_, e_, ALU.subtract), VG)
                step(dve.scalar_tensor_tensor(r_, t_, 0.0, r_, ALU.max, ALU.add), VG)
                dve.wait_ge(*AG.at(l, "ea"))
                step(dve.scalar_tensor_tensor(g_, r_, -1.0, rows(gs[:, 9, 0, :]), ALU.mult, ALU.mult), VG, (l, "g"))
                dve.wait_ge(*AG.at(l, "eb"))
                step(dve.tensor_scalar(beta, beta, 1.0, None, ALU.add), VG)
                step(dve.reciprocal(beta, beta), VG)

            def gates_b(l):
                dve.wait_ge(*AG.at(l, "gexp", 1, 2))
                step(dve.tensor_tensor(gs[:, 7, :, :], gs[:, 5, :, :], gs[:, 6, :, :], ALU.mult), VG)

            def head_scale(l, c):
                for u, s in units_of(l, c):
                    w = SEG[s][1]
                    dve.wait_ge(*AG.at(l, "sqrt", u))
                    rs = roots()[:, u % 2, 0:w]
                    dve.reciprocal(rs, rs).then_inc(*VG.did((l, "nrec", u)))

            def gdn_proj(l):
                qkv = wk(W_QKV, 12, TOK)
                q0 = PIECE[block_no(l, "in", 7), 0]
                split_lo(q0)
                for k in range(DC):
                    dve.wait_ge(*A.at("hT_hi", l, k))
                    dve.tensor_tensor(hpart[1][:, k, :], hT[:, k, :], hpart[0][:, k, :].bitcast(F32), ALU.subtract)\
                        .then_inc(*V.did(("hT_lo", l, k)))
                split_lo(q0 + 1)
                gates_a(l)
                for i in range(16):
                    if 0 < i < 15:
                        split_lo(q0 + i + 1)
                    if i >= 12:
                        continue
                    conv("gd", l, i, W_GRAW, segs(l, both=(i >= 4)), qkv[:, i, :], GCW, None)
                    if i == 1:
                        gates_b(l)
                    if 3 <= i < 11:
                        head_scale(l, i - 3)

            def residual(key, item, s, gate, bank):
                t0, w = SEG[s]
                e = 0 if s == "lat" else 1
                x = xT[:, item, t0:t0 + w]
                dve.scalar_tensor_tensor(x, ps[:, bank, 0:w], modv[:, gate + item, e:e + 1], x,
                                         ALU.mult, ALU.add).then_inc(*V.did(key))

            def split_lo(q):
                n, k0, kc, raw, parts = piece(q)
                dve.wait_ge(*A.at("hi", q))
                dve.tensor_tensor(parts[1], raw, parts[0].bitcast(F32), ALU.subtract).then_inc(*V.did(("lo", q)))

            def out_proj(l):
                q0 = PIECE[block_no(l, "out", 0), 0]
                split_lo(q0)
                for k in range(DC):
                    lo = 0 if l == 0 else CTX
                    dve.wait_ge(*A.at("mix_hi", l, k))
                    dve.tensor_tensor(mixp[1][:, k, lo:TOK], mix[:, k, lo:TOK],
                                      mixp[0][:, k, lo:TOK].bitcast(F32), ALU.subtract)\
                        .then_inc(*V.did(("mix_lo", l, k)))
                for i in range(DC):
                    if i < DC - 1:
                        split_lo(q0 + i + 1)
                    for s in segs(l):
                        dve.wait_ge(*T.at("out", l, i, s))
                        residual(("out", l, i, s), i, s, 16, i % 3 + (0 if s == "lat" else 3))

            def ffn_in(l, s):
                w = SEG[s][1]
                q0 = PIECE[block_no(l, "fi_" + s, 0), 0]
                for item in range(2 * FC):
                    split_lo(q0 + item + 1)
                    if item % 2:
                        i = item // 2
                        h = tmp[:, 2 + i % 2, 0:w]
                        dve.wait_ge(*T.at("fi", l, s, item))
                        dve.wait_ge(*A.at("fi", l, s, item - 1))
                        step(dve.tensor_tensor(h, ps[:, item % 6, 0:w], tmp[:, i % 2, 0:w], ALU.mult), V,
                             ("fi", l, s, item))
                        dve.wait_ge(*A.at("hid_hi", l, s, i))
                        dve.tensor_tensor(hid[1][:, i, 0:w], h, hid[0][:, i, 0:w].bitcast(F32), ALU.subtract)\
                            .then_inc(*V.did(("hid_lo", l, s, i)))

            def ffn_out(l, s):
                q0 = PIECE[block_no(l, "fo_" + s, 0), 0]
                for i in range(DC):
                    for part in range(4):
                        if 4 * i + part < 2 * N_FOB - 1:
                            split_lo(q0 + 4 * i + part + 1)
                    dve.wait_ge(*T.at("fo", l, s, i, 3))
                    residual(("fo", l, s, i), i, s, 40, i % 6)

            def filters(l, s):
                L = SEG[s][1]
                nt = L // P
                o = 0 if s == "lat" else 1536
                fp = mixf[0:64, o:o + NFP]
                o += NFP
                arg, rnd = mixf[0:64, o + 2 * L:o + 3 * L], mixf[0:64, o + 3 * L:o + 4 * L]
                win = mixf[:, o + 4 * L:o + 4 * L + 256 * (nt + 1)].rearrange("p (t c) -> p t c", c=256)
                for i in range(2):
                    dve.wait_ge(*TH.at(l, s, "h1" if i == 0 else "h2"))
                    b_, f_ = fp[:, FVEC + 2 * i:FVEC + 2 * i + 1], fp[:, FVEC + 2 * i + 1:FVEC + 2 * i + 2]
                    if i == 0:
                        dve.wait_ge(filter_in, filters_count(l, s))
                    step(dve.tensor_scalar(arg, ps[0:64, 2 + i, 0:L], b_, f_, ALU.add, ALU.mult), VH)
                    step(dve.tensor_scalar(rnd, arg, 1.0 / (2 * math.pi), MAGIC, ALU.mult, ALU.add), VH)
                    step(dve.tensor_scalar(rnd, rnd, -MAGIC, None, ALU.add), VH)
                    step(dve.scalar_tensor_tensor(arg, rnd, -TWO_PI_HI, arg, ALU.mult, ALU.add), VH)
                    step(dve.scalar_tensor_tensor(arg, rnd, -TWO_PI_LO, arg, ALU.mult, ALU.add), VH)
                    step(dve.tensor_scalar(arg, arg, PI_IN, -PI_IN, ALU.min, ALU.max), VH, (l, s, "arg", i))
                    yield
                hp, hn = halves(s)
                dve.wait_ge(tables_in, tables_count(("mod" if s == "lat" else "filter_ctx"), l))
                for t in range(nt):
                    dve.wait_ge(*TH.at(l, s, "h3", t))
                    if t >= 2:
                        dve.wait_ge(*GH.at(l, s, "diff", t - 2))
                    b = ps[:, 2 + 2 * (t % 2):4 + 2 * (t % 2), :]
                    wp = win[:, t, :].unsqueeze(1).broadcast_to([P, 2, 256])
                    wn = (win[:, nt, :] if t == 0 else win[:, t, :]).unsqueeze(1).broadcast_to([P, 2, 256])
                    dve.tensor_tensor(hp[:, t % 2, :].rearrange("p (n c) -> p n c", n=2), b[:, :, 0:256], wp, ALU.mult)\
                        .then_inc(*VH.did((l, s, "hp", t)))
                    dve.tensor_tensor(hn[:, t % 2, :].rearrange("p (n c) -> p n c", n=2), b[:, :, 256:512], wn, ALU.mult)\
                        .then_inc(*VH.did((l, s, "hn", t)))
                    yield
                sd = sum_diff(s)
                dve.wait_ge(*GH.at(l, s, "diff", nt - 1))
                for i in range(2):
                    ins = dve.tensor_tensor(sd[0:1, i, 0, :], sd[0:1, i, 0, :], fp[0:1, FBIAS:FBIAS + 512], ALU.add)
                    ins.then_inc(*VH.did((l, s, "bias") if i == 1 else None))

            def long_conv(l, s):
                t0, L = SEG[s]
                nt = L // P
                K = spectrum()
                tok = wk(W_TOK, 4, 512)
                prod = products()
                for n in range(2):
                    for j in range(nt):
                        dve.wait_ge(*TH.at(l, s, n, "U", j))
                        if j >= 2 or n > 0:
                            dve.wait_ge(*GH.at(l, s, n, "Y", j - 2) if j >= 2 else GH.at(l, s, 0, "Y", nt - 2 + j))
                        b = ps[:, 2 + j % 2, :]
                        k = K[:, j, 768 * n:768 * n + 768]
                        dve.tensor_tensor(prod[:, 2 * (j % 2), :], b, k[:, 0:512], ALU.mult).then_inc(*VH.did())
                        dve.tensor_tensor(prod[:, 2 * (j % 2) + 1, :], b, k[:, 256:768], ALU.mult)\
                            .then_inc(*VH.did((l, s, n, "p2", j)))
                    if n == 0:
                        for t in range(nt):
                            dve.wait_ge(*TH.at(l, s, "y1", t))
                            dve.tensor_tensor(tok[:, t, 0:256], ps[:, 4 + t % 2, 0:256], tok[:, t, 256:512], ALU.mult)\
                                .then_inc(*VH.did((l, s, "z1", t)))
                    else:
                        for c in range(2):
                            dve.wait_ge(*TH.at(l, s, "y2", c))
                            x2 = mix[:, c, t0:t0 + L]
                            dve.tensor_tensor(x2, ps[:, 6 + c, 0:L], x2, ALU.mult).then_inc(*VH.did())

            def retention(l):
                rc = work[:, W_RC:W_RC + 3968]
                rope = wk(W_ROPE, 2, 512)
                rqk = wk(W_RQK, 4, TOK)
                dve.wait_ge(tables_in, tables_count("ret_proj", l))

                def darg(h):
                    dt, tmp = decay_of(h)
                    if h >= 2:
                        dve.wait_ge(*VR.at(l, "P", 6 * (h - 2) + 5))
                        if l == 0:
                            dve.wait_ge(*GR.at(l, "CD", h - 2))
                    step(dve.tensor_scalar(tmp[:, 0:896], rc[:, RC_NEG:RC_NEG + 896], lam[:, 3, 4 + h:5 + h], None,
                                           ALU.mult), VR)
                    step(dve.scalar_tensor_tensor(dt[:, 0:896], rc[:, RC_POS:RC_POS + 896], lam[:, 3, h:h + 1],
                                                  tmp[:, 0:896], ALU.mult, ALU.add), VR, (l, "darg", h))
                darg(0)
                for c in range(4):
                    q = rqk[:, c, CTX:TOK]
                    tmp = wk(W_P, 6, 512)[:, c, :]
                    dve.wait_ge(*TR.at(l, "perm", c))
                    step(dve.tensor_tensor(tmp, ps[:, c, :], rope[:, 1, :], ALU.mult), VR)
                    step(dve.tensor_tensor(q, q, rope[:, 0, :], ALU.mult), VR)
                    step(dve.tensor_tensor(q, q, tmp, ALU.add), VR, (l, "rope", c))
                gate_inputs(l)
                work_list = list(ret_work(l))
                for s, h, chunks in work_list:
                    w = SEG[s][1]
                    if s == "lat":
                        if h + 1 < HEADS:
                            darg(h + 1)
                        dt = decay_of(h)[0]
                        dve.wait_ge(*GR.at(l, "D1", h))
                        dve.wait_ge(*GR.at(l, "D2", h))
                    else:
                        dve.wait_ge(*GR.at(l, "CD", h))
                    for i, c in enumerate(chunks):
                        u = ret_unit(l, s, h, i)
                        if s == "lat":
                            o = 896 + 128 - P * c if c < 2 else 384 - P * (c - 2)
                        else:
                            o = 384 - P * c
                        dve.wait_ge(*TR.at(l, "S", u))
                        if u >= 6:
                            dve.wait_ge(*TR.at(l, "PV", u - 6))
                        src = dt if s == "lat" else ctx_decay(h)
                        dve.scalar_tensor_tensor(wk(W_P, 6, 512)[:, u % 6, 0:w], ps[:, u % 4, 0:w], 0.125,
                                                 src[:, o:o + w], ALU.mult, ALU.mult)\
                            .then_inc(*VR.did((l, "P", u)))
                for s in segs(l):
                    t0, w = SEG[s]
                    for p in range(2):
                        oc, cc, sq, rs = ret_out(s, p)
                        dve.wait_ge(*TR.at(l, s, p, "mu"))
                        dve.tensor_tensor(cc, oc, ps[:, p, 0:w], ALU.subtract).then_inc(*VR.did((l, s, p, "cc")))
                    for p in range(2):
                        oc, cc, sq, rs = ret_out(s, p)
                        dve.wait_ge(*AR.at(l, s, p, "sqrt"))
                        step(dve.reciprocal(rs, rs), VR)
                        step(dve.tensor_tensor(cc, cc, rs, ALU.mult), VR)
                        gate = mix[:, 6 + p, t0:t0 + w]
                        step(dve.tensor_tensor(gate, cc, gate, ALU.mult), VR, (l, "y", s, p))

            def gdn(l):
                G_ = [group(d) for d in range(2)]

                def bank(d, i):
                    return ps[:, 4 * d + i, :].rearrange("p (h c) -> p h c", c=P)

                def l_matrix(n, d):
                    g, c = G_[d], chunk_of(n, d)
                    dve.wait_ge(*TG.at(l, n, d, "G"))
                    dve.wait_ge(*GG.at(l, n, d, "decm"))
                    for h in range(HEADS):
                        dve.scalar_tensor_tensor(g["L"][:, h, :], bank(d, 0)[:, h, :],
                                                 gs[:, 5, c, 4 * d + h:4 * d + h + 1], g["dec"][:, h, :],
                                                 ALU.mult, ALU.mult)\
                            .then_inc(*VG.did((l, n, d, "L") if h == HEADS - 1 else None))

                def attention(n, d):
                    g = G_[d]
                    if need_o(l, n):
                        dve.wait_ge(*TG.at(l, n, d, "A"))
                        dve.tensor_tensor(g["attn"], bank(d, 0), g["dec"], ALU.mult).then_inc(*VG.did((l, n, d, "attn")))

                def queries(n, d):
                    g, c = G_[d], chunk_of(n, d)
                    if need_o(l, n) and n > 0:
                        dve.wait_ge(*TG.at(l, n, d, "egc"))
                        dve.tensor_tensor(g["qgT"], wk(W_QKV, 12, TOK)[:, 0:HEADS, P * c:P * c + P], bank(d, 0),
                                          ALU.mult).then_inc(*VG.did((l, n, d, "qgT")))

                def state(n, d):
                    g, c = G_[d], chunk_of(n, d)
                    dve.wait_ge(*TG.at(l, n, d, "upd"))
                    if n == 0:
                        dve.tensor_copy(g["S"], bank(d, 3)).then_inc(*VG.did((l, n, d, "S")))
                    else:
                        dve.wait_ge(*GG.at(l, n, d, "Sgl"))
                        dve.tensor_tensor(g["S"], g["Sgl"], bank(d, 3), ALU.add).then_inc(*VG.did((l, n, d, "S")))

                def output(n, d):
                    c = chunk_of(n, d)
                    if need_o(l, n):
                        dve.wait_ge(*TG.at(l, n, d, "o"))
                        o = oacc[:, :, P * c:P * c + P]
                        other = next(m for m in range(CHUNKS) if chunk_of(m, 1 - d) == c)
                        if n < other:
                            dve.tensor_copy(o, bank(d, 2)).then_inc(*VG.did((l, n, d, "o")))
                        else:
                            dve.wait_ge(*VG.at(l, other, 1 - d, "o"))
                            dve.tensor_tensor(o, o, bank(d, 2), ALU.add).then_inc(*VG.did((l, n, d, "o")))

                for part in (l_matrix, attention):
                    for d in range(2):
                        part(0, d)
                for n in range(CHUNKS):
                    for d in range(2):
                        g = G_[d]
                        if n > 0:
                            dve.wait_ge(*TG.at(l, n - 1, d, "YT", NLEV - 1))
                        dve.wait_ge(*VG.at(l, n, d, "L"))
                        dve.tensor_tensor(g["X"], g["L"], all_heads(lev[:, d, 0:P]), ALU.mult)\
                            .then_inc(*VG.did((l, n, d, "x")))
                    for d in range(2):
                        g = G_[d]
                        dve.wait_ge(*VG.at(l, n, d, "x"))
                        dve.tensor_tensor(g["X"], all_heads(ident), g["X"], ALU.subtract)\
                            .then_inc(*VG.did((l, n, d, "X", 0)))
                    if n > 0:
                        for d in range(2):
                            output(n - 1, d)
                            state(n - 1, d)
                    for i in range(1, NLEV):
                        for d in range(2):
                            g = G_[d]
                            dve.wait_ge(*TG.at(l, n, d, "P", i))
                            mask = lev[:, d, P + 64 * (i - 1):P + 64 * i].rearrange("p (n b) -> p n b", b=1 << i)\
                                .unsqueeze(1).broadcast_to([P, HEADS, 64 >> i, 1 << i])
                            dve.tensor_tensor(packed(g["P"], i), joined(bank(d, 1), d, i), mask, ALU.mult)\
                                .then_inc(*VG.did((l, n, d, "P", i)))
                        for d in range(2):
                            g = G_[d]
                            dve.wait_ge(*TG.at(l, n, d, "XP", i))
                            x = joined(g["X"], d, i)
                            dve.tensor_tensor(x, x, packed(ps[:, 4 * d + 2, 0:256], i), ALU.subtract)\
                                .then_inc(*VG.did((l, n, d, "X", i)))
                        for d in range(2):
                            if i == 2:
                                queries(n, d)
                            elif i == 5 and n + 1 < CHUNKS:
                                l_matrix(n + 1, d)
                            elif i == 6 and n + 1 < CHUNKS:
                                attention(n + 1, d)
                for d in range(2):
                    state(CHUNKS - 1, d)
                    output(CHUNKS - 1, d)

            def gdn_out(l):
                rs = head_roots_of()
                for s in segs(l):
                    dve.wait_ge(*AG.at(l, "osqrt", s))
                    step(dve.reciprocal(rs[s], rs[s]), VG, (l, "orec", s))
                for s in segs(l):
                    t0, w = SEG[s]
                    for h in range(HEADS):
                        dve.wait_ge(*TG.at(l, "ospread", s, h))
                        o = oacc[:, h, t0:t0 + w]
                        step(dve.scalar_tensor_tensor(o, o, par[:, GNG:GNG + 1], norm_place(s, h), ALU.mult, ALU.mult), VG)
                        z = mix[:, 2 + h, t0:t0 + w]
                        step(dve.tensor_tensor(z, z, o, ALU.mult), VG)

            for stage, l in ORDER:
                if before((stage, l)) and not chained("vector", stage):
                    fence(dve, before((stage, l)))
                if stage == "mod":
                    mod(l)
                elif stage == "norm1":
                    norm("norm1", l, ["lat", "ctx"])
                elif stage == "filter_ctx":
                    for _ in filters(l, "ctx"):
                        pass
                elif stage == "hy_proj":
                    hy_proj(l)
                elif stage.startswith("conv_"):
                    long_conv(l, stage[5:])
                elif stage == "ret_proj":
                    ret_proj(l)
                elif stage == "ret":
                    retention(l)
                elif stage == "gdn_proj":
                    gdn_proj(l)
                elif stage == "gdn":
                    gdn(l)
                elif stage == "gdn_out":
                    gdn_out(l)
                elif stage == "out":
                    out_proj(l)
                elif stage.startswith("norm2_"):
                    norm("norm2", l, [stage[6:]])
                elif stage.startswith("ffn_in_"):
                    ffn_in(l, stage[7:])
                elif stage.startswith("ffn_out_"):
                    ffn_out(l, stage[8:])
                elif stage == "final":
                    norm("final", l, ["lat"])
                close("vector", (stage, l))

        @block.gpsimd
        def _(pool):
            T, V, A, G = (S[e, "proj"] for e in engines)
            TH, VH, AH, GH = (S[e, "hyena"] for e in engines)
            TR, VR, AR, GR = (S[e, "ret"] for e in engines)
            TG, VG, AG, GG = (S[e, "gdn"] for e in engines)

            def halo(l, name, at):
                raw = wk(at, 3, 772)
                for o, w in ((0, 1), (257, 2), (771, 1)):
                    ins = pool.memset(raw[:, :, o:o + w], 0.0)
                    ins.then_inc(*G.did(("halo", l, name) if o == 771 else None))

            def filters(l, s):
                L = SEG[s][1]
                nt = L // P
                o = 0 if s == "lat" else 1536
                n0 = 0 if s == "lat" else LAT
                pool.dma_start(mixf[0:64, o:o + NFP], filter_params[l, :, :]).then_inc(filter_in, 16)
                pool.dma_start(mixf[0:64, o + NFP:o + NFP + L], zpos[:, n0:n0 + L]).then_inc(filter_in, 16)
                o += NFP + 4 * L
                pool.dma_start(mixf[:, o:o + 256 * (nt + 1)], win_lat if s == "lat" else win_ctx).then_inc(tables_in, 16)
                pool.dma_start(work[:, W_TAB:W_TAB + 4 * nt * L], tab_lat if s == "lat" else tab_ctx)\
                    .then_inc(tables_in, 16)
                hp, hn = halves(s)
                sd = sum_diff(s)
                for t in range(nt):
                    pool.wait_ge(*VH.at(l, s, "hn", t))
                    pool.tensor_tensor(sd[:, 0, t, :], hp[:, t % 2, :], hn[:, t % 2, :], ALU.add).then_inc(*GH.did())
                    pool.tensor_tensor(sd[:, 1, t, :], hp[:, t % 2, :], hn[:, t % 2, :], ALU.subtract)\
                        .then_inc(*GH.did((l, s, "diff", t)))

            def long_conv(l, s):
                nt = SEG[s][1] // P
                prod = products()
                yf = wk(W_RAW, 4, 512)
                for n in range(2):
                    for j in range(nt):
                        pool.wait_ge(*VH.at(l, s, n, "p2", j))
                        if n == 1:
                            pool.wait_ge(*TH.at(l, s, "y1", nt - 1))
                        a, b = prod[:, 2 * (j % 2), :], prod[:, 2 * (j % 2) + 1, :]
                        pool.tensor_tensor(yf[:, j, 0:256], a[:, 0:256], a[:, 256:512], ALU.subtract).then_inc(*GH.did())
                        pool.tensor_tensor(yf[:, j, 256:512], b[:, 0:256], b[:, 256:512], ALU.add)\
                            .then_inc(*GH.did((l, s, n, "Y", j)))

            def retention(l):
                rc = work[:, W_RC:W_RC + 3968]
                pool.wait_ge(tables_in, tables_count("ret_proj", l))
                for h in range(HEADS):
                    dt, tmp = decay_of(h)
                    pool.wait_ge(*AR.at(l, "D", h))
                    pool.tensor_tensor(dt[:, 0:896], dt[:, 0:896], rc[:, RC_EYE:RC_EYE + 896], ALU.add)\
                        .then_inc(*GR.did((l, "D1", h)))
                    pool.wait_ge(*AR.at(l, "D2", h))
                    pool.tensor_tensor(dt[:, 896:1536], dt[:, 896:1536], tmp[:, 896:1536], ALU.add)\
                        .then_inc(*GR.did((l, "D2", h)))
                    if l == 0:
                        pool.wait_ge(*GR.at(l, "D1", h))
                        pool.tensor_copy(work[:, W_CD + 384 * h:W_CD + 384 * h + 384], dt[:, 256:640])\
                            .then_inc(*GR.did((l, "CD", h)))

            def head_scale(l):
                qkv = wk(W_QKV, 12, TOK)
                for c in range(8):
                    for u, s in units_of(l, c):
                        t0, w = SEG[s]
                        pool.wait_ge(*VG.at(l, "nrec", u))
                        pool.tensor_tensor(qkv[:, c, t0:t0 + w], qkv[:, c, t0:t0 + w], roots()[:, u % 2, 0:w],
                                           ALU.mult).then_inc(*GG.did((l, "nmul", u)))

            def gdn(l):
                G_ = [group(d) for d in range(2)]

                def decays(n, d):
                    g, c = G_[d], chunk_of(n, d)
                    if n > 0:
                        if need_o(l, n - 1) and n > 1:
                            pool.wait_ge(*TG.at(l, n - 1, d, "egc"))
                        elif n > 1:
                            pool.wait_ge(*TG.at(l, n - 2, d, "upd"))
                    pool.tensor_tensor(g["Ag"], all_heads(mat[:, LE if d == 0 else GE, :]),
                                       per_head(gs[:, 0, c, 4 * d:4 * d + 4]), ALU.mult)\
                        .then_inc(*GG.did((l, n, d, "Ag")))

                def masked(n, d):
                    g = G_[d]
                    pool.wait_ge(*AG.at(l, n, d, "dec"))
                    pool.tensor_tensor(g["dec"], g["dec"], all_heads(mat[:, GE if d == 0 else LE, :]), ALU.mult)\
                        .then_inc(*GG.did((l, n, d, "decm")))

                for part in (decays, masked):
                    for d in range(2):
                        part(0, d)
                for n in range(CHUNKS):
                    if n > 0 and need_o(l, n):
                        for d in range(2):
                            pool.wait_ge(*TG.at(l, n - 1, d, "upd"))
                            pool.tensor_tensor(G_[d]["egc"], all_heads(ident),
                                               per_head(gs[:, 6, chunk_of(n, d), 4 * d:4 * d + 4]), ALU.mult)\
                                .then_inc(*GG.did((l, n, d, "egc")))
                    if n > 0:
                        for d in range(2):
                            g, c = G_[d], chunk_of(n, d)
                            pool.wait_ge(*VG.at(l, n - 1, d, "S"))
                            pool.tensor_tensor(g["Sgl"], g["S"], per_head(gs[:, 9, c, 4 * d:4 * d + 4]), ALU.mult)\
                                .then_inc(*GG.did((l, n, d, "Sgl")))
                    for d in range(2):
                        g, c = G_[d], chunk_of(n, d)

                        def scaled(to, src, k, key):
                            pool.tensor_tensor(g[to], g[src], per_head(gs[:, k, c, 4 * d:4 * d + 4]), ALU.mult)\
                                .then_inc(*GG.did((l, n, d, key)))
                        pool.wait_ge(*AG.at(l, n, d, "k"))
                        scaled("kg", "kbg", 8, "kg")
                        pool.wait_ge(*GG.at(l, n, d, "kg"))
                        scaled("kbg", "kbg", 7, "kbg")
                        pool.wait_ge(*AG.at(l, n, d, "v"))
                        scaled("vb", "vb", 5, "vb")
                    if n + 1 < CHUNKS:
                        for part in (decays, masked):
                            for d in range(2):
                                part(n + 1, d)

            for stage, l in ORDER:
                if before((stage, l)):
                    fence(pool, before((stage, l)))
                if stage == "mod":
                    pool.dma_start(par[:, :], layer_params[l, :, :]).then_inc(params_in, 16)
                    pool.dma_start(wab[:, :], w_ab[l, :, :]).then_inc(params_in, 16)
                    filters(l, "lat")
                elif stage == "filter_ctx":
                    filters(l, "ctx")
                elif stage == "hy_proj":
                    halo(l, "hy", W_RAW)
                elif stage.startswith("conv_"):
                    long_conv(l, stage[5:])
                elif stage == "ret_proj":
                    pool.dma_start(work[:, W_RC:W_RC + 3968], ret_tab).then_inc(tables_in, 16)
                    pool.dma_start(wk(W_ROPE, 2, 512), rope_tab).then_inc(tables_in, 16)
                elif stage == "ret":
                    retention(l)
                elif stage == "gdn_proj":
                    halo(l, "gd", W_GRAW)
                    head_scale(l)
                elif stage == "gdn":
                    gdn(l)
                close("pool", (stage, l))


W_CD = W_RM + 2048


def constants():
    i = np.arange(P)
    r, c = i[:, None], i[None, :]
    mats = np.zeros((P, 8, P))
    mats[:, IDENT] = r == c
    mats[:, ONES] = 1
    half = (c % 64) // 32
    mats[:, PERM] = np.where(half == 0, -(r == c + 32).astype(float), (r == c - 32).astype(float))
    mats[:, BD64] = (r // 64 == c // 64) / 64.0
    mats[:, LE], mats[:, GT], mats[:, GE], mats[:, LT] = r <= c, r > c, r >= c, r < c
    lev = [[], []]
    for k in range(NLEV):
        b = 1 << k
        m = (r // (2 * b) == c // (2 * b)) & ((r // b) % 2 == 1) & ((c // b) % 2 == 0)
        for d, v in enumerate((m, m.T)):
            lev[d].append(v if k == 0 else v.reshape(P, P // (2 * b), 2, b)[:, :, d, :].reshape(P, 64))
    lev = np.stack([np.concatenate(v, axis=1) for v in lev], axis=1)

    def dft(L):
        n = L // P
        k, t = np.arange(L), np.arange(L)
        th = 2 * np.pi * ((2 * k[None, :] + 1) * t[:, None] % (4 * L)) / (4 * L)
        fw = [f(th).reshape(n, P, L).transpose(1, 0, 2) for f in (np.cos, np.sin)]
        bw = [(f(th).T / L).reshape(n, P, L).transpose(1, 0, 2) for f in (np.cos, np.sin)]
        return np.stack(fw + bw, axis=1).reshape(P, -1)

    def window(L):
        t = np.linspace(0.0, 1.0, L)
        lo, hi = math.log(1e-2) / 1.5, math.log(1e-2) / 0.3
        w = np.exp(-t[:, None] * np.abs(np.linspace(lo, hi, HYW))[None, :])
        w = w.reshape(L // P, P, HYW)
        first = w[0:1].copy()
        first[0, 0] = 0
        return np.concatenate([w, first]).transpose(1, 0, 2).reshape(P, -1)

    f32 = np.float32
    z = np.zeros((64, TOK), f32)
    for L, at in ((LAT, 0), (CTX, LAT)):
        pos = np.arange(L, dtype=f32)
        f = np.linspace(1e-4, 15, 16, dtype=f32)
        ang = (f32(2.0 * math.pi / L) * pos[:, None]) * f[None, :]
        z[0, at:at + L] = np.linspace(0.0, 1.0, L, dtype=f32)
        z[1:17, at:at + L] = np.cos(ang).T
        z[17:33, at:at + L] = -np.sin(ang).T
    d = np.arange(896)[None, :] - 384 - r
    dc = np.arange(640)[None, :] - 128 - r
    ret = np.concatenate([np.maximum(d, 0), np.maximum(-d, 0), d == 0, dc + 256, 512 - dc], axis=1)
    inv = 10000.0 ** (-np.arange(16) / 16)
    tok = np.arange(LAT)
    ang = np.concatenate([(tok // 64)[:, None] * inv, (tok % 64)[:, None] * inv], axis=1)
    rope = np.stack([f(ang).T[np.arange(P) % 32] for f in (np.cos, np.sin)], axis=1)
    return {"mats": mats.astype(f32), "level_masks": lev, "tab_lat": dft(LAT).astype(f32),
            "tab_ctx": dft(CTX).astype(f32), "win_lat": window(LAT).astype(f32),
            "win_ctx": window(CTX).astype(f32), "zpos": z, "ret_tab": ret.astype(f32),
            "rope_tab": rope.astype(f32)}


def kernel(**inputs):
    import ml_dtypes
    import concourse.bacc as bacc
    from concourse.bass_utils import run_bass_kernel_spmd

    a = {k: np.asarray(v) for k, v in inputs.items()}
    f32 = np.float32

    def feature_major(v):
        return v.T.reshape(v.shape[1] // P, P, v.shape[0]).transpose(1, 0, 2)

    def per_partition(v):
        return v.reshape(-1, P).T

    blocks = []

    def add(w):
        v = w.reshape(w.shape[0] // P, P, w.shape[1]).transpose(1, 0, 2).reshape(P, -1)
        b = np.zeros((P, BLK), f32)
        b[:, :v.shape[1]] = v
        blocks.append(b)

    params, fparams, wabs = [], [], []
    for l in range(DEPTH):
        for b in range(N_MODB):
            add(a["mod_w"][l][:, 256 * b:256 * b + 256])
        for c in IN_BLOCKS:
            add(a["w_in"][l][:, c:c + 256])
        for b in range(N_OUTB):
            add(a["w_out"][l][:, 256 * b:256 * b + 256])
        for b in range(N_FIB):
            add(np.concatenate([a["ffn_w_in"][l][:, P * b:P * b + P],
                                a["ffn_w_in"][l][:, FF + P * b:FF + P * b + P]], axis=1))
        for b in range(DC):
            for half in range(2):
                add(a["ffn_w_out"][l][FF // 2 * half:FF // 2 * (half + 1), P * b:P * b + P])
        p = np.zeros((P, NPAR), f32)
        p[:, MODB:MODB + 48] = per_partition(a["mod_b"][l])
        p[:, N1G:N1G + 8] = per_partition(a["norm1_g"][l])
        p[:, N2G:N2G + 8] = per_partition(a["norm2_g"][l])
        p[:, FNG:FNG + 8] = per_partition(a["final_norm_g"])
        p[:, HCW:HCW + 18] = per_partition(a["hy_conv_w"][l].reshape(-1))
        p[:, HCB:HCB + 6] = per_partition(a["hy_conv_b"][l])
        p[:, GCW:GCW + 36] = per_partition(a["gdn_conv_w"][l].reshape(-1))
        p[:, GNG] = a["gdn_norm_g"][l]
        p[:, ALOG:ALOG + 8] = a["gdn_a_log"][l].reshape(-1)
        p[:, DTB:DTB + 8] = a["gdn_dt_bias"][l].reshape(-1)
        p[:, RLOG:RLOG + 8] = a["ret_decay_logit"][l].reshape(-1)
        p[:, EPSC] = EPS
        p[:, EPSQ] = EPS * P
        params.append(p)
        q = np.zeros((64, NFP), f32)
        q[0:33, FW1:FW1 + 64] = a["hy_f_w1"][l]
        q[:, FW2:FW2 + 64] = a["hy_f_w2"][l]
        q[:, FW3:FW3 + 1024] = a["hy_f_w3"][l]
        for i, k in enumerate(("hy_f_b1", "hy_f_freq1", "hy_f_b2", "hy_f_freq2")):
            q[:, FVEC + i] = a[k][l]
        q[0, FBIAS:FBIAS + 512] = a["hy_bias"][l].reshape(-1)
        fparams.append(q)
        wabs.append(a["w_in"][l][:, AB_COL:AB_COL + 16].reshape(DC, P, 16).transpose(1, 0, 2).reshape(P, -1))

    cst = constants()
    arrays = {
        "tokens": feature_major(np.concatenate([a["ctx"][0], a["x"][0]])),
        "cond": feature_major(np.stack([a["c"][0], a["c_ctx"]])),
        "weights": np.stack(blocks),
        "w_ab": np.stack(wabs),
        "layer_params": np.stack(params),
        "filter_params": np.stack(fparams),
        "mats": cst["mats"],
        "level_masks": cst["level_masks"].astype(ml_dtypes.bfloat16),
    }
    for k in ("tab_lat", "tab_ctx", "win_lat", "win_ctx", "zpos", "ret_tab", "rope_tab"):
        arrays[k] = cst[k]
    arrays = {k: np.ascontiguousarray(v) for k, v in arrays.items()}

    def program(values):
        nc = bacc.Bacc("TRN2", target_bir_lowering=False, num_devices=1)
        args = [nc.dram_tensor(f"in_{k}", v.shape, mybir.dt.from_np(v.dtype), kind="ExternalInput").ap()
                for k, v in arrays.items()]
        out = nc.dram_tensor("out_y", (P, DC, LAT), F32, kind="ExternalOutput").ap()
        backbone(nc, values, *args, out)
        return nc

    values = {}
    program(values)
    nc = program(values)
    r = run_bass_kernel_spmd(nc, [{f"in_{k}": v for k, v in arrays.items()}], core_ids=[0])
    y = r.results[0]["out_y"]
    return y.transpose(2, 1, 0).reshape(1, LAT, D)
```
